# Optimizing a Trainium2 kernel written in Bass

```python
import math
import jax, jax.numpy as jnp
from jax import lax
import numpy as np

D_MODEL = 2048
BATCH = 1
SEQ = 256
DEPTH = 1
DEC_BATCH = 8
DEC_SEQ = 1
PAST_LEN = 1024
PAGE_SIZE = 128

FOX_HEADS = 8
FOX_HD = 128
FOX_W = FOX_HEADS * FOX_HD
Q_BLOCK = 128
FOX_F_BIAS = 8.0
GDN_HEADS = 8
GDN_DK = 128
GDN_DV = 128
GDN_KW = GDN_HEADS * GDN_DK
GDN_VW = GDN_HEADS * GDN_DV
CONV_W = 4
CONV_CH = 2 * GDN_KW + GDN_VW
GDN_CHUNK = 64
PEER_HEADS = 8
N_KEYS = 128
N_EXPERTS = N_KEYS * N_KEYS
PEER_DK = 128
PEER_TOPK = 16
PEER_TOKEN_BLOCK = 128
PLE_DIM = 256
EPS = 1e-6

OFF_FQ = 0
OFF_FK = OFF_FQ + FOX_W
OFF_FV = OFF_FK + FOX_W
OFF_FF = OFF_FV + FOX_W
OFF_GQKV = OFF_FF + FOX_HEADS
OFF_GA = OFF_GQKV + CONV_CH
OFF_GB = OFF_GA + GDN_HEADS
OFF_GZ = OFF_GB + GDN_HEADS
OFF_GATE = OFF_GZ + GDN_VW
N_IN = OFF_GATE + 2 * D_MODEL

kernel_name = 'fox_gdn_peer_hybrid_step'

def rmsnorm(x, g):
    xf = x.astype(jnp.float32)
    y = xf * lax.rsqrt(jnp.mean(xf * xf, axis=-1, keepdims=True) + EPS)
    return (y * g.astype(jnp.float32)).astype(x.dtype)

def l2norm(x):
    xf = x.astype(jnp.float32)
    return xf * lax.rsqrt(jnp.sum(xf * xf, axis=-1, keepdims=True) + EPS)

def suffix_logf(logf, axis):
    lf = logf.astype(jnp.float32)
    return lax.cumsum(lf, axis=axis, reverse=True) - lf

def fox_inputs(proj, lw):
    B, L, _ = proj.shape
    q = proj[..., OFF_FQ:OFF_FK].reshape(B, L, FOX_HEADS, FOX_HD)
    k = proj[..., OFF_FK:OFF_FV].reshape(B, L, FOX_HEADS, FOX_HD)
    v = proj[..., OFF_FV:OFF_FF].reshape(B, L, FOX_HEADS, FOX_HD)
    logf = jax.nn.log_sigmoid(proj[..., OFF_FF:OFF_GQKV].astype(jnp.float32) + lw['fox_f_bias'].astype(jnp.float32))
    return rmsnorm(q, lw['fox_q_norm']), rmsnorm(k, lw['fox_k_norm']), v, logf

def fox_prompt(q, k, v, logf):
    B, L = q.shape[:2]
    nb = L // Q_BLOCK
    scale = FOX_HD ** -0.5
    d = suffix_logf(logf, 1).transpose(0, 2, 1)
    q_blocks = q.reshape(B, nb, Q_BLOCK, FOX_HEADS, FOX_HD).transpose(1, 0, 2, 3, 4)
    key_pos = jnp.arange(L)

    def one_block(args):
        qi, b = args
        q_pos = b * Q_BLOCK + jnp.arange(Q_BLOCK)
        dq = lax.dynamic_slice_in_dim(d, b * Q_BLOCK, Q_BLOCK, axis=2)
        s = jnp.einsum('bqhd,bkhd->bhqk', qi, k).astype(jnp.float32) * scale
        s = s + d[:, :, None, :] - dq[:, :, :, None]
        s = jnp.where(key_pos[None, :] <= q_pos[:, None], s, -jnp.inf)
        pr = jax.nn.softmax(s, axis=-1).astype(v.dtype)
        return jnp.einsum('bhqk,bkhd->bqhd', pr, v)

    o = lax.map(one_block, (q_blocks, jnp.arange(nb)))
    return o.transpose(1, 0, 2, 3, 4).reshape(B, L, FOX_W)

def fox_sample(q, k, v, logf, cache_k, cache_v, cache_logf, page_table, layer):
    n_ctx = page_table.shape[1] * PAGE_SIZE
    ds = q.shape[1]
    scale = FOX_HD ** -0.5
    key_pos = jnp.arange(n_ctx + ds)
    q_pos = n_ctx + jnp.arange(ds)
    mask = key_pos[None, :] <= q_pos[:, None]

    def one_seq(args):
        qi, ki, vi, lfi, pages = args
        kp = cache_k[layer, pages].reshape(n_ctx, FOX_HEADS, FOX_HD)
        vp = cache_v[layer, pages].reshape(n_ctx, FOX_HEADS, FOX_HD)
        lfp = cache_logf[layer, pages].reshape(n_ctx, FOX_HEADS)
        ka = jnp.concatenate([kp.astype(ki.dtype), ki], axis=0)
        va = jnp.concatenate([vp.astype(vi.dtype), vi], axis=0)
        d = suffix_logf(jnp.concatenate([lfp.astype(jnp.float32), lfi], axis=0), 0)
        s = jnp.einsum('qhd,khd->hqk', qi, ka).astype(jnp.float32) * scale
        s = s + d.T[:, None, :] - d[n_ctx:].T[:, :, None]
        s = jnp.where(mask[None], s, -jnp.inf)
        pr = jax.nn.softmax(s, axis=-1).astype(va.dtype)
        return jnp.einsum('hqk,khd->qhd', pr, va)

    o = lax.map(one_seq, (q, k, v, logf, page_table))
    return o.reshape(q.shape[0], ds, FOX_W)

def causal_conv(xc, conv_state, w_conv):
    L = xc.shape[1]
    xp = jnp.concatenate([conv_state.astype(xc.dtype), xc], axis=1)
    y = xp[:, 0:L] * w_conv[0]
    for j in range(1, CONV_W):
        y = y + xp[:, j:j + L] * w_conv[j]
    return jax.nn.silu(y), xp[:, L:]

def gdn_inputs(proj, conv_state, lw):
    B, L, _ = proj.shape
    y, new_conv = causal_conv(proj[..., OFF_GQKV:OFF_GA], conv_state, lw['gdn_conv_w'])
    q = l2norm(y[..., :GDN_KW].reshape(B, L, GDN_HEADS, GDN_DK)) * (GDN_DK ** -0.5)
    k = l2norm(y[..., GDN_KW:2 * GDN_KW].reshape(B, L, GDN_HEADS, GDN_DK))
    v = y[..., 2 * GDN_KW:].reshape(B, L, GDN_HEADS, GDN_DV).astype(jnp.float32)
    a = proj[..., OFF_GA:OFF_GB].astype(jnp.float32)
    b = proj[..., OFF_GB:OFF_GZ].astype(jnp.float32)
    g = -jnp.exp(lw['gdn_a_log'].astype(jnp.float32)) * jax.nn.softplus(a + lw['gdn_dt_bias'].astype(jnp.float32))
    beta = jax.nn.sigmoid(b)
    z = proj[..., OFF_GZ:OFF_GATE].reshape(B, L, GDN_HEADS, GDN_DV)
    return q, k, v, g, beta, z, new_conv

def gdn_chunked(q, k, v, g, beta, s0):
    B, L = q.shape[:2]
    C = GDN_CHUNK
    n = L // C

    def chunks(t):
        return t.reshape((B, n, C) + t.shape[2:]).swapaxes(2, 3).swapaxes(0, 1)

    qc, kc, vc, gc, bc = chunks(q), chunks(k), chunks(v), chunks(g), chunks(beta)
    gcum = jnp.cumsum(gc, axis=-1)
    incl = jnp.tril(jnp.ones((C, C), dtype=bool))
    strict = jnp.tril(jnp.ones((C, C), dtype=bool), -1)
    diff = gcum[..., :, None] - gcum[..., None, :]
    decay = jnp.where(incl, jnp.exp(jnp.where(incl, diff, 0.0)), 0.0)
    kb = kc * bc[..., None]
    a = jnp.where(strict, jnp.einsum('nbhid,nbhjd->nbhij', kb, kc) * decay, 0.0)
    eye = jnp.eye(C, dtype=a.dtype)
    t_inv = lax.linalg.triangular_solve(a + eye, jnp.broadcast_to(eye, a.shape), left_side=True, lower=True, unit_diagonal=True)
    u = jnp.einsum('nbhij,nbhjd->nbhid', t_inv, vc * bc[..., None])
    w = jnp.einsum('nbhij,nbhjd->nbhid', t_inv, kb * jnp.exp(gcum)[..., None])

    def step(S, xs):
        qi, ki, ui, wi, gi, di = xs
        attn = jnp.einsum('bhid,bhjd->bhij', qi, ki) * di
        v_new = ui - jnp.einsum('bhcd,bhde->bhce', wi, S)
        o = jnp.einsum('bhcd,bhde->bhce', qi * jnp.exp(gi)[..., None], S) + jnp.einsum('bhij,bhje->bhie', attn, v_new)
        g_last = gi[..., -1]
        S = S * jnp.exp(g_last)[..., None, None] + jnp.einsum('bhcd,bhce->bhde', ki * jnp.exp(g_last[..., None] - gi)[..., None], v_new)
        return S, o

    S, o = lax.scan(step, s0, (qc, kc, u, w, gcum, decay))
    return o.swapaxes(0, 1).swapaxes(2, 3).reshape(B, L, GDN_HEADS, GDN_DV), S

def gdn_recurrent(q, k, v, g, beta, s0):
    def step(S, xs):
        qt, kt, vt, gt, bt = xs
        S = S * jnp.exp(gt)[..., None, None]
        kv = jnp.einsum('bhd,bhde->bhe', kt, S)
        S = S + kt[..., :, None] * ((vt - kv) * bt[..., None])[..., None, :]
        return S, jnp.einsum('bhd,bhde->bhe', qt, S)

    xs = (q.swapaxes(0, 1), k.swapaxes(0, 1), v.swapaxes(0, 1), g.swapaxes(0, 1), beta.swapaxes(0, 1))
    S, o = lax.scan(step, s0, xs)
    return o.swapaxes(0, 1), S

def gdn_output(o, z, lw):
    B, L = o.shape[:2]
    o = rmsnorm(o, lw['gdn_norm_g']).astype(z.dtype) * jax.nn.silu(z)
    return o.reshape(B, L, GDN_VW)

def merge_branches(proj, o_fox, o_gdn, lw):
    ga = jax.nn.sigmoid(proj[..., OFF_GATE:OFF_GATE + D_MODEL])
    gb = jax.nn.sigmoid(proj[..., OFF_GATE + D_MODEL:N_IN])
    m = ga * (o_fox @ lw['w_up_fox']) + gb * (o_gdn @ lw['w_up_gdn'])
    return m @ lw['w_out']

def peer_route(h, w_q, sub_keys):
    T = h.shape[0]
    q = (h @ w_q).reshape(T, PEER_HEADS, 2, PEER_DK)
    s = jnp.einsum('thpd,hpkd->thpk', q, sub_keys).astype(jnp.float32)
    sv, si = lax.top_k(s, PEER_TOPK)
    cand = (sv[:, :, 0, :, None] + sv[:, :, 1, None, :]).reshape(T, PEER_HEADS, PEER_TOPK * PEER_TOPK)
    cv, ci = lax.top_k(cand, PEER_TOPK)
    ia = jnp.take_along_axis(si[:, :, 0], ci // PEER_TOPK, axis=-1)
    ib = jnp.take_along_axis(si[:, :, 1], ci % PEER_TOPK, axis=-1)
    return ia * N_KEYS + ib, jax.nn.softmax(cv, axis=-1)

def peer_ffn(h, lw):
    B, L, D = h.shape
    T = B * L
    hf = h.reshape(T, D)
    idx, gate = peer_route(hf, lw['peer_w_q'], lw['peer_sub_keys'])
    nb = -(-T // PEER_TOKEN_BLOCK)
    pad = nb * PEER_TOKEN_BLOCK - T
    hb = jnp.pad(hf, ((0, pad), (0, 0))).reshape(nb, PEER_TOKEN_BLOCK, D)
    ib = jnp.pad(idx, ((0, pad), (0, 0), (0, 0))).reshape(nb, PEER_TOKEN_BLOCK, PEER_HEADS, PEER_TOPK)
    gb = jnp.pad(gate, ((0, pad), (0, 0), (0, 0))).reshape(nb, PEER_TOKEN_BLOCK, PEER_HEADS, PEER_TOPK)
    eu, ev = lw['peer_u'], lw['peer_v']

    def one_block(args):
        hi, ii, gi = args
        act = jax.nn.gelu(jnp.einsum('td,thkd->thk', hi, eu[ii]).astype(jnp.float32), approximate=False)
        return jnp.einsum('thk,thkd->td', (act * gi).astype(hi.dtype), ev[ii])

    y = lax.map(one_block, (hb, ib, gb)).reshape(nb * PEER_TOKEN_BLOCK, D)[:T]
    return y.reshape(B, L, D)

def channel_and_ple(x, p_i, lw):
    x = x + peer_ffn(rmsnorm(x, lw['norm_ffn_g']), lw)
    gate = jax.nn.sigmoid(rmsnorm(x, lw['norm_ple_g']) @ lw['w_ple_gate'])
    return x + gate * (p_i.astype(x.dtype) @ lw['w_ple'])

def block_prompt(x, p_i, lw):
    B = x.shape[0]
    proj = rmsnorm(x, lw['norm_mix_g']) @ lw['w_in']
    q, k, v, logf = fox_inputs(proj, lw)
    o_fox = fox_prompt(q, k, v, logf)
    conv0 = jnp.zeros((B, CONV_W - 1, CONV_CH), x.dtype)
    gq, gk, gv, g, beta, z, conv_new = gdn_inputs(proj, conv0, lw)
    s0 = jnp.zeros((B, GDN_HEADS, GDN_DK, GDN_DV), jnp.float32)
    o_g, s_new = gdn_chunked(gq, gk, gv, g, beta, s0)
    x = x + merge_branches(proj, o_fox, gdn_output(o_g, z, lw), lw)
    x = channel_and_ple(x, p_i, lw)
    return x, k, v, logf, s_new, conv_new

def block_sample(x, p_i, cache_k, cache_v, cache_logf, s0, conv0, page_table, layer, lw):
    proj = rmsnorm(x, lw['norm_mix_g']) @ lw['w_in']
    q, k, v, logf = fox_inputs(proj, lw)
    o_fox = fox_sample(q, k, v, logf, cache_k, cache_v, cache_logf, page_table, layer)
    gq, gk, gv, g, beta, z, conv_new = gdn_inputs(proj, conv0, lw)
    o_g, s_new = gdn_recurrent(gq, gk, gv, g, beta, s0.astype(jnp.float32))
    x = x + merge_branches(proj, o_fox, gdn_output(o_g, z, lw), lw)
    x = channel_and_ple(x, p_i, lw)
    return x, k, v, logf, s_new, conv_new

def setup_inputs(seed: int = 0) -> dict:
    key = jax.random.key(seed)
    ks = jax.random.split(key, 32)
    f32 = jnp.float32
    n_pages = PAST_LEN // PAGE_SIZE
    n_used = DEC_BATCH * n_pages
    n_pool = n_used + max(n_used // 4, 1)

    def nrm(k, shape, s):
        return jax.random.normal(k, shape, f32) * s

    def gain(k, shape):
        return 1.0 + 0.02 * jax.random.normal(k, shape, f32)

    page_table = jax.random.permutation(ks[9], n_pool)[:n_used].reshape(DEC_BATCH, n_pages).astype(jnp.int32)
    dt = jnp.exp(jax.random.uniform(ks[17], (DEPTH, GDN_HEADS), f32, math.log(1e-3), math.log(1e-1)))
    return {
        'x_prompt': nrm(ks[0], (BATCH, SEQ, D_MODEL), 1.0),
        'x_sample': nrm(ks[1], (DEC_BATCH, DEC_SEQ, D_MODEL), 1.0),
        'p_prompt': nrm(ks[2], (DEPTH, BATCH, SEQ, PLE_DIM), 1.0),
        'p_sample': nrm(ks[3], (DEPTH, DEC_BATCH, DEC_SEQ, PLE_DIM), 1.0),
        'cache_fox_k': nrm(ks[4], (DEPTH, n_pool, PAGE_SIZE, FOX_HEADS, FOX_HD), 1.0),
        'cache_fox_v': nrm(ks[5], (DEPTH, n_pool, PAGE_SIZE, FOX_HEADS, FOX_HD), 1.0),
        'cache_fox_logf': jax.nn.log_sigmoid(FOX_F_BIAS + nrm(ks[6], (DEPTH, n_pool, PAGE_SIZE, FOX_HEADS), 1.0)),
        'state_gdn': nrm(ks[7], (DEPTH, DEC_BATCH, GDN_HEADS, GDN_DK, GDN_DV), 0.3),
        'state_conv': nrm(ks[8], (DEPTH, DEC_BATCH, CONV_W - 1, CONV_CH), 1.0),
        'page_table': page_table,
        'norm_mix_g': gain(ks[10], (DEPTH, D_MODEL)),
        'w_in': nrm(ks[11], (DEPTH, D_MODEL, N_IN), D_MODEL ** -0.5),
        'fox_f_bias': FOX_F_BIAS + nrm(ks[12], (DEPTH, FOX_HEADS), 0.1),
        'fox_q_norm': gain(ks[13], (DEPTH, FOX_HD)),
        'fox_k_norm': gain(ks[14], (DEPTH, FOX_HD)),
        'gdn_conv_w': nrm(ks[15], (DEPTH, CONV_W, CONV_CH), CONV_W ** -0.5),
        'gdn_a_log': jnp.log(jax.random.uniform(ks[16], (DEPTH, GDN_HEADS), f32, 1.0, 16.0)),
        'gdn_dt_bias': dt + jnp.log(-jnp.expm1(-dt)),
        'gdn_norm_g': gain(ks[18], (DEPTH, GDN_DV)),
        'w_up_fox': nrm(ks[19], (DEPTH, FOX_W, D_MODEL), FOX_W ** -0.5),
        'w_up_gdn': nrm(ks[20], (DEPTH, GDN_VW, D_MODEL), GDN_VW ** -0.5),
        'w_out': nrm(ks[21], (DEPTH, D_MODEL, D_MODEL), D_MODEL ** -0.5),
        'norm_ffn_g': gain(ks[22], (DEPTH, D_MODEL)),
        'peer_w_q': nrm(ks[23], (DEPTH, D_MODEL, PEER_HEADS * 2 * PEER_DK), D_MODEL ** -0.5),
        'peer_sub_keys': nrm(ks[24], (DEPTH, PEER_HEADS, 2, N_KEYS, PEER_DK), PEER_DK ** -0.5),
        'peer_u': nrm(ks[25], (DEPTH, N_EXPERTS, D_MODEL), D_MODEL ** -0.5),
        'peer_v': nrm(ks[26], (DEPTH, N_EXPERTS, D_MODEL), PEER_HEADS ** -0.5),
        'norm_ple_g': gain(ks[27], (DEPTH, D_MODEL)),
        'w_ple': nrm(ks[28], (DEPTH, PLE_DIM, D_MODEL), PLE_DIM ** -0.5),
        'w_ple_gate': nrm(ks[29], (DEPTH, D_MODEL, D_MODEL), D_MODEL ** -0.5),
    }

def reference(x_prompt, x_sample, p_prompt, p_sample, cache_fox_k, cache_fox_v, cache_fox_logf, state_gdn, state_conv, page_table,
              norm_mix_g, w_in, fox_f_bias, fox_q_norm, fox_k_norm, gdn_conv_w, gdn_a_log, gdn_dt_bias, gdn_norm_g,
              w_up_fox, w_up_gdn, w_out, norm_ffn_g, peer_w_q, peer_sub_keys, peer_u, peer_v, norm_ple_g, w_ple, w_ple_gate):
    xp, xs = x_prompt, x_sample
    kp_l, vp_l, lfp_l, sp_l, cp_l = [], [], [], [], []
    ks_l, vs_l, lfs_l, ss_l, cs_l = [], [], [], [], []
    for i in range(DEPTH):
        lw = {
            'norm_mix_g': norm_mix_g[i], 'w_in': w_in[i], 'fox_f_bias': fox_f_bias[i],
            'fox_q_norm': fox_q_norm[i], 'fox_k_norm': fox_k_norm[i], 'gdn_conv_w': gdn_conv_w[i],
            'gdn_a_log': gdn_a_log[i], 'gdn_dt_bias': gdn_dt_bias[i], 'gdn_norm_g': gdn_norm_g[i],
            'w_up_fox': w_up_fox[i], 'w_up_gdn': w_up_gdn[i], 'w_out': w_out[i], 'norm_ffn_g': norm_ffn_g[i],
            'peer_w_q': peer_w_q[i], 'peer_sub_keys': peer_sub_keys[i], 'peer_u': peer_u[i], 'peer_v': peer_v[i],
            'norm_ple_g': norm_ple_g[i], 'w_ple': w_ple[i], 'w_ple_gate': w_ple_gate[i],
        }
        xp, kp, vp, lfp, sp, cp = block_prompt(xp, p_prompt[i], lw)
        xs, ks_, vs_, lfs, ss, cs = block_sample(xs, p_sample[i], cache_fox_k, cache_fox_v, cache_fox_logf,
                                                 state_gdn[i], state_conv[i], page_table, i, lw)
        kp_l.append(kp); vp_l.append(vp); lfp_l.append(lfp.astype(cache_fox_logf.dtype))
        sp_l.append(sp.astype(state_gdn.dtype)); cp_l.append(cp.astype(state_conv.dtype))
        ks_l.append(ks_); vs_l.append(vs_); lfs_l.append(lfs.astype(cache_fox_logf.dtype))
        ss_l.append(ss.astype(state_gdn.dtype)); cs_l.append(cs.astype(state_conv.dtype))
    fox_k_prompt = jnp.stack(kp_l)
    fox_v_prompt = jnp.stack(vp_l)
    fox_logf_prompt = jnp.stack(lfp_l)
    gdn_state_prompt = jnp.stack(sp_l)
    conv_state_prompt = jnp.stack(cp_l)
    fox_k_sample = jnp.stack(ks_l)
    fox_v_sample = jnp.stack(vs_l)
    fox_logf_sample = jnp.stack(lfs_l)
    gdn_state_sample = jnp.stack(ss_l)
    conv_state_sample = jnp.stack(cs_l)
    return (xp, xs, fox_k_prompt, fox_v_prompt, fox_logf_prompt, gdn_state_prompt, conv_state_prompt,
            fox_k_sample, fox_v_sample, fox_logf_sample, gdn_state_sample, conv_state_sample)


_drawn_inputs = setup_inputs


def setup_inputs(seed=0):
    import zlib

    import numpy as np

    out = dict(_drawn_inputs(seed))
    spreads = {}
    factors = {'cache_fox_logf': 200.0,
     'fox_q_norm': 22.511,
     'fox_k_norm': 8.157,
     'gdn_norm_g': 11.951,
     'norm_ple_g': 200.0,
     'norm_ffn_g': 3.702}
    for name, (base, spread) in spreads.items():
        noise = np.random.default_rng([zlib.crc32(name.encode()), seed]).standard_normal(out[name].shape)
        drawn = base * np.exp(spread * noise) if base else spread * noise
        out[name] = __import__('jax').numpy.asarray(drawn.astype(out[name].dtype))
    for name, factor in factors.items():
        out[name] = (out[name] * factor).astype(out[name].dtype)
    return out
```

```python
from contextlib import ExitStack

import numpy as np
import concourse.bass as bass
from concourse import mybir

ALU = mybir.AluOpType
ACT = mybir.ActivationFunctionType
AX = mybir.AxisListType
F32 = mybir.dt.float32
I32 = mybir.dt.int32
U32 = mybir.dt.uint32

P = 128
D_MODEL = 2048
KT = D_MODEL // P
SEQ, NS = 256, 8
T = SEQ + NS
NH = 8
PAGES = 8
POOL = 80
PEER_K = 16
N_KEYS = 128
PLE_KT = 2
EPS = 1e-6
SCALE = 128 ** -0.5
NEG = -1e30
BIGNEG = -3e38
LEVELS = 7
RING = 4
HALF = N_KEYS // 2
PGW = NH * P + NH
EG = 4

W_PHASES = [("A", 56), ("gates", 32), ("up", 16), ("out", 16), ("wq", 16), ("u", 128), ("ple", 16)]

JOB_LIST = [("norm0", 1), ("A", 56), ("small", 1), ("fqk", 16), ("gqk", 16), ("cum", 1), ("bc", 1), ("fvt", 4),
            ("fs", 8), ("fpt", 8), ("fo", 4),
            ("gdk", 16), ("gat", 4), ("inv", 12 * LEVELS), ("gkt", 4), ("gvt", 4), ("gu", 4), ("gw", 2),
            ("gs1", 2), ("gq", 2), ("gws", 2), ("go", 4), ("gs2", 2),
            ("sg1", 1), ("sgk", 2), ("sgd", 2), ("sgo", 16), ("gn", 8),
            ("gates0", 16), ("smt", 1), ("smb", 1), ("sden", 1), ("gates1", 16), ("up", 16), ("out", 16),
            ("norm1", 1), ("wq", 16), ("route", 15)]
for _h in range(2):
    JOB_LIST += [(f"wb{_h}", 33), (f"u{_h}", 64)]
JOB_LIST += [("norm2", 1), ("ple", 16)]
JOB = {}
_n = 0
for _name, _c in JOB_LIST:
    JOB[_name] = _n
    _n += _c

RS_JOB = [JOB["route"] + o for o in (0, 4, 9)]
IDX_JOB = [JOB["route"] + o for o in (8, 13, 14)]

C_ID, C_ONE, C_UPI, C_LOW, C_IOTA, C_INV, C_CAUS, C_ZERO = 0, 128, 256, 384, 512, 640, 1536, 1920
C_EPS, C_EPS128, C_END = 1984, 1985, 1986


def constants():
    i = np.arange(P)[:, None]
    j = np.arange(P)[None, :]
    c = np.zeros((P, C_END), np.float32)
    c[:, C_ID:C_ID + P] = i == j
    c[:, C_ONE:C_ONE + P] = 1
    c[:, C_UPI:C_UPI + P] = i <= j
    c[:, C_LOW:C_LOW + P] = i > j
    c[:, C_IOTA:C_IOTA + P] = j
    for lv in range(LEVELS):
        s = 1 << lv
        c[:, C_INV + lv * P:C_INV + (lv + 1) * P] = (i // (2 * s) == j // (2 * s)) & (i // s % 2 == 1) & (j // s % 2 == 0)
    caus = np.where(j > i, NEG, 0)
    c[:, C_CAUS:C_CAUS + P] = caus
    c[:, C_CAUS + 2 * P:C_CAUS + 3 * P] = caus
    c[:, C_EPS] = EPS
    c[:, C_EPS128] = P * EPS
    return c


G_MIX, G_FFN, G_PLE, G_FQ, G_FK, G_GN, G_CONV, G_BIAS, G_ALOG, G_END = 0, 16, 32, 48, 49, 50, 51, 147, 171, 179


def build(nc, xT, pT, wd, vd, wsmall, wple, subk, kx, vx, state, convst, params, consts, ptab,
          o_x, o_k, o_v, o_lf, o_sp, o_ss, o_cs):
    with ExitStack() as ctx:
        NF = 53100
        arena = ctx.enter_context(nc.sbuf_tensor("arena", [P, NF], F32))
        ptb = ctx.enter_context(nc.sbuf_tensor("ptb", [1, NS * PAGES], I32))
        ps = ctx.enter_context(nc.psum_tensor("ps", [P, 8, 512], F32))
        top = [0]

        def take(n):
            a = top[0]
            top[0] += n
            assert top[0] <= NF, top[0]
            return a

        def at(a, n, p=P):
            return arena[0:p, a:a + n]

        CST = take(C_END)
        PAR = take(G_END)
        XT = take(KT * T)
        HT = take(KT * T)
        WR = take(RING * D_MODEL)
        small_base = take(820)
        BIG = top[0]
        PT = take(56 * T)
        OT = take(2 * NH * T)
        PG = take(8 * PGW)
        SC = take(6144)
        BIG_END = NF

        cst = lambda c, n=P, p=P: arena[0:p, CST + c:CST + c + n]
        par = lambda c, n=1, p=P: arena[0:p, PAR + c:PAR + c + n]
        ident, ones, upi, low = cst(C_ID), cst(C_ONE), cst(C_UPI), cst(C_LOW)
        eps, eps128 = cst(C_EPS, 1), cst(C_EPS128, 1)
        wr = lambda j: at(WR + j * D_MODEL, D_MODEL)
        blk = lambda base, b: at(base + b * T, T)
        xt3 = at(XT, KT * T).rearrange("p (k t) -> p k t", t=T)
        ht3 = at(HT, KT * T).rearrange("p (k t) -> p k t", t=T)
        pt3 = at(PT, 56 * T).rearrange("p (k t) -> p k t", t=T)
        ot3 = at(OT, 2 * NH * T).rearrange("p (k t) -> p k t", t=T)
        page = lambda j: at(PG + j * PGW, PGW)

        st_top = [small_base]

        def stake(n):
            a = st_top[0]
            st_top[0] += n
            assert st_top[0] <= small_base + 820, st_top[0] - small_base
            return a

        LGB = stake(72)
        EXS = stake(48)
        BEG = stake(16)
        BCS = stake(256)
        QS = stake(64)
        KS = stake(64)
        VS = stake(64)
        NEGM = stake(16)
        SUMS = stake(16)
        DEL = stake(64)
        ALE = stake(8)
        PSF = stake(64)
        lgb = at(LGB, 72).rearrange("p (c k) -> p c k", c=3)

        SMX, SMU, SMY, SMZ, SMZ2, SMP = (SC + 5184 + 72 * i for i in range(6))
        CST_ST = SC + 3100
        CACC, CSAMP, CPROD, CCOPY = SC + 1500, SC + 2012, SC + 2204, SC + 2396

        WH = BIG
        VR = WH + HALF * T
        AB = VR + EG * D_MODEL
        IDX = AB + 2 * EG * T
        OHA = IDX + 3 * T
        OHB = OHA + 2 * 8 * HALF
        assert OHB + 2 * 8 * P <= BIG_END, OHB + 2 * 8 * P
        QT = BIG
        SK = QT + 16 * T
        RS = SK + 16 * P
        RS2 = RS + 2048
        CA = RS2 + 2048
        CA2 = CA + 2048
        SV = CA2 + 2048
        SI = SV + 256
        SIF = SI + 256
        CV = SIF + 256
        CI = CV + 128
        CSA = CI + 128
        CSB = CSA + 128
        CFA = CSB + 128
        CFB = CFA + 128
        RES = CFB + 128
        RSM = RES + 384
        assert RSM + 32 <= VR + EG * D_MODEL, (RSM, VR)
        GPL = BIG
        WPL = BIG + 16 * T
        PTI = WPL + PLE_KT * D_MODEL
        TMP = PTI + PLE_KT * T

        GT = PT
        MT = SC
        TMU = PT + 40 * T

        def sem(name):
            return ctx.enter_context(nc.semaphore(name))

        pe_job = sem("pe_job")
        evac = [sem(f"evac{b}") for b in range(4)]
        w_loaded = [sem(f"w_loaded{j}") for j in range(RING)]
        v_loaded = [sem(f"v_loaded{j}") for j in range(EG)]
        pg_loaded = [sem(f"pg_loaded{j}") for j in range(PAGES)]
        st_loaded = [sem(f"st_loaded{s}") for s in range(NS)]
        page_done = sem("page_done")
        x_in, c_in, p_in, ws_in, cs_in, pt_in, sk_in, ple_in = (sem(n) for n in (
            "x_in", "c_in", "p_in", "ws_in", "cs_in", "pt_in", "sk_in", "ple_in"))
        out_dma = sem("out_dma")
        state_saved = sem("state_saved")
        sq_ready, rt_ready, ht_ready = sem("sq_ready"), sem("rt_ready"), sem("ht_ready")
        bsq_ready, brt_ready, bn_ready = sem("bsq_ready"), sem("brt_ready"), sem("bn_ready")
        dch, ach, pch = sem("dve_chain"), sem("act_chain"), sem("pool_chain")
        sm_u, sm_e = sem("small_u"), sem("small_e")
        gates_ready = sem("token_gates_ready")
        conv_acc, conv_out = sem("conv_acc"), sem("conv_out")
        lfl_ready = sem("lfl_ready")
        neg_ready, prob_raw, prob_ready = sem("neg_ready"), sem("prob_raw"), sem("prob_ready")
        dec_ready, a_ready = sem("dec_ready"), sem("a_ready")
        t_init = sem("t_init")
        kd_ready, vb_ready, gb_ready, qe_ready = sem("kd_ready"), sem("vb_ready"), sem("gb_ready"), sem("qe_ready")
        vn_ready, s2_ready = sem("vn_ready"), sem("s2_ready")
        kqm_ready, del_ready, dm_ready, dmn_ready, st_ready = (sem(n) for n in (
            "kqm_ready", "del_ready", "dm_ready", "dmn_ready", "st_ready"))
        bcx_ready, og_ready, lfd_ready = sem("bcx_ready"), sem("og_ready"), sem("lfd_ready")
        mx_ready, dg_ready, sp_in, sp_exp, sp_ready, of_ready = (sem(n) for n in (
            "mx_ready", "dg_ready", "sp_in", "sp_exp", "sp_ready", "of_ready"))
        mt_ready, x1_ready, x2_ready = sem("mt_ready"), sem("x1_ready"), sem("x2_ready")
        re_in, re_exp, res_ready = sem("re_in"), sem("re_exp"), sem("res_ready")
        oha_ready, ohb_ready = sem("oha_ready"), sem("ohb_ready")
        gelu_ready, a_blk = sem("gelu_ready"), sem("a_blk")
        y_done, y_added = sem("y_done"), sem("y_added")
        pw_done, pw_used, fin_ready = sem("pw_done"), sem("pw_used"), sem("fin_ready")
        lf_saved = sem("lf_saved")
        conv_copied, cs_saved, kv_saved, sp_saved, qs_copied = (sem(n) for n in (
            "conv_copied", "cs_saved", "kv_saved", "sp_saved", "qs_copied"))
        eg_ready, convs_ready = sem("eg_ready"), sem("convs_ready")
        mg_step, oh_step = sem("merge_step"), sem("onehot_step")

        def wait_done(eng, n):
            eng.wait_ge(pe_job, n + 1)

        def wait_evac(eng, n):
            eng.wait_ge(evac[n % 4], n // 4 + 1)

        def claim(pe, n):
            if n >= 4:
                wait_evac(pe, n - 4)

        def bank(n):
            return ps[:, n % 4, :]

        class Chain:

            def __init__(self, eng, s):
                self.eng, self.s, self.n = eng, s, 0

            def __call__(self, ins):
                self.n += 1
                ins.then_inc(self.s, 1)
                self.eng.wait_ge(self.s, self.n)

        def unit_job(n):
            for name, count in W_PHASES:
                if n < count:
                    if name == "gates":
                        return JOB["gates0"] + n if n < 16 else JOB["gates1"] + n - 16
                    if name == "u":
                        return JOB["u0"] + n if n < 64 else JOB["u1"] + n - 64
                    return JOB[name] + n
                n -= count

        def load_pages(eng, part, s, odd):
            for j in range(odd, PAGES, 2):
                if part == 0 and isinstance(s, int) and s == 0:
                    if j == odd:
                        eng.wait_ge(state_saved, 16 * NS)
                else:
                    eng.wait_ge(page_done, s * 8 + (64 * part + j - 7))
                r = eng.value_load(ptb[0:1, bass.ds(s * PAGES + j, 1)])
                src = (kx, vx)[part]
                dst = page(j) if part == 0 else page(j)[:, 0:NH * P]
                eng.dma_start(dst, src[bass.ds(r, 1)].rearrange("o p c -> (o p) c")).then_inc(pg_loaded[j], 16)

        W0 = {}
        n0 = 0
        for name, count in W_PHASES:
            W0[name] = n0
            n0 += count

        block = ctx.enter_context(nc.Block())

        @block.sync
        def _(sp):
            sp.dma_start(at(XT, KT * T), xT).then_inc(x_in, 16)
            sp.dma_start(at(CST, C_END), consts).then_inc(c_in, 16)
            sp.dma_start(at(PAR, G_END), params).then_inc(p_in, 16)
            sp.dma_start(at(SC + 4224, 384), wsmall).then_inc(ws_in, 16)
            sp.dma_start(ptb[:, :], ptab).then_inc(pt_in, 16)

            def load_w(n, j):
                sp.dma_start(wr(j), wd[n]).then_inc(w_loaded[j], 16)

            def dyn_w(n, j):
                sp.dma_start(wr(j), wd[bass.ds(n, 1)].rearrange("o p c -> (o p) c")).then_inc(w_loaded[j], 16)

            def peel(n0):
                for j in range(RING):
                    if n0 + j >= RING:
                        sp.wait_ge(pe_job, unit_job(n0 + j - RING) + 1)
                    load_w(n0 + j, j)

            def loop(n0, its):
                peel(n0)
                with sp.Fori(1, its) as it:
                    for j in range(RING):
                        sp.wait_ge(pe_job, it * 4 + (unit_job(n0) - 3 + j))
                        dyn_w(it * 4 + (n0 + j), j)

            loop(W0["A"], 14)

            sp.wait_ge(pt_in, 16)

            for part in range(2):
                g0 = W0["gates"] + 16 * part
                for half in range(2):
                    for j in (2 * half, 2 * half + 1):
                        sp.wait_ge(pe_job, unit_job(g0 + j - RING) + 1)
                        load_w(g0 + j, j)
                    load_pages(sp, part, half, 0)
                with sp.Fori(1, 4) as it:
                    for half in range(2):
                        for j in (2 * half, 2 * half + 1):
                            sp.wait_ge(pe_job, it * 4 + (unit_job(g0) - 3 + j))
                            dyn_w(it * 4 + (g0 + j), j)
                        load_pages(sp, part, it * 2 + half, 0)

            loop(W0["up"], 4)
            loop(W0["out"], 4)
            sp.wait_ge(mt_ready, 1)
            sp.dma_start(at(SK, 16 * P), subk).then_inc(sk_in, 16)
            loop(W0["wq"], 4)

            for half in range(2):
                u0 = W0["u"] + 64 * half
                peel(u0)
                with sp.Fori(1, 16) as it:
                    for j in range(RING):
                        sp.wait_ge(pe_job, it * 4 + (unit_job(u0) - 3 + j))
                        dyn_w(it * 4 + (u0 + j), j)
            loop(W0["ple"], 4)
            for q in range(4):
                sp.wait_ge(fin_ready, 4 * q + 4)
                sp.dma_start(o_x[:, 4 * q * T:(4 * q + 4) * T], at(XT + 4 * q * T, 4 * T)).then_inc(out_dma, 16)
            sp.wait_ge(out_dma, 16 * 4)
            sp.wait_ge(lf_saved, 16)
            sp.wait_ge(cs_saved, 16)
            sp.wait_ge(kv_saved, 32)
            sp.wait_ge(sp_saved, 16)
            sp.wait_ge(state_saved, 16 * NS)

        @block.tensor
        def _(pe):
            mm = nc.tensor.matmul

            def norm(r):
                n = JOB[f"norm{r}"]
                claim(pe, n)
                if r == 0:
                    pe.wait_ge(c_in, 16)
                pe.wait_ge(sq_ready, r + 1)
                for k in range(KT):
                    last = mm(bank(n)[:, 0:T], ones, blk(SC, k), start=(k == 0), stop=(k == KT - 1))
                last.then_inc(pe_job, 1)

            def dense_unit(it, jb, u0, j, src3, kts=range(KT), out_bank=None):
                n = jb + j
                pe.wait_ge(w_loaded[j], it * 16 + 16 * ((u0 + j) // 4 + 1))
                if n >= 4 or not isinstance(it, int):
                    pe.wait_ge(evac[n % 4], it + n // 4)
                for k in range(KT):
                    last = mm(bank(n)[:, 0:T], wr(j)[:, k * P:(k + 1) * P], src3[:, k, :],
                              start=(k == 0), stop=(k == KT - 1))
                last.then_inc(pe_job, 1)

            def dense(name, its, src3, u0=None, jb=None):
                u0 = W0[name] if u0 is None else u0
                jb = JOB[name] if jb is None else jb
                with pe.Fori(0, its) as it:
                    for j in range(RING):
                        dense_unit(it, jb, u0, j, src3)

            norm(0)
            pe.wait_ge(ht_ready, 1)
            for j in range(RING):
                dense_unit(0, JOB["A"], W0["A"], j, ht3)
            with pe.Fori(1, 14) as it:
                for j in range(RING):
                    dense_unit(it, JOB["A"], W0["A"], j, ht3)

            n = JOB["small"]
            claim(pe, n)
            pe.wait_ge(ws_in, 16)
            for c, m in ((0, P), (1, P), (2, NS)):
                for k in range(KT):
                    last = mm(bank(n)[0:m, c * 24:c * 24 + 24], ht3[:, k, c * P:c * P + m],
                              at(SC + 4224 + k * 24, 24), start=(k == 0), stop=(k == KT - 1))
            last.then_inc(pe_job, 1)

            def block_norm(name, count, c0):
                for b in range(count):
                    n = JOB[name] + b
                    claim(pe, n)
                    pe.wait_ge(bsq_ready, c0 + b + 1)
                    mm(bank(n)[:, 0:T], ones, at(SC + (b % 2) * T, T), start=True, stop=True).then_inc(pe_job, 1)

            block_norm("fqk", 16, 0)
            block_norm("gqk", 16, 16)

            n = JOB["cum"]
            claim(pe, n)
            pe.wait_ge(gates_ready, 1)
            g2 = lgb[:, 0:2, 8:16]
            for q, lhs in enumerate((upi, low, ones)):
                last = mm(bank(n)[:, 16 * q:16 * q + 16].rearrange("p (c h) -> p c h", c=2), lhs, g2, start=True, stop=True)
            last.then_inc(pe_job, 1)

            n = JOB["bc"]
            claim(pe, n)
            pe.wait_ge(bcx_ready, 1)
            mm(bank(n)[:, 0:128], cst(C_ONE, P, NS), at(SC + 1200, 128, NS), start=True, stop=True)
            mm(bank(n)[:, 128:192], ones, at(SC + 1328, 64), start=True, stop=True)
            mm(bank(n)[:, 192:256], ones, at(SC + 1392, 64), start=True, stop=True).then_inc(pe_job, 1)

            for q in range(4):
                n = JOB["fvt"] + q
                claim(pe, n)
                for i in range(4):
                    last = nc.tensor.transpose(bank(n)[:, i * P:(i + 1) * P],
                                               pt3[:, 16 + 2 * q + i // 2, (i % 2) * P:(i % 2 + 1) * P], ident)
                last.then_inc(pe_job, 1)
            wait_evac(pe, JOB["fvt"] + 3)
            pe.wait_ge(bn_ready, 32)
            for h in range(NH):
                n = JOB["fs"] + h
                claim(pe, n)
                pe.wait_ge(lfl_ready, 3 * h + 3)
                lfl = lambda i: at(OT + (h % 2) * 384 + i * P, P)
                q, k = pt3[:, h, :], pt3[:, 8 + h, :]
                b = bank(n)
                mm(b[:, 0:P], q[:, 0:P], k[:, 0:P], start=True, stop=False)
                mm(b[:, 0:P], upi, lfl(0), start=False, stop=True)
                mm(b[:, P:2 * P], q[:, P:2 * P], k[:, 0:P], start=True, stop=False)
                mm(b[:, P:2 * P], ones, lfl(0), start=False, stop=False)
                mm(b[:, P:2 * P], upi, lfl(2), start=False, stop=True)
                mm(b[:, 2 * P:3 * P], q[:, P:2 * P], k[:, P:2 * P], start=True, stop=False)
                mm(b[:, 2 * P:3 * P], upi, lfl(1), start=False, stop=True).then_inc(pe_job, 1)
            for h in range(NH):
                n = JOB["fpt"] + h
                claim(pe, n)
                pe.wait_ge(prob_ready, 2 * h + 2)
                for i in range(3):
                    last = nc.tensor.transpose(bank(n)[:, i * P:(i + 1) * P], at(SC + h * 384 + i * P, P), ident)
                last.then_inc(pe_job, 1)
            vn = lambda h, c: at(OT + (8 + h) * T + c * P, P)
            for g in range(4):
                n = JOB["fo"] + g
                claim(pe, n)
                wait_evac(pe, JOB["fpt"] + 2 * g + 1)
                for i in range(2):
                    h = 2 * g + i
                    b = bank(n)[:, i * 256:i * 256 + 256]
                    pt_ = lambda c: at(SC + 3072 + h * 384 + c * P, P)
                    mm(b[:, 0:P], vn(h, 0), pt_(0), start=True, stop=True)
                    mm(b[:, P:2 * P], vn(h, 0), pt_(1), start=True, stop=False)
                    last = mm(b[:, P:2 * P], vn(h, 1), pt_(2), start=False, stop=True)
                last.then_inc(pe_job, 1)

            B1, B2, B3 = SC, SC + 2048, SC + 4096
            B4, B5, B6 = PT, PT + 2048, PT + 4096
            pair = lambda base, h, c: at(base + (2 * h + c) * P, P)
            wait_evac(pe, JOB["fo"] + 3)
            for h in range(NH):
                n = JOB["gdk"] + 2 * h
                claim(pe, n)
                pe.wait_ge(lfl_ready, 24 + 2 * h + 2)
                for c in range(2):
                    gl = at(OT + 8 * T + (h % 2) * 256 + c * P, P)
                    mm(bank(n)[:, c * P:(c + 1) * P], upi, gl, start=True, stop=True)
                    last = mm(bank(n)[:, (2 + c) * P:(3 + c) * P], gl, upi, start=True, stop=True)
                last.then_inc(pe_job, 1)
                n += 1
                claim(pe, n)
                for c in range(2):
                    k = pt3[:, 32 + h, c * P:(c + 1) * P]
                    q = pt3[:, 24 + h, c * P:(c + 1) * P]
                    mm(bank(n)[:, c * P:(c + 1) * P], k, k, start=True, stop=True)
                    last = mm(bank(n)[:, (2 + c) * P:(3 + c) * P], k, q, start=True, stop=True)
                last.then_inc(pe_job, 1)
            for g in range(4):
                n = JOB["gat"] + g
                claim(pe, n)
                pe.wait_ge(a_ready, 2 * g + 2)
                for i in range(4):
                    last = nc.tensor.transpose(bank(n)[:, i * P:(i + 1) * P], at(B1 + (4 * g + i) * P, P), ident)
                last.then_inc(pe_job, 1)
            inv = lambda lv, kind, g: JOB["inv"] + 12 * lv + (g if kind == 0 else 4 + 2 * g + kind - 1)
            pe.wait_ge(t_init, 2)
            for lv in range(LEVELS):
                for g in range(4):
                    n = inv(lv, 0, g)
                    claim(pe, n)
                    if lv == 0:
                        wait_evac(pe, JOB["gat"] + g)
                    else:
                        wait_evac(pe, inv(lv - 1, 1, g))
                    for i in range(4):
                        o = (4 * g + i) * P
                        last = mm(bank(n)[:, i * P:(i + 1) * P], at(B2 + o, P), at(B3 + o, P), start=True, stop=True)
                    last.then_inc(pe_job, 1)
                for g in range(4):
                    for kind in (1, 2):
                        n = inv(lv, kind, g)
                        claim(pe, n)
                        wait_evac(pe, inv(lv, 0, g))
                        if lv:
                            wait_evac(pe, inv(lv - 1, 2, g))
                        for i in range(4):
                            o = (4 * g + i) * P
                            lhs, rhs = (B4, B1) if kind == 1 else (B1, B4)
                            last = mm(bank(n)[:, i * P:(i + 1) * P], at(lhs + o, P), at(rhs + o, P), start=True, stop=True)
                        last.then_inc(pe_job, 1)
            for name, blk0 in (("gkt", 32), ("gvt", 40)):
                for g in range(4):
                    n = JOB[name] + g
                    claim(pe, n)
                    for i in range(4):
                        last = nc.tensor.transpose(bank(n)[:, i * P:(i + 1) * P],
                                                   pt3[:, blk0 + 2 * g + i // 2, (i % 2) * P:(i % 2 + 1) * P], ident)
                    last.then_inc(pe_job, 1)
            for g in range(4):
                n = JOB["gu"] + g
                claim(pe, n)
                wait_evac(pe, JOB["gvt"] + g)
                wait_evac(pe, inv(LEVELS - 1, 2, g))
                for i in range(4):
                    o = (4 * g + i) * P
                    last = mm(bank(n)[:, i * P:(i + 1) * P], at(B4 + o, P), at(B1 + o, P), start=True, stop=True)
                last.then_inc(pe_job, 1)
            for g in range(2):
                n = JOB["gw"] + g
                claim(pe, n)
                wait_evac(pe, JOB["gkt"] + 2 * g + 1)
                for i in range(4):
                    h = 4 * g + i
                    last = mm(bank(n)[:, i * P:(i + 1) * P], pair(B2, h, 1), pair(B4, h, 1), start=True, stop=True)
                last.then_inc(pe_job, 1)
            for g in range(2):
                n = JOB["gs1"] + g
                claim(pe, n)
                wait_evac(pe, JOB["gu"] + 2 * g + 1)
                for i in range(4):
                    h = 4 * g + i
                    last = mm(bank(n)[:, i * P:(i + 1) * P], pair(B3, h, 0), pair(B6, h, 0), start=True, stop=True)
                last.then_inc(pe_job, 1)
            for g in range(2):
                n = JOB["gq"] + g
                claim(pe, n)
                pe.wait_ge(gb_ready, 8)
                for i in range(4):
                    h = 4 * g + i
                    last = mm(bank(n)[:, i * P:(i + 1) * P], at(B2 + h * P, P), upi, start=True, stop=True)
                last.then_inc(pe_job, 1)
            for g in range(2):
                n = JOB["gws"] + g
                claim(pe, n)
                wait_evac(pe, JOB["gw"] + g)
                wait_evac(pe, JOB["gs1"] + g)
                for i in range(4):
                    h = 4 * g + i
                    last = mm(bank(n)[:, i * P:(i + 1) * P], at(B1 + h * P, P), at(B1 + 1024 + h * P, P), start=True, stop=True)
                last.then_inc(pe_job, 1)
            for g in range(4):
                n = JOB["go"] + g
                claim(pe, n)
                wait_evac(pe, JOB["gws"] + g // 2)
                pe.wait_ge(qe_ready, 2)
                for i in range(2):
                    h = 2 * g + i
                    b = bank(n)[:, i * 256:i * 256 + 256]
                    mm(b[:, 0:P], pair(B6, h, 0), pair(B5, h, 0), start=True, stop=True)
                    mm(b[:, P:2 * P], at(B1 + 1024 + h * P, P), pt3[:, 24 + h, P:2 * P], start=True, stop=False)
                    last = mm(b[:, P:2 * P], pair(B6, h, 1), pair(B5, h, 1), start=False, stop=True)
                last.then_inc(pe_job, 1)
            for g in range(2):
                n = JOB["gs2"] + g
                claim(pe, n)
                for i in range(4):
                    h = 4 * g + i
                    last = mm(bank(n)[:, i * P:(i + 1) * P], pair(B3, h, 1), pair(B6, h, 1), start=True, stop=True)
                last.then_inc(pe_job, 1)

            n = JOB["sg1"]
            claim(pe, n)
            for s in range(NS):
                pe.wait_ge(st_loaded[s], 16)
                for h in range(NH):
                    c = (s * NH + h) * 2
                    last = mm(bank(n)[:, c:c + 2], page(s)[:, h * P:(h + 1) * P],
                              pt3[:, 24 + h:33 + h:8, SEQ + s], start=True, stop=True)
            last.then_inc(pe_job, 1)
            for name, srcs in (("sgk", None), ("sgd", DEL)):
                for g in range(2):
                    n = JOB[name] + g
                    claim(pe, n)
                    if srcs is not None:
                        pe.wait_ge(del_ready, 1)
                    for i in range(4):
                        h = 4 * g + i
                        src = pt3[:, 32 + h, SEQ:T] if srcs is None else at(DEL + h * NS, NS)
                        last = nc.tensor.transpose(bank(n)[0:NS, i * P:(i + 1) * P], src, ident)
                    last.then_inc(pe_job, 1)
            for h in range(NH):
                for g in range(2):
                    n = JOB["sgo"] + 2 * h + g
                    claim(pe, n)
                    pe.wait_ge(dmn_ready, h + 1)
                    mm(bank(n), at(B1 + h * P, P, NS), at(B2 + (h % 2) * 1024 + g * 512, 512, NS),
                       start=True, stop=True).then_inc(pe_job, 1)
            block_norm("gn", 8, 32)

            score, attn = ps[:, 4, :], ps[:, 5, :]
            pe.wait_ge(lfd_ready, 1)
            mm(score, cst(C_ONE, P, NS), at(SC + 600, 512, NS), start=True, stop=True, skip_group_check=True)
            mm(attn[:, 0:64], ident, cst(C_ZERO, 64), start=True, stop=True, skip_group_check=True)

            def k_pages(s):
                for j in range(PAGES):
                    pe.wait_ge(pg_loaded[j], s * 16 + 16)
                    for h in range(NH):
                        mm(score[:, s * 64 + j * 8 + h:s * 64 + j * 8 + h + 1], page(j)[:, h * P:(h + 1) * P],
                           at(QS + h * NS + s, 1), start=False, stop=False, skip_group_check=True)
                    lf = page(j)[:, NH * P:PGW]
                    last = mm(score[:, s * 64 + j * 8:s * 64 + j * 8 + 8], low, lf, start=False, stop=False, skip_group_check=True)
                    if j:
                        last = mm(score[:, s * 64:s * 64 + 8 * j].rearrange("p (a b) -> p a b", b=8), ones,
                                  lf.unsqueeze(1).broadcast_to([P, j, 8]), start=False, stop=False, skip_group_check=True)
                    last.then_inc(page_done, 1)

            def v_pages(s):
                for j in range(PAGES):
                    pe.wait_ge(pg_loaded[j], s * 16 + 144)
                    for h in range(NH):
                        last = mm(attn[:, s + h * NS:s + h * NS + 1], page(j)[:, h * P:(h + 1) * P],
                                  at(SC + s * 64 + j * 8 + h, 1), start=False, stop=False, skip_group_check=True)
                    last.then_inc(page_done, 1)

            for it in range(4):
                for half in range(2):
                    for j in (2 * half, 2 * half + 1):
                        dense_unit(it, JOB["gates0"], W0["gates"], j, ht3)
                    k_pages(it * 2 + half)
            n = JOB["smt"]
            claim(pe, n)
            pe.wait_ge(mx_ready, 1)
            nc.tensor.transpose(bank(n)[0:64, 0:P], at(SC + 1200, 64), ident).then_inc(pe_job, 1)
            n = JOB["smb"]
            claim(pe, n)
            pe.wait_ge(dg_ready, 1)
            mm(bank(n)[:, 0:64], cst(C_ONE, P, 64), at(SC + 1300, 64, 64), start=True, stop=True).then_inc(pe_job, 1)
            n = JOB["sden"]
            claim(pe, n)
            pe.wait_ge(sp_ready, 1)
            mm(bank(n)[:, 0:64], ones, at(SC + 1200, 64), start=True, stop=True).then_inc(pe_job, 1)
            for it in range(4):
                for half in range(2):
                    for j in (2 * half, 2 * half + 1):
                        dense_unit(it, JOB["gates1"], W0["gates"] + 16, j, ht3)
                    v_pages(it * 2 + half)

            pe.wait_ge(of_ready, 1)
            with pe.Fori(0, 4) as it:
                for j in range(RING):
                    n = JOB["up"] + j
                    pe.wait_ge(w_loaded[j], it * 16 + 16 * ((W0["up"] + j) // 4 + 1))
                    pe.wait_ge(evac[n % 4], it + n // 4)
                    for half in range(2):
                        for k in range(NH):
                            last = mm(ps[:, n % 4 + 4 * half, 0:T], wr(j)[:, (half * NH + k) * P:(half * NH + k + 1) * P],
                                      ot3[:, half * NH + k, :], start=(k == 0), stop=(k == NH - 1))
                    last.then_inc(pe_job, 1)
            pe.wait_ge(mt_ready, 1)
            mt3 = at(MT, KT * T).rearrange("p (k t) -> p k t", t=T)
            dense("out", 4, mt3)
            norm(1)
            pe.wait_ge(ht_ready, 2)
            dense("wq", 4, ht3)

            pe.wait_ge(sk_in, 16)
            wait_evac(pe, JOB["wq"] + 15)
            def key_scores(c):
                m = P if c < 2 else NS
                for g in range(4):
                    n = RS_JOB[c] + g
                    claim(pe, n)
                    for i in range(4):
                        hp = 4 * g + i
                        last = mm(bank(n)[0:m, i * P:(i + 1) * P], at(QT + hp * T + c * P, m), at(SK + hp * P, P),
                                  start=True, stop=True)
                    last.then_inc(pe_job, 1)

            def turn_results(c):
                m = P if c < 2 else NS
                n = IDX_JOB[c]
                claim(pe, n)
                pe.wait_ge(res_ready, c + 1)
                for i in range(3):
                    last = nc.tensor.transpose(bank(n)[:, i * P:i * P + m], at(RES + i * P, P, m), cst(C_ID, m, m))
                last.then_inc(pe_job, 1)

            key_scores(0)
            key_scores(1)
            turn_results(0)
            key_scores(2)
            turn_results(1)
            turn_results(2)

            for half in range(2):
                wb, ub, g0 = JOB[f"wb{half}"], JOB[f"u{half}"], 16 * half

                def weights_of(it, j):
                    n = wb + j
                    pe.wait_ge(oha_ready, it * 4 + (33 * half + j + 1))
                    pe.wait_ge(ohb_ready, it * 4 + (33 * half + j + 1))
                    pe.wait_ge(evac[n % 4], it + n // 4)
                    for t in range(8):
                        last = mm(bank(n)[:, t * HALF:(t + 1) * HALF], at(OHB + (j % 2) * 8 * P + t * P, P),
                                  at(OHA + (j % 2) * 8 * HALF + t * HALF, HALF), start=True, stop=True)
                    last.then_inc(pe_job, 1)

                with pe.Fori(0, 8) as it:
                    for j in range(4):
                        weights_of(it, j)
                weights_of(8, 0)

                def scores(it):
                    for j in range(RING):
                        dense_unit(it, ub, W0["u"] + 64 * half, j, ht3)

                def outputs(it, buf):
                    for d in range(KT):
                        pe.wait_ge(y_added, it * 16 + (256 * half + d + 1))
                        for j in range(EG):
                            if d == 0:
                                pe.wait_ge(v_loaded[j], it * 16 + 16 * (g0 + 1))
                                pe.wait_ge(a_blk, it * 4 + (4 * g0 + j + 1))
                            last = mm(ps[:, 4 + d % 4, 0:T], at(VR + j * D_MODEL + d * P, P),
                                      at(AB + (buf * EG + j) * T, T), start=(j == 0), stop=(j == EG - 1))
                        last.then_inc(y_done, 1)

                scores(0)
                with pe.Fori(0, 7) as i2:
                    for b in range(2):
                        scores(i2 * 2 + (b + 1))
                        outputs(i2 * 2 + b, b)
                scores(15)
                outputs(14, 0)
                outputs(15, 1)

            norm(2)
            pe.wait_ge(ht_ready, 3)
            pe.wait_ge(ple_in, 32)
            for b in range(16):
                if b >= 4:
                    pe.wait_ge(fin_ready, b - 3)
                for k in range(PLE_KT):
                    last = mm(ps[:, 4 + b % 4, 0:T], at(WPL + k * D_MODEL + b * P, P), at(PTI + k * T, T),
                              start=(k == 0), stop=(k == PLE_KT - 1))
                last.then_inc(pw_done, 1)
                dense_unit(b // 4, JOB["ple"], W0["ple"], b % 4, ht3)

        @block.scalar
        def _(act):
            A = nc.scalar.activation
            self_ = Chain(act, ach)

            def norm(r):
                if r == 0:
                    act.wait_ge(x_in, 16)
                else:
                    act.wait_ge((x1_ready, x2_ready)[r - 1], 1)
                A(at(SC, KT * T), at(XT, KT * T), ACT.Square).then_inc(sq_ready, 1)
                n = JOB[f"norm{r}"]
                wait_done(act, n)
                if r == 0:
                    act.wait_ge(c_in, 16)
                A(at(SC + 4608, T), bank(n)[:, 0:T], ACT.Sqrt, bias=eps, scale=1.0 / D_MODEL).then_inc(evac[n % 4], 1)

            def each_block(name, its, func, base, jb=None, b0=0):
                jb = JOB[name] if jb is None else jb
                with act.Fori(0, its) as it:
                    for j in range(RING):
                        n = jb + j
                        act.wait_ge(pe_job, it * 4 + (n + 1))
                        A(arena[:, bass.ds(it * (4 * T) + (base + (b0 + j) * T), T)], bank(n)[:, 0:T],
                          func).then_inc(evac[n % 4], 1)

            norm(0)
            each_block("A", 14, ACT.Copy, PT)

            act.wait_ge(p_in, 16)
            A(at(ALE, 8), par(G_ALOG, 8), ACT.Exp).then_inc(sm_e, 1)
            act.wait_ge(sm_u, 1)
            A(at(SMY, 72), at(SMU, 72), ACT.Exp, scale=-1.0).then_inc(sm_e, 1)

            def block_norm(name, count, c0, src, scale_bias):
                def square(b):
                    if b >= 2:
                        wait_done(act, JOB[name] + b - 2)
                    A(at(SC + (b % 2) * T, T), src(b), ACT.Square).then_inc(bsq_ready, 1)
                for b in range(2):
                    square(b)
                for b in range(count):
                    n = JOB[name] + b
                    wait_done(act, n)
                    if c0 + b >= 2:
                        act.wait_ge(bn_ready, c0 + b - 1)
                    sc, bi = scale_bias(b)
                    A(at(SC + (2 + b % 2) * T, T), bank(n)[:, 0:T], ACT.Sqrt, bias=bi, scale=sc).then_inc(evac[n % 4], 1)
                    if b + 2 < count:
                        square(b + 2)

            wait_done(act, JOB["small"])
            block_norm("fqk", 16, 0, lambda b: blk(PT, b), lambda b: (1.0, eps128) if b < 8 else (1.0 / P, eps))
            for b in range(24):
                act.wait_ge(conv_acc, b + 1)
                if b == 0:
                    act.wait_ge(conv_copied, 1)
                A(pt3[:, 24 + b, 0:SEQ], at(CACC + (b % 2) * SEQ, SEQ), ACT.Silu).then_inc(conv_out, 1)
            act.wait_ge(convs_ready, 1)
            A(pt3[:, 24:48, SEQ:T], at(CSAMP, 192).rearrange("p (b s) -> p b s", s=NS), ACT.Silu).then_inc(conv_out, 1)
            A(at(PT + 48 * T, 8 * T), at(PT + 48 * T, 8 * T), ACT.Silu).then_inc(conv_out, 1)
            act.wait_ge(conv_out, 26)
            block_norm("gqk", 16, 16, lambda b: blk(PT, 24 + b), lambda b: (float(P), eps128) if b < 8 else (1.0, eps))

            n = JOB["cum"]
            wait_done(act, n)
            A(at(EXS, 48), bank(n)[:, 0:48], ACT.Exp).then_inc(evac[n % 4], 1)

            wait_evac(act, JOB["bc"])
            A(at(BCS, 64), at(BCS, 64), ACT.Exp).then_inc(eg_ready, 1)

            for h in range(NH):
                act.wait_ge(neg_ready, h + 1)
                s = at(SC + h * 384, 384)
                A(s[:, 0:P], s[:, 0:P], ACT.Exp, bias=at(NEGM + 2 * h, 1), accum_out=at(SUMS + 2 * h, 1)).then_inc(prob_raw, 1)
                A(s[:, P:384], s[:, P:384], ACT.Exp, bias=at(NEGM + 2 * h + 1, 1),
                  accum_out=at(SUMS + 2 * h + 1, 1)).then_inc(prob_raw, 1)
            for h in range(NH):
                n = JOB["fpt"] + h
                wait_done(act, n)
                A(at(SC + 3072 + h * 384, 384), bank(n)[:, 0:384], ACT.Copy).then_inc(evac[n % 4], 1)
            for g in range(4):
                n = JOB["fo"] + g
                wait_done(act, n)
                A(ot3[:, 2 * g:2 * g + 2, 0:SEQ], bank(n).rearrange("p (h t) -> p h t", h=2), ACT.Copy).then_inc(evac[n % 4], 1)

            act.wait_ge(kv_saved, 32)
            act.wait_ge(qs_copied, 3)
            B1, B2, B3 = SC, SC + 2048, SC + 4096
            B4, B5, B6 = PT, PT + 2048, PT + 4096
            for h in range(NH):
                n = JOB["gdk"] + 2 * h
                wait_done(act, n)
                if h >= 2:
                    wait_evac(act, n - 3)
                A(at(B6 + (h % 2) * 512, 512), bank(n), ACT.Exp).then_inc(evac[n % 4], 1)
            for g in range(4):
                n = JOB["gat"] + g
                wait_done(act, n)
                A(at(B2 + g * 512, 512), bank(n), ACT.Copy).then_inc(evac[n % 4], 1)
            for name, dst in (("gu", B6), ("gw", B1), ("gs1", B1 + 1024)):
                for g in range(4 if name == "gu" else 2):
                    n = JOB[name] + g
                    wait_done(act, n)
                    if name == "gw" and g == 0:
                        wait_done(act, JOB["gu"] + 3)
                    A(at(dst + g * 512, 512), bank(n), ACT.Copy).then_inc(evac[n % 4], 1)
            for g in range(2):
                n = JOB["gq"] + g
                wait_done(act, n)
                A(at(B2 + 1024 + g * 512, 512), bank(n), ACT.Exp).then_inc(evac[n % 4], 1)
            for g in range(4):
                n = JOB["go"] + g
                wait_done(act, n)
                A(ot3[:, NH + 2 * g:NH + 2 * g + 2, 0:SEQ], bank(n).rearrange("p (h t) -> p h t", h=2), ACT.Copy).then_inc(evac[n % 4], 1)
            for name, dst in (("sgk", B1), ("sgd", B3)):
                for g in range(2):
                    n = JOB[name] + g
                    wait_done(act, n)
                    A(at(dst + g * 512, 512, NS), bank(n)[0:NS, :], ACT.Copy).then_inc(evac[n % 4], 1)
            act.wait_ge(st_ready, 64)
            for s in range(NS):
                act.dma_start(o_ss[s], page(s)[:, 0:NH * P]).then_inc(state_saved, 16)
            act.wait_ge(og_ready, 1)
            act.wait_ge(sp_saved, 16)
            block_norm("gn", 8, 32, lambda b: blk(OT, NH + b), lambda b: (1.0 / P, eps))

            each_block("gates0", 4, ACT.Sigmoid, GT)
            act.wait_ge(sp_in, 1)
            A(at(SC, 512), at(SC, 512), ACT.Exp).then_inc(sp_exp, 1)
            A(at(PSF, 64), at(PSF, 64), ACT.Exp).then_inc(sp_exp, 1)
            each_block("gates1", 4, ACT.Sigmoid, GT, b0=16)

            norm(1)
            each_block("wq", 4, ACT.Copy, QT)
            for c in range(3):
                m = P if c < 2 else NS
                for g in range(4):
                    n = RS_JOB[c] + g
                    wait_done(act, n)
                    if c and g == 0:
                        act.wait_ge(res_ready, c)
                    A(at(RS + 512 * g, 512, m), bank(n)[0:m, :], ACT.Copy).then_inc(evac[n % 4], 1)
                act.wait_ge(re_in, c + 1)
                A(at(RES + 2 * P, P, m), at(RES + 2 * P, P, m), ACT.Exp).then_inc(re_exp, 1)

            wh3 = at(WH, HALF * T).rearrange("p (a t) -> p t a", t=T)
            for half in range(2):
                wb, ub, g0 = JOB[f"wb{half}"], JOB[f"u{half}"], 16 * half
                if half:
                    act.wait_ge(a_blk, 64)
                else:
                    wait_evac(act, IDX_JOB[2])

                def weights_of(it, j):
                    n = wb + j
                    act.wait_ge(pe_job, it * 4 + (n + 1))
                    A(wh3[:, bass.ds(it * 32 + 8 * j, 8), :], bank(n).rearrange("p (t a) -> p t a", t=8),
                      ACT.Copy).then_inc(evac[n % 4], 1)

                with act.Fori(0, 8) as it:
                    for j in range(4):
                        weights_of(it, j)
                weights_of(8, 0)

                def gelu(it, buf):
                    for j in range(RING):
                        n = ub + j
                        act.wait_ge(pe_job, it * 4 + (n + 1))
                        if j == 0 and (half or not isinstance(it, int)):
                            act.wait_ge(y_done, it * 16 + (256 * half - 16))
                        A(at(AB + (buf * EG + j) * T, T), bank(n)[:, 0:T], ACT.Gelu).then_inc(evac[n % 4], 1)

                gelu(0, 0)
                gelu(1, 1)
                with act.Fori(1, 8) as i2:
                    for b in range(2):
                        gelu(i2 * 2 + b, b)

            norm(2)
            each_block("ple", 4, ACT.Sigmoid, GPL)

        @block.gpsimd
        def _(pool):
            pc = Chain(pool, pch)
            wait_done(pool, JOB["norm0"])
            pool.dma_start(at(CST_ST, 576), convst).then_inc(cs_in, 16)
            for s in range(NS):
                pool.dma_start(page(s)[:, 0:NH * P], state[s]).then_inc(st_loaded[s], 16)

            pool.wait_ge(bn_ready, 16)
            pool.dma_start(o_k, at(PT + 8 * T, 8 * T)).then_inc(kv_saved, 16)
            pool.dma_start(o_v, at(PT + 16 * T, 8 * T)).then_inc(kv_saved, 16)
            pool.wait_ge(gates_ready, 1)
            pool.dma_start(o_lf, lgb[:, :, 0:8]).then_inc(lf_saved, 16)
            pool.wait_ge(conv_copied, 1)
            pool.dma_start(o_cs, at(CCOPY, 24 * 27)).then_inc(cs_saved, 16)
            pool.wait_ge(gates_ready, 1)
            wait_evac(pool, JOB["A"] + 55)
            for h in range(NH):
                if h >= 2:
                    wait_done(pool, JOB["fs"] + h - 2)
                for i, (c, m) in enumerate(((0, low), (1, low), (1, ones))):
                    nc.gpsimd.tensor_scalar(at(OT + (h % 2) * 384 + i * P, P), m, lgb[:, c, h:h + 1], 1.0,
                                            ALU.mult, ALU.mult).then_inc(lfl_ready, 1)
            pool.wait_ge(kv_saved, 32)
            pool.wait_ge(qs_copied, 3)
            wait_done(pool, JOB["fo"] + 3)
            for h in range(NH):
                if h >= 2:
                    wait_done(pool, JOB["gdk"] + 2 * h - 4)
                for c in range(2):
                    nc.gpsimd.tensor_scalar(at(OT + 8 * T + (h % 2) * 256 + c * P, P), low, lgb[:, c, 8 + h:9 + h], 1.0,
                                            ALU.mult, ALU.mult).then_inc(lfl_ready, 1)
            B2, B3, B4 = SC + 2048, SC + 4096, PT
            for base in (B3, B4):
                nc.gpsimd.tensor_copy(at(base, 2048).rearrange("p (a b) -> p a b", b=P),
                                      ident.unsqueeze(1).broadcast_to([P, 16, P])).then_inc(t_init, 1)
            wait_done(pool, JOB["gw"] + 1)
            for h in range(NH):
                nc.gpsimd.tensor_scalar(at(B2 + h * P, P), ones, lgb[:, 1, 8 + h:9 + h], 1.0,
                                        ALU.mult, ALU.mult).then_inc(gb_ready, 1)
            pool.wait_ge(s2_ready, 8)
            pool.dma_start(o_sp, at(SC + 1024, 1024)).then_inc(sp_saved, 16)

            pool.wait_ge(sp_saved, 16)
            pool.wait_ge(pt_in, 16)
            for part in range(2):
                load_pages(pool, part, 0, 1)
                with pool.Fori(1, 8) as s:
                    load_pages(pool, part, s, 1)

            wait_evac(pool, IDX_JOB[2])

            def v_load(g, j):
                pool.dma_start(at(VR + j * D_MODEL, D_MODEL), g).then_inc(v_loaded[j], 16)

            for j in range(EG):
                v_load(vd[j], j)
            with pool.Fori(1, 32) as g:
                pool.wait_ge(y_done, g * 16)
                for j in range(EG):
                    v_load(vd[bass.ds(g * 4 + j, 1)].rearrange("o p c -> (o p) c"), j)

            pool.wait_ge(y_done, 512)
            pool.dma_start(at(WPL, PLE_KT * D_MODEL), wple).then_inc(ple_in, 16)
            pool.dma_start(at(PTI, PLE_KT * T), pT).then_inc(ple_in, 16)

        @block.vector
        def _(dve):
            V = nc.vector
            ch = Chain(dve, dch)

            def norm(r, gain):
                n = JOB[f"norm{r}"]
                wait_evac(dve, n)
                rt = at(SC + 4608, T)
                ch(V.reciprocal(rt, rt))
                if r == 0:
                    dve.wait_ge(p_in, 16)
                for k in range(KT):
                    last = V.scalar_tensor_tensor(out=ht3[:, k, :], in0=xt3[:, k, :], scalar=par(gain + k), in1=rt,
                                                  op0=ALU.mult, op1=ALU.mult)
                last.then_inc(ht_ready, 1)

            for b in range(4):
                dve.sem_inc(y_added, 1)
            norm(0, G_MIX)

            smx = at(SMX, 72).rearrange("p (c k) -> p c k", c=3)
            smu = at(SMU, 72).rearrange("p (c k) -> p c k", c=3)
            dve.wait_ge(ws_in, 16)
            wait_done(dve, JOB["small"])
            ch(V.memset(at(SMX, 72), 0.0))
            bias = par(G_BIAS, 24)
            b3 = bank(JOB["small"])[:, 0:72].rearrange("p (c k) -> p c k", c=3)
            ch(V.tensor_tensor(smx[:, 0:2, :], b3[:, 0:2, :], bias.unsqueeze(1).broadcast_to([P, 2, 24]), ALU.add))
            V.tensor_tensor(smx[0:NS, 2, :], b3[0:NS, 2, :], par(G_BIAS, 24, NS), ALU.add).then_inc(evac[JOB["small"] % 4], 1)
            wait_evac(dve, JOB["small"])
            ch(V.tensor_scalar(smx[:, :, 0:8], smx[:, :, 0:8], -1.0, None, ALU.mult))
            ch(V.scalar_tensor_tensor(out=smu[:, :, 0:16], in0=smx[:, :, 0:16], scalar=-1.0, in1=smx[:, :, 0:16],
                                      op0=ALU.mult, op1=ALU.max))
            V.tensor_copy(smu[:, :, 16:24], smx[:, :, 16:24]).then_inc(sm_u, 1)
            dve.wait_ge(sm_e, 2)
            y, z, z2, pl = at(SMY, 72), at(SMZ, 72), at(SMZ2, 72), at(SMP, 72)
            ch(V.tensor_scalar(z, y, 2.0, None, ALU.add))
            ch(V.reciprocal(z, z))
            ch(V.tensor_tensor(z, z, y, ALU.mult))
            ch(V.tensor_tensor(z2, z, z, ALU.mult))
            ch(V.tensor_scalar(pl, z2, 1.0 / 21, None, ALU.mult))
            for k in (19, 17, 15, 13, 11, 9, 7, 5, 3):
                ch(V.scalar_tensor_tensor(out=pl, in0=pl, scalar=1.0 / k, in1=z2, op0=ALU.add, op1=ALU.mult))
            ch(V.scalar_tensor_tensor(out=pl, in0=pl, scalar=1.0, in1=z, op0=ALU.add, op1=ALU.mult))
            ch(V.tensor_scalar(at(SMX, 72), at(SMX, 72), 0.0, None, ALU.max))
            ch(V.scalar_tensor_tensor(out=pl, in0=pl, scalar=2.0, in1=at(SMX, 72), op0=ALU.mult, op1=ALU.add))
            pl3 = pl.rearrange("p (c k) -> p c k", c=3)
            y3 = y.rearrange("p (c k) -> p c k", c=3)
            V.tensor_scalar(lgb[:, :, 0:8], pl3[:, :, 0:8], -1.0, None, ALU.mult).then_inc(dch, 1)
            ch.n += 1
            ch(V.scalar_tensor_tensor(out=lgb[:, :, 8:16], in0=pl3[:, :, 8:16], scalar=-1.0,
                                      in1=at(ALE, 8).unsqueeze(1).broadcast_to([P, 3, 8]), op0=ALU.mult, op1=ALU.mult))
            ch(V.tensor_scalar(y3[:, :, 16:24], y3[:, :, 16:24], 1.0, None, ALU.add))
            V.reciprocal(lgb[:, :, 16:24], y3[:, :, 16:24]).then_inc(gates_ready, 1)

            def block_norm(name, count, c0, src, factor, extra=None):
                for b in range(count):
                    n = JOB[name] + b
                    wait_evac(dve, n)
                    rt = at(SC + (2 + b % 2) * T, T)
                    ch(V.reciprocal(rt, rt))
                    x = src(b)
                    ins = V.scalar_tensor_tensor(out=x, in0=x, scalar=factor(b), in1=rt, op0=ALU.mult, op1=ALU.mult)
                    if extra is None:
                        ins.then_inc(bn_ready, 1)
                    else:
                        ch(ins)
                        V.tensor_tensor(x, x, extra(b), ALU.mult).then_inc(bn_ready, 1)

            block_norm("fqk", 16, 0, lambda b: blk(PT, b), lambda b: par(G_FQ if b < 8 else G_FK))
            dve.wait_ge(bn_ready, 16)
            for dst, b0 in ((QS, 0), (KS, 8), (VS, 16)):
                V.tensor_copy(at(dst, 64).rearrange("p (h s) -> p h s", s=NS), pt3[:, b0:b0 + 8, SEQ:T]).then_inc(qs_copied, 1)

            dve.wait_ge(cs_in, 16)
            st4 = at(CST_ST, 576).rearrange("p (b s j) -> p b s j", s=NS, j=3)
            cp3 = at(CCOPY, 24 * 27).rearrange("p (b c) -> p b c", c=27)
            cps = cp3[:, :, 3:27].rearrange("p b (s j) -> p b s j", j=3)
            wj = lambda j: par(G_CONV + 24 * j, 24).unsqueeze(2).broadcast_to([P, 24, NS])
            c24 = lambda a: at(a, 192).rearrange("p (b s) -> p b s", s=NS)
            V.tensor_copy(cp3[:, :, 0:3], pt3[:, 24:48, SEQ - 3:SEQ])
            V.tensor_copy(cps[:, :, :, 0:2], st4[:, :, :, 1:3])
            V.tensor_copy(cps[:, :, :, 2], pt3[:, 24:48, SEQ:T]).then_inc(conv_copied, 1)
            ch(V.tensor_tensor(c24(CSAMP), pt3[:, 24:48, SEQ:T], wj(3), ALU.mult))
            for j in range(3):
                ch(V.tensor_tensor(c24(CPROD), st4[:, :, :, j], wj(j), ALU.mult))
                ch(V.tensor_tensor(c24(CSAMP), c24(CSAMP), c24(CPROD), ALU.add))
            dve.sem_inc(convs_ready, 1)
            for b in range(24):
                if b >= 2:
                    dve.wait_ge(conv_out, b - 1)
                a0 = CACC + (b % 2) * SEQ
                x = pt3[:, 24 + b, :]
                w = lambda j: par(G_CONV + 24 * j + b)
                ch(V.tensor_scalar(at(a0, SEQ), x[:, 0:SEQ], w(3), None, ALU.mult))
                for j in (2, 1, 0):
                    d = 3 - j
                    ins = V.scalar_tensor_tensor(out=at(a0 + d, SEQ - d), in0=x[:, 0:SEQ - d], scalar=w(j),
                                                 in1=at(a0 + d, SEQ - d), op0=ALU.mult, op1=ALU.add)
                    if j:
                        ch(ins)
                    else:
                        ins.then_inc(conv_acc, 1)
            block_norm("gqk", 16, 16, lambda b: blk(PT, 24 + b), lambda b: 1.0)
            dve.wait_ge(bn_ready, 32)

            wait_evac(dve, JOB["cum"])
            ch(V.tensor_tensor(at(BEG, 16).rearrange("p (c h) -> p c h", c=2), lgb[:, 0:2, 16:24],
                               at(EXS, 16).rearrange("p (c h) -> p c h", c=2), ALU.mult))
            eyeb = cst(C_ID, NS, NS).unsqueeze(2).broadcast_to([NS, NS, NH])
            x3 = lambda a: at(a, 64, NS).rearrange("p (s h) -> p s h", h=NH)
            V.tensor_tensor(x3(SC + 1200), lgb[0:NS, 2, 8:16].unsqueeze(1).broadcast_to([NS, NS, NH]), eyeb, ALU.mult)
            V.tensor_tensor(x3(SC + 1264), lgb[0:NS, 2, 16:24].unsqueeze(1).broadcast_to([NS, NS, NH]), eyeb, ALU.mult)
            sh = lambda a: at(a, 64).rearrange("p (s h) -> p h s", h=NH)
            hs = lambda a: at(a, 64).rearrange("p (h s) -> p h s", s=NS)
            dve.wait_ge(qs_copied, 3)
            V.tensor_tensor(sh(SC + 1328), hs(QS), hs(KS), ALU.mult)
            V.tensor_tensor(sh(SC + 1392), pt3[:, 24:32, SEQ:T], pt3[:, 32:40, SEQ:T], ALU.mult).then_inc(bcx_ready, 1)
            n = JOB["bc"]
            wait_done(dve, n)
            V.tensor_copy(at(BCS, 256), bank(n)[:, 0:256]).then_inc(evac[n % 4], 1)

            for q in range(4):
                n = JOB["fvt"] + q
                wait_done(dve, n)
                V.tensor_copy(ot3[:, 8 + 2 * q:10 + 2 * q, 0:SEQ], bank(n).rearrange("p (h t) -> p h t", h=2)).then_inc(evac[n % 4], 1)

            dve.wait_ge(cs_saved, 16)
            for h in range(NH):
                n = JOB["fs"] + h
                wait_done(dve, n)
                s = at(SC + h * 384, 384)
                V.tensor_tensor(s, bank(n)[:, 0:384], cst(C_CAUS, 384), ALU.add).then_inc(evac[n % 4], 1)
                wait_evac(dve, n)
                ch(V.tensor_reduce(at(NEGM + 2 * h, 1), s[:, 0:P], AX.X, ALU.max, negate=True))
                V.tensor_reduce(at(NEGM + 2 * h + 1, 1), s[:, P:384], AX.X, ALU.max, negate=True).then_inc(neg_ready, 1)
            for h in range(NH):
                dve.wait_ge(prob_raw, 2 * h + 2)
                ch(V.reciprocal(at(SUMS + 2 * h, 2), at(SUMS + 2 * h, 2)))
                s = at(SC + h * 384, 384)
                V.tensor_scalar(s[:, 0:P], s[:, 0:P], at(SUMS + 2 * h, 1), None, ALU.mult).then_inc(prob_ready, 1)
                V.tensor_scalar(s[:, P:384], s[:, P:384], at(SUMS + 2 * h + 1, 1), None, ALU.mult).then_inc(prob_ready, 1)

            B1, B2, B3 = SC, SC + 2048, SC + 4096
            B4, B5, B6 = PT, PT + 2048, PT + 4096
            dve.wait_ge(kv_saved, 32)
            for h in range(NH):
                nd, nk = JOB["gdk"] + 2 * h, JOB["gdk"] + 2 * h + 1
                wait_evac(dve, nd)
                d0 = B6 + (h % 2) * 512
                two = lambda a: at(a, 256).rearrange("p (c t) -> p c t", c=2)
                V.tensor_tensor(two(d0), two(d0), low.unsqueeze(1).broadcast_to([P, 2, P]), ALU.mult).then_inc(dch, 1)
                ch.n += 1
                ch(V.tensor_tensor(two(d0 + 256), two(d0 + 256), upi.unsqueeze(1).broadcast_to([P, 2, P]), ALU.mult))
                wait_done(dve, nk)
                for c in range(2):
                    ins = V.scalar_tensor_tensor(out=at(B1 + (2 * h + c) * P, P), in0=bank(nk)[:, c * P:(c + 1) * P],
                                                 scalar=lgb[:, c, 16 + h:17 + h], in1=at(d0 + c * P, P),
                                                 op0=ALU.mult, op1=ALU.mult)
                ins.then_inc(a_ready, 1)
                V.tensor_tensor(at(B5 + h * 256, 256), bank(nk)[:, 256:512], at(d0 + 256, 256), ALU.mult).then_inc(evac[nk % 4], 1)
            inv = lambda lv, kind, g: JOB["inv"] + 12 * lv + (g if kind == 0 else 4 + 2 * g + kind - 1)
            dve.wait_ge(t_init, 2)
            for lv in range(LEVELS):
                mask = cst(C_INV + lv * P).unsqueeze(1).broadcast_to([P, 4, P])
                for g in range(4):
                    n = inv(lv, 0, g)
                    wait_done(dve, n)
                    V.tensor_tensor(at(B1 + g * 512, 512).rearrange("p (a b) -> p a b", b=P),
                                    bank(n).rearrange("p (a b) -> p a b", b=P), mask, ALU.mult).then_inc(evac[n % 4], 1)
                for g in range(4):
                    for kind, base in ((1, B3), (2, B4)):
                        n = inv(lv, kind, g)
                        wait_done(dve, n)
                        if lv:
                            wait_evac(dve, inv(lv - 1, kind, g))
                        t = at(base + g * 512, 512)
                        V.tensor_tensor(t, t, bank(n), ALU.subtract).then_inc(evac[n % 4], 1)
            for g in range(4):
                n = JOB["gkt"] + g
                wait_done(dve, n)
                for i in range(4):
                    h, c = 2 * g + i // 2, i % 2
                    o = (4 * g + i) * P
                    V.tensor_scalar(at(B2 + o, P), bank(n)[:, i * P:(i + 1) * P], at(BEG + c * 8 + h, 1), None, ALU.mult)
                    ins = V.tensor_scalar(at(B3 + o, P), bank(n)[:, i * P:(i + 1) * P], at(EXS + 16 + c * 8 + h, 1), None, ALU.mult)
                ins.then_inc(evac[n % 4], 1)
            for g in range(4):
                n = JOB["gvt"] + g
                wait_done(dve, n)
                for i in range(4):
                    h, c = 2 * g + i // 2, i % 2
                    ins = V.tensor_scalar(at(B1 + (4 * g + i) * P, P), bank(n)[:, i * P:(i + 1) * P],
                                          lgb[:, c, 16 + h:17 + h], None, ALU.mult)
                ins.then_inc(evac[n % 4], 1)
            for g in range(2):
                wait_evac(dve, JOB["gq"] + g)
                q = pt3[:, 24 + 4 * g:28 + 4 * g, P:2 * P]
                V.tensor_tensor(q, q, at(B2 + 1024 + g * 512, 512).rearrange("p (h t) -> p h t", t=P), ALU.mult).then_inc(qe_ready, 1)
            u1 = at(B6, 2048).rearrange("p (h c t) -> p h c t", c=2, t=P)[:, :, 1, :]
            for g in range(2):
                n = JOB["gws"] + g
                wait_done(dve, n)
                V.tensor_tensor(u1[:, 4 * g:4 * g + 4, :], u1[:, 4 * g:4 * g + 4, :],
                                bank(n).rearrange("p (h t) -> p h t", t=P), ALU.subtract).then_inc(evac[n % 4], 1)
            for g in range(2):
                n = JOB["gs2"] + g
                wait_done(dve, n)
                for i in range(4):
                    h = 4 * g + i
                    s1 = at(B1 + 1024 + h * P, P)
                    ins = V.scalar_tensor_tensor(out=s1, in0=s1, scalar=at(EXS + 40 + h, 1), in1=bank(n)[:, i * P:(i + 1) * P],
                                                 op0=ALU.mult, op1=ALU.add)
                    if i < 3:
                        ins.then_inc(s2_ready, 1)
                    else:
                        ins.then_inc(evac[n % 4], 1)
                wait_evac(dve, n)
                dve.sem_inc(s2_ready, 1)

            n = JOB["sg1"]
            wait_done(dve, n)
            sg = bank(n)[:, 0:128].rearrange("p (s h q) -> p h s q", h=NH, q=2)
            egs, bes, kqs = sh(BCS), sh(BCS + 64), sh(BCS + 192)
            dve.wait_ge(eg_ready, 1)
            dl, os_ = hs(DEL), ot3[:, 8:16, SEQ:T]
            ch(V.tensor_tensor(dl, sg[:, :, :, 1], egs, ALU.mult))
            V.tensor_tensor(os_, sg[:, :, :, 0], egs, ALU.mult).then_inc(evac[n % 4], 1)
            wait_evac(dve, n)
            ch(V.tensor_tensor(dl, pt3[:, 40:48, SEQ:T], dl, ALU.subtract))
            V.tensor_tensor(dl, dl, bes, ALU.mult).then_inc(del_ready, 1)
            dve.wait_ge(del_ready, 1)
            ch(V.tensor_tensor(hs(PSF), dl, kqs, ALU.mult))
            ch(V.tensor_tensor(os_, os_, hs(PSF), ALU.add))
            for g in range(4):
                wait_evac(dve, JOB["go"] + g)
            dve.sem_inc(og_ready, 1)
            wait_evac(dve, JOB["sgd"])
            wait_evac(dve, JOB["sgd"] + 1)
            for h in range(NH):
                if h >= 2:
                    wait_done(dve, JOB["sgo"] + 2 * h - 3)
                V.tensor_tensor(at(B2 + (h % 2) * 1024, 1024, NS).rearrange("p (s e) -> p s e", e=P),
                                at(B3 + h * P, P, NS).unsqueeze(1).broadcast_to([NS, NS, P]),
                                cst(C_ID, NS, NS).unsqueeze(2).broadcast_to([NS, NS, P]), ALU.mult).then_inc(dmn_ready, 1)
                for g in range(2):
                    n = JOB["sgo"] + 2 * h + g
                    wait_done(dve, n)
                    for i in range(4):
                        s = 4 * g + i
                        st = page(s)[:, h * P:(h + 1) * P]
                        ins = V.scalar_tensor_tensor(out=st, in0=st, scalar=at(BCS + s * NH + h, 1),
                                                     in1=bank(n)[:, i * P:(i + 1) * P], op0=ALU.mult, op1=ALU.add)
                    ins.then_inc(evac[n % 4], 1)
            wait_evac(dve, JOB["sgo"] + 15)
            dve.sem_inc(st_ready, 64)
            block_norm("gn", 8, 32, lambda b: blk(OT, NH + b), lambda b: par(G_GN), extra=lambda b: blk(PT, 48 + b))

            for pg in range(PAGES):
                ins = V.tensor_tensor(at(SC + 600, 512, NS).rearrange("p (s g h) -> p s g h", g=PAGES, h=NH)[:, :, pg, :],
                                      lgb[0:NS, 2, 0:8].unsqueeze(1).broadcast_to([NS, NS, NH]), eyeb, ALU.mult)
            ins.then_inc(lfd_ready, 1)
            dve.wait_ge(page_done, 64)
            sc4 = lambda ap: ap.rearrange("p (s g h) -> p s h g", g=PAGES, h=NH)
            flat = lambda a: at(a, 64).rearrange("p (s h) -> p s h", h=NH)
            ch(V.tensor_reduce(flat(SC + 1200), sc4(ps[:, 4, :]), AX.X, ALU.max))
            V.tensor_tensor(at(SC + 1200, 64), at(SC + 1200, 64), at(BCS + 128, 64), ALU.max).then_inc(mx_ready, 1)
            n = JOB["smt"]
            wait_done(dve, n)
            V.tensor_reduce(at(SC + 1400, 1, 64), bank(n)[0:64, 0:P], AX.X, ALU.max).then_inc(evac[n % 4], 1)
            wait_evac(dve, n)
            V.tensor_scalar(at(SC + 1300, 64, 64), cst(C_ID, 64, 64), at(SC + 1400, 1, 64), None, ALU.mult).then_inc(dg_ready, 1)
            n = JOB["smb"]
            wait_done(dve, n)
            V.tensor_copy(at(SC + 1410, 64), bank(n)[:, 0:64]).then_inc(evac[n % 4], 1)
            wait_evac(dve, n)
            ch(V.tensor_tensor(at(PSF, 64), at(BCS + 128, 64), at(SC + 1410, 64), ALU.subtract))
            for s in range(NS):
                ins = V.tensor_tensor(at(SC + s * 64, 64).rearrange("p (g h) -> p g h", h=NH),
                                      ps[:, 4, s * 64:(s + 1) * 64].rearrange("p (g h) -> p g h", h=NH),
                                      at(SC + 1410 + s * 8, 8).unsqueeze(1).broadcast_to([P, PAGES, NH]), ALU.subtract)
            ins.then_inc(sp_in, 1)
            dve.wait_ge(sp_exp, 2)
            V.tensor_reduce(flat(SC + 1200), sc4(at(SC, 512)), AX.X, ALU.add).then_inc(sp_ready, 1)
            n = JOB["sden"]
            wait_done(dve, n)
            V.tensor_tensor(at(SC + 1300, 64), bank(n)[:, 0:64], at(PSF, 64), ALU.add).then_inc(evac[n % 4], 1)
            wait_evac(dve, n)
            ch(V.reciprocal(at(SC + 1300, 64), at(SC + 1300, 64)))
            ch(V.tensor_tensor(hs(SC + 1400), hs(VS), sh(PSF), ALU.mult))
            dve.wait_ge(page_done, 128)
            ch(V.tensor_tensor(hs(SC + 1400), hs(SC + 1400), ps[:, 5, 0:64].rearrange("p (h s) -> p h s", s=NS), ALU.add))
            V.tensor_tensor(ot3[:, 0:8, SEQ:T], hs(SC + 1400), sh(SC + 1300), ALU.mult).then_inc(of_ready, 1)
            wait_evac(dve, JOB["gates1"] + 15)

            dve.wait_ge(of_ready, 1)
            with dve.Fori(0, 4) as it:
                for j in range(RING):
                    n = JOB["up"] + j
                    dve.wait_ge(pe_job, it * 4 + (n + 1))
                    m = arena[:, bass.ds(it * (4 * T) + (MT + j * T), T)]
                    ga = arena[:, bass.ds(it * (4 * T) + (GT + j * T), T)]
                    gb = arena[:, bass.ds(it * (4 * T) + (GT + (16 + j) * T), T)]
                    t = at(TMU + (j % 2) * T, T)
                    V.tensor_tensor(t, gb, ps[:, 4 + n % 4, 0:T], ALU.mult).then_inc(mg_step, 1)
                    V.tensor_tensor(m, ga, ps[:, n % 4, 0:T], ALU.mult).then_inc(mg_step, 1)
                    dve.wait_ge(mg_step, it * 8 + (2 * j + 2))
                    V.tensor_tensor(m, m, t, ALU.add).then_inc(evac[n % 4], 1)
            wait_evac(dve, JOB["up"] + 15)
            dve.sem_inc(mt_ready, 1)

            def add_to_x(jb, done):
                with dve.Fori(0, 4) as it:
                    for j in range(RING):
                        n = jb + j
                        dve.wait_ge(pe_job, it * 4 + (n + 1))
                        x = arena[:, bass.ds(it * (4 * T) + (XT + j * T), T)]
                        V.tensor_tensor(x, x, bank(n)[:, 0:T], ALU.add).then_inc(evac[n % 4], 1)
                wait_evac(dve, jb + 15)
                dve.sem_inc(done, 1)

            add_to_x(JOB["out"], x1_ready)
            norm(1, G_FFN)

            for c in range(3):
                m = P if c < 2 else NS

                def v(a, n):
                    return at(a, n, m)

                for g in range(4):
                    wait_evac(dve, RS_JOB[c] + g)

                def top16(src, src2, vals, idxs, count, width):
                    for q in range(count):
                        ch(V.max(out=v(vals + 16 * q, 8), in_=v(src + width * q, width)))
                        V.max_index(v(idxs + 16 * q, 8).bitcast(U32), v(vals + 16 * q, 8), v(src + width * q, width))
                        ch(V.match_replace(v(src2 + width * q, width), v(vals + 16 * q, 8), v(src + width * q, width), BIGNEG))
                        ch(V.max(out=v(vals + 16 * q + 8, 8), in_=v(src2 + width * q, width)))
                        ch(V.max_index(v(idxs + 16 * q + 8, 8).bitcast(U32), v(vals + 16 * q + 8, 8), v(src2 + width * q, width)))

                top16(RS, RS2, SV, SI, 16, P)
                sv = v(SV, 256).rearrange("p (h q k) -> p h q k", q=2, k=16)
                ca = v(CA, 2048).rearrange("p (h i j) -> p h i j", i=16, j=16)
                for h in range(NH):
                    ch(V.tensor_tensor(ca[:, h], sv[:, h, 0, :].unsqueeze(2).broadcast_to([m, 16, 16]),
                                       sv[:, h, 1, :].unsqueeze(1).broadcast_to([m, 16, 16]), ALU.add))
                top16(CA, CA2, CV, CI, 8, 256)
                ch(V.tensor_copy(v(SIF, 256), v(SI, 256).bitcast(U32)))
                ch(V.tensor_scalar(v(CSA, P).bitcast(U32), v(CI, P).bitcast(U32), 4, None, ALU.logical_shift_right))
                ch(V.tensor_scalar(v(CSB, P).bitcast(U32), v(CI, P).bitcast(U32), 15, None, ALU.bitwise_and))
                ch(V.tensor_copy(v(CFA, P), v(CSA, P).bitcast(U32)))
                ch(V.tensor_copy(v(CFB, P), v(CSB, P).bitcast(U32)))
                if c:
                    wait_done(dve, IDX_JOB[c - 1])
                for side, cf in ((0, CFA), (1, CFB)):
                    eq = v(CA, 2048).rearrange("p (a j) -> p a j", j=16)
                    ch(V.tensor_tensor(eq, v(cf, P).unsqueeze(2).broadcast_to([m, P, 16]),
                                       cst(C_IOTA, 16, m).unsqueeze(1).broadcast_to([m, P, 16]), ALU.is_equal))
                    e4 = v(CA, 2048).rearrange("p (h k j) -> p h k j", k=16, j=16)
                    sif = v(SIF, 256).rearrange("p (h q k) -> p h q k", q=2, k=16)
                    for h in range(NH):
                        ins = V.tensor_tensor(e4[:, h], e4[:, h], sif[:, h, side, :].unsqueeze(1).broadcast_to([m, 16, 16]), ALU.mult)
                    ch(ins)
                    ch(V.tensor_reduce(v(RES + side * P, P), eq, AX.X, ALU.add))
                cv = v(CV, P).rearrange("p (h k) -> p h k", k=16)
                gt = v(RES + 2 * P, P).rearrange("p (h k) -> p h k", k=16)
                V.tensor_tensor(gt, cv, cv[:, :, 0:1].broadcast_to([m, 8, 16]), ALU.subtract).then_inc(re_in, 1)
                dve.wait_ge(re_exp, c + 1)
                ch(V.tensor_reduce(v(RSM, 8), gt, AX.X, ALU.add))
                ch(V.reciprocal(v(RSM, 8), v(RSM, 8)))
                V.tensor_tensor(gt, gt, v(RSM, 8).unsqueeze(2).broadcast_to([m, 8, 16]), ALU.mult).then_inc(res_ready, 1)
                n = IDX_JOB[c]
                wait_done(dve, n)
                V.tensor_copy(at(IDX, 3 * T).rearrange("p (i t) -> p i t", t=T)[:, :, c * P:c * P + m],
                              bank(n)[:, 0:384].rearrange("p (i t) -> p i t", t=P)[:, :, 0:m]).then_inc(evac[n % 4], 1)
            wait_evac(dve, IDX_JOB[2])

            for half in range(2):
                wb, ub, g0 = JOB[f"wb{half}"], JOB[f"u{half}"], 16 * half

                def onehot_a(it, j, lead):
                    if not lead:
                        dve.wait_ge(pe_job, it * 4 + (wb + j - 1))
                    oh = at(OHA + (j % 2) * 8 * HALF, 8 * HALF).rearrange("p (t a) -> p t a", a=HALF)
                    col = lambda q: arena[:, bass.ds(it * 32 + (IDX + q * T + 8 * j), 8)].unsqueeze(2).broadcast_to([P, 8, HALF])
                    V.tensor_tensor(oh, cst(C_IOTA + half * HALF, HALF).unsqueeze(1).broadcast_to([P, 8, HALF]), col(0),
                                    ALU.is_equal).then_inc(oh_step, 1)
                    dve.wait_ge(oh_step, it * 4 + (33 * half + j + 1))
                    V.tensor_tensor(at(OHB + (j % 2) * 8 * P, 8 * P).rearrange("p (t b) -> p t b", b=P),
                                    cst(C_IOTA).unsqueeze(1).broadcast_to([P, 8, P]),
                                    arena[:, bass.ds(it * 32 + (IDX + T + 8 * j), 8)].unsqueeze(2).broadcast_to([P, 8, P]),
                                    ALU.is_equal).then_inc(ohb_ready, 1)
                    V.tensor_tensor(oh, oh, col(2), ALU.mult).then_inc(oha_ready, 1)

                if half:
                    wait_done(dve, JOB["wb0"] + 32)
                for j in range(4):
                    onehot_a(0, j, j < 2)
                with dve.Fori(1, 8) as it:
                    for j in range(4):
                        onehot_a(it, j, False)
                onehot_a(8, 0, False)
                for b in range(4):
                    wait_evac(dve, wb + 29 + b)

                def weigh(it, buf):
                    for j in range(RING):
                        n = ub + j
                        dve.wait_ge(evac[n % 4], it + (n // 4 + 1))
                        a = at(AB + (buf * EG + j) * T, T)
                        V.tensor_tensor(a, a, arena[:, bass.ds(it * (4 * T) + (WH + j * T), T)], ALU.mult).then_inc(a_blk, 1)

                def add_outputs(it):
                    for d in range(KT):
                        dve.wait_ge(y_done, it * 16 + (256 * half + d + 1))
                        V.tensor_tensor(xt3[:, d, :], xt3[:, d, :], ps[:, 4 + d % 4, 0:T], ALU.add).then_inc(y_added, 1)

                weigh(0, 0)
                with dve.Fori(0, 7) as i2:
                    for b in range(2):
                        weigh(i2 * 2 + (b + 1), 1 - b)
                        add_outputs(i2 * 2 + b)
                weigh(15, 1)
                add_outputs(14)
                add_outputs(15)
            dve.wait_ge(y_added, 516)
            dve.sem_inc(x2_ready, 1)
            norm(2, G_PLE)
            for b in range(16):
                n = JOB["ple"] + b
                wait_evac(dve, n)
                dve.wait_ge(pw_done, b + 1)
                t = at(TMP + (b % 2) * T, T)
                ch(V.tensor_tensor(t, blk(GPL, b), ps[:, 4 + b % 4, 0:T], ALU.mult))
                V.tensor_tensor(xt3[:, b, :], xt3[:, b, :], t, ALU.add).then_inc(fin_ready, 1)


def kernel(**inputs):
    import concourse.bacc as bacc
    from concourse.bass_utils import run_bass_kernel_spmd

    x = {k: np.asarray(v) for k, v in inputs.items()}
    c = np.ascontiguousarray
    FW = NH * P
    OFF_F, OFF_G = 3 * FW, 3 * FW + NH
    OFF_A = OFF_G + 3 * FW
    OFF_Z = OFF_A + 2 * NH
    OFF_GATE = OFF_Z + FW
    w_in = x["w_in"][0]

    def blocks(w):
        k, n = w.shape
        return w.reshape(k // P, P, n // P, P).transpose(2, 1, 0, 3).reshape(n // P, P, k)

    def cols(a, tiles):
        return c(a.reshape(T, tiles, P).transpose(2, 1, 0)).reshape(P, tiles * T)

    up = np.concatenate([x["w_up_fox"][0], x["w_up_gdn"][0]], 0)
    wd = np.concatenate([
        blocks(w_in[:, 0:OFF_F]), blocks(w_in[:, OFF_G:OFF_A]), blocks(w_in[:, OFF_Z:OFF_GATE]),
        blocks(w_in[:, OFF_GATE:]), blocks(up), blocks(x["w_out"][0]), blocks(x["peer_w_q"][0]),
        x["peer_u"][0].reshape(N_KEYS, P, KT, P).transpose(0, 3, 2, 1).reshape(N_KEYS, P, D_MODEL),
        blocks(x["w_ple_gate"][0])], 0)
    small = np.concatenate([w_in[:, OFF_F:OFF_G], w_in[:, OFF_A:OFF_Z]], 1)
    rows = lambda v: np.broadcast_to(v, (P, v.shape[-1]))
    gain = lambda v: v.reshape(-1, P).T
    params = np.zeros((P, G_END), np.float32)
    params[:, G_MIX:G_FFN] = gain(x["norm_mix_g"][0])
    params[:, G_FFN:G_PLE] = gain(x["norm_ffn_g"][0])
    params[:, G_PLE:G_FQ] = gain(x["norm_ple_g"][0])
    params[:, G_FQ] = x["fox_q_norm"][0]
    params[:, G_FK] = x["fox_k_norm"][0]
    params[:, G_GN] = x["gdn_norm_g"][0]
    params[:, G_CONV:G_BIAS] = x["gdn_conv_w"][0].reshape(4, 24, P).transpose(2, 0, 1).reshape(P, 96)
    params[:, G_BIAS:G_BIAS + 8] = rows(x["fox_f_bias"])
    params[:, G_BIAS + 8:G_BIAS + 16] = rows(x["gdn_dt_bias"])
    params[:, G_ALOG:G_END] = rows(x["gdn_a_log"])
    kx = np.concatenate([x["cache_fox_k"][0].transpose(0, 3, 2, 1).reshape(POOL, P, FW), x["cache_fox_logf"][0]], 2)

    arrays = {
        "xT": cols(np.concatenate([x["x_prompt"][0], x["x_sample"][:, 0]], 0), KT),
        "pT": cols(np.concatenate([x["p_prompt"][0, 0], x["p_sample"][0, :, 0]], 0), PLE_KT),
        "wd": wd, "vd": x["peer_v"][0].reshape(N_KEYS, P, D_MODEL),
        "wsmall": c(small.reshape(KT, P, 24).transpose(1, 0, 2)).reshape(P, KT * 24),
        "wple": c(x["w_ple"][0].reshape(PLE_KT, P, D_MODEL).transpose(1, 0, 2)).reshape(P, PLE_KT * D_MODEL),
        "subk": c(x["peer_sub_keys"][0].transpose(3, 0, 1, 2)).reshape(P, 16 * P),
        "kx": kx, "vx": x["cache_fox_v"][0].reshape(POOL, P, FW),
        "state": x["state_gdn"][0].transpose(0, 2, 1, 3).reshape(NS, P, FW),
        "convst": x["state_conv"][0].reshape(NS, 3, 24, P).transpose(3, 2, 0, 1).reshape(P, 576),
        "params": params, "consts": constants(),
        "ptab": x["page_table"].reshape(1, NS * PAGES).astype(np.int32),
    }
    nc = bacc.Bacc("TRN2", target_bir_lowering=False, num_devices=1)
    args = []
    for k, a in arrays.items():
        arrays[k] = a = c(a)
        args.append(nc.dram_tensor("in_" + k, a.shape, mybir.dt.from_np(a.dtype), kind="ExternalInput").ap())
    outs = {"o_x": (P, KT * T), "o_k": (P, NH * T), "o_v": (P, NH * T), "o_lf": (P, 3, NH), "o_sp": (P, FW),
            "o_ss": (NS, P, FW), "o_cs": (P, 24 * 27)}
    for k, s in outs.items():
        args.append(nc.dram_tensor(k, s, F32, kind="ExternalOutput").ap())
    build(nc, *args)
    r = run_bass_kernel_spmd(nc, [{"in_" + k: a for k, a in arrays.items()}], core_ids=[0]).results[0]

    tok = lambda a, tiles: np.asarray(a).reshape(P, tiles, T).transpose(2, 1, 0)
    y = tok(r["o_x"], KT).reshape(T, D_MODEL)
    k, v = tok(r["o_k"], NH), tok(r["o_v"], NH)
    lf = np.asarray(r["o_lf"]).transpose(1, 0, 2)
    sp = np.asarray(r["o_sp"]).reshape(P, NH, P).transpose(1, 0, 2)
    ss = np.asarray(r["o_ss"]).reshape(NS, P, NH, P).transpose(0, 2, 1, 3)
    cs = np.asarray(r["o_cs"]).reshape(P, 24, 27)
    cp = cs[:, :, 0:3].transpose(2, 1, 0).reshape(3, 3 * FW)
    css = cs[:, :, 3:].reshape(P, 24, NS, 3).transpose(2, 3, 1, 0).reshape(NS, 3, 3 * FW)
    return (c(y[None, :SEQ]), c(y[SEQ:, None]), c(k[None, None, :SEQ]), c(v[None, None, :SEQ]),
            c(lf[0:2].reshape(1, 1, SEQ, NH)), c(sp[None, None]), c(cp[None, None]),
            c(k[None, SEQ:, None]), c(v[None, SEQ:, None]), c(lf[2, 0:NS].reshape(1, NS, 1, NH)),
            c(ss[None]), c(css[None]))
```

```python
from contextlib import ExitStack

import numpy as np
import concourse.bass as bass
from concourse import mybir

ALU = mybir.AluOpType
ACT = mybir.ActivationFunctionType
AX = mybir.AxisListType
F32 = mybir.dt.float32
F32R = mybir.dt.float32r
I32 = mybir.dt.int32
U32 = mybir.dt.uint32

P = 128
D_MODEL = 2048
KT = D_MODEL // P
SEQ, NS = 256, 8
T = SEQ + NS
NH = 8
PAGES = 8
POOL = 80
PEER_K = 16
N_KEYS = 128
PLE_KT = 2
EPS = 1e-6
SCALE = 128 ** -0.5
NEG = -1e30
BIGNEG = -3e38
LEVELS = 7
RING = 4
QK = KT // RING
HALF = N_KEYS // 2
PGW = NH * P
EG = 4

STREAM = [("A", 56), ("gates", 32), ("up", 16), ("out", 16), ("wq", 16), ("peer0", 128), ("peer1", 128), ("ple", 16)]
S0 = {}
_n = 0
for _name, _c in STREAM:
    S0[_name] = _n
    _n += _c

JOB_LIST = [("norm0", 1), ("A", 56), ("small", 1), ("fqk", 16), ("gqk", 16), ("cum", 1), ("bc", 1), ("fvt", 4),
            ("fs", 8), ("fpt", 8), ("fo", 4),
            ("gdk", 16), ("gat", 4), ("inv", 12 * LEVELS), ("gkt", 4), ("gvt", 4), ("gu", 4), ("gw", 2),
            ("gs1", 2), ("gq", 2), ("gws", 2), ("go", 4), ("gs2", 2),
            ("sg1", 1), ("sgk", 2), ("sgd", 2), ("sgo", 16), ("gn", 8),
            ("slf", 1), ("sown", 1),
            ("gates0", 16), ("spt", 1), ("spb", 1), ("gates1", 16), ("sot", 1), ("up", 16), ("out", 16),
            ("norm1", 1), ("wq", 16), ("route", 15)]
for _h in range(2):
    JOB_LIST += [(f"wb{_h}", 33), (f"u{_h}", 64)]
JOB_LIST += [("norm2", 1), ("ple", 16)]
JOB = {}
SPLIT_JOBS = ("A", "gates0", "gates1", "out", "wq", "u0", "u1", "ple")
PJ = []
_n = _p = 0
for _name, _c in JOB_LIST:
    JOB[_name] = _n
    for _ in range(_c):
        _p += _name not in SPLIT_JOBS
        PJ.append(_p)
    _n += _c


def split_index(s):
    return s if s < S0["up"] else s - 16


def stream_of(n):
    for name, s in (("A", S0["A"]), ("gates0", S0["gates"]), ("gates1", S0["gates"] + 16), ("out", S0["out"]),
                    ("wq", S0["wq"]), ("ple", S0["ple"])):
        count = dict(JOB_LIST)[name]
        if JOB[name] <= n < JOB[name] + count:
            return s + n - JOB[name]
    for h in range(2):
        k = n - JOB[f"u{h}"]
        if 0 <= k < 64:
            return S0[f"peer{h}"] + (k if k < 4 else 4 + 8 * ((k - 4) // 4) + k % 4)
    return None


RS_JOB = [JOB["route"] + o for o in (0, 4, 9)]
IDX_JOB = [JOB["route"] + o for o in (8, 13, 14)]

C_ID, C_ONE, C_UPI, C_LOW, C_IOTA, C_INV, C_CAUS, C_ZERO = 0, 128, 256, 384, 512, 640, 1536, 1920
C_EPS, C_EPS128, C_END = 1984, 1985, 1986


def constants():
    i = np.arange(P)[:, None]
    j = np.arange(P)[None, :]
    c = np.zeros((P, C_END), np.float32)
    c[:, C_ID:C_ID + P] = i == j
    c[:, C_ONE:C_ONE + P] = 1
    c[:, C_UPI:C_UPI + P] = i <= j
    c[:, C_LOW:C_LOW + P] = i > j
    c[:, C_IOTA:C_IOTA + P] = j
    for lv in range(LEVELS):
        s = 1 << lv
        c[:, C_INV + lv * P:C_INV + (lv + 1) * P] = (i // (2 * s) == j // (2 * s)) & (i // s % 2 == 1) & (j // s % 2 == 0)
    caus = np.where(j > i, NEG, 0)
    c[:, C_CAUS:C_CAUS + P] = caus
    c[:, C_CAUS + 2 * P:C_CAUS + 3 * P] = caus
    c[:, C_EPS] = EPS
    c[:, C_EPS128] = P * EPS
    return c


G_MIX, G_FFN, G_PLE, G_FQ, G_FK, G_GN, G_CONV, G_BIAS, G_ALOG, G_END = 0, 16, 32, 48, 49, 50, 51, 147, 171, 179


def build(nc, xT, pT, wd, vd, wsmall, wple, subk, kx, vx, lx, state, convst, params, consts, ptab,
          o_x, o_k, o_v, o_lf, o_sp, o_ss, o_cs):
    with ExitStack() as ctx:
        NF, NR = 36332, 16768
        arena = ctx.enter_context(nc.sbuf_tensor("arena", [P, NF], F32))
        split = ctx.enter_context(nc.sbuf_tensor("split", [P, NR], F32R))
        ptb = ctx.enter_context(nc.sbuf_tensor("ptb", [1, NS * PAGES], I32))
        ps = ctx.enter_context(nc.psum_tensor("ps", [P, 8, 512], F32))
        top = [0]

        def take(n):
            a = top[0]
            top[0] += n
            assert top[0] <= NF, top[0]
            return a

        def at(a, n, p=P):
            return arena[0:p, a:a + n]

        CST = take(C_END)
        PAR = take(G_END)
        small_base = take(820)
        WR = take(RING * D_MODEL)
        XT = take(KT * T)
        SC = XT
        BIG = top[0]
        take(6144 - KT * T)
        PT = take(56 * T)
        OT = take(2 * NH * T)
        BIG_END = NF
        PG = PT + 32 * T
        SQ = PT
        HRAW = PT + KT * T

        HH, HL = 0, KT * T
        CKH = 2 * KT * T
        CKL = CKH + D_MODEL
        AH = CKL + D_MODEL
        AL = AH + 2 * EG * T
        WSH, WSL = AH, AH + 384
        assert AL + 2 * EG * T <= NR
        sp_ = lambda a, n: split[:, a:a + n]
        as_f32 = lambda ap: ap.bitcast(F32)
        hh3 = sp_(HH, KT * T).rearrange("p (k t) -> p k t", t=T)
        hl3 = sp_(HL, KT * T).rearrange("p (k t) -> p k t", t=T)
        QW = QK * P
        ckh = lambda q: sp_(CKH + q * QW, QW)
        ckl = lambda q: sp_(CKL + q * QW, QW)

        cst = lambda c, n=P, p=P: arena[0:p, CST + c:CST + c + n]
        par = lambda c, n=1, p=P: arena[0:p, PAR + c:PAR + c + n]
        ident, ones, upi, low = cst(C_ID), cst(C_ONE), cst(C_UPI), cst(C_LOW)
        eps, eps128 = cst(C_EPS, 1), cst(C_EPS128, 1)
        wr = lambda j: at(WR + j * D_MODEL, D_MODEL)
        blk = lambda base, b: at(base + b * T, T)
        xt3 = at(XT, KT * T).rearrange("p (k t) -> p k t", t=T)
        pt3 = at(PT, 56 * T).rearrange("p (k t) -> p k t", t=T)
        ot3 = at(OT, 2 * NH * T).rearrange("p (k t) -> p k t", t=T)
        page = lambda j: at(PG + (j % 4) * PGW, PGW)
        state_of = lambda s: at(WR + s * NH * P, NH * P)

        st_top = [small_base]

        def stake(n):
            a = st_top[0]
            st_top[0] += n
            assert st_top[0] <= small_base + 820, st_top[0] - small_base
            return a

        LGB = stake(72)
        EXS = stake(48)
        BEG = stake(16)
        BCS = stake(256)
        QS = stake(64)
        KS = stake(64)
        VS = stake(64)
        NEGM = stake(16)
        SUMS = stake(16)
        DEL = stake(64)
        ALE = stake(8)
        PSF = stake(64)
        lgb = at(LGB, 72).rearrange("p (c k) -> p c k", c=3)

        SMX, SMU, SMY, SMZ, SMZ2, SMP = (SC + 5184 + 72 * i for i in range(6))
        CST_ST = SC + 3100
        CACC, CSAMP, CPROD, CCOPY = SC + 1500, SC + 2012, SC + 2204, SC + 2396

        WH = BIG
        AB = WH + HALF * T
        IDX = AB + 2 * T
        assert IDX + 3 * T <= BIG_END, IDX + 3 * T
        OHA = WR + 2 * D_MODEL
        OHB = OHA + 2 * 8 * HALF
        assert OHB + 2 * 8 * P <= WR + RING * D_MODEL
        QT = BIG
        RS = QT + 16 * T
        RS2 = RS + 2048
        CA = RS2 + 2048
        CA2 = CA + 2048
        SV = CA2 + 2048
        SI = SV + 256
        SIF = SI + 256
        CV = SIF + 256
        CI = CV + 128
        CSA = CI + 128
        CSB = CSA + 128
        CFA = CSB + 128
        CFB = CFA + 128
        RES = CFB + 128
        RSM = RES + 384
        SK = RSM + 32
        assert SK >= HRAW + KT * T and SK + 16 * P <= IDX
        GPL = BIG
        WPL = HRAW + KT * T
        PTI = WPL + PLE_KT * D_MODEL
        TMP = PTI + PLE_KT * T

        GT = PT
        TMU = PT + 40 * T

        def sem(name):
            return ctx.enter_context(nc.semaphore(name))

        QM = SC
        LFR = SC + 4096
        LF = LFR + NH * P
        LFS = LF + 512
        PROB = SC
        PRT = PROB + PAGES * P
        OSEL = PRT + 1024
        ON = OSEL + NH * P
        OWN = LFR

        pe_job = sem("pe_job")
        evac = [sem(f"evac{b}") for b in range(4)]
        w_loaded = [sem(f"w_loaded{j}") for j in range(RING)]
        quarter_done = sem("quarter_done")
        hi_ready, lo_ready = sem("hi_ready"), sem("lo_ready")
        hraw_ready, hh_ready = sem("hraw_ready"), sem("hh_ready")
        merged, mh_ready = sem("merged"), sem("mh_ready")
        ws_hi, ws_lo = sem("ws_hi"), sem("ws_lo")
        x_again = sem("x_again")
        aw_ready, ah_ready = sem("aw_ready"), sem("ah_ready")
        pg_loaded = [sem(f"pg_loaded{j}") for j in range(PAGES)]
        st_loaded = [sem(f"st_loaded{s}") for s in range(NS)]
        page_done = sem("page_done")
        x_in, c_in, p_in, ws_in, cs_in, pt_in, sk_in, ple_in = (sem(n) for n in (
            "x_in", "c_in", "p_in", "ws_in", "cs_in", "pt_in", "sk_in", "ple_in"))
        out_dma = sem("out_dma")
        state_saved = sem("state_saved")
        sq_ready, rt_ready, ht_ready = sem("sq_ready"), sem("rt_ready"), sem("ht_ready")
        bsq_ready, brt_ready, bn_ready = sem("bsq_ready"), sem("brt_ready"), sem("bn_ready")
        dch, ach, pch = sem("dve_chain"), sem("act_chain"), sem("pool_chain")
        sm_u, sm_e = sem("small_u"), sem("small_e")
        gates_ready = sem("token_gates_ready")
        conv_acc, conv_out = sem("conv_acc"), sem("conv_out")
        lfl_ready = sem("lfl_ready")
        lf_in, qm_zero, qm_ready, own_ready = sem("lf_in"), sem("qm_zero"), sem("qm_ready"), sem("own_ready")
        lfs_ready, score_ready, on_ready = sem("lfs_ready"), sem("score_ready"), sem("on_ready")
        neg_ready, prob_raw, prob_ready = sem("neg_ready"), sem("prob_raw"), sem("prob_ready")
        dec_ready, a_ready = sem("dec_ready"), sem("a_ready")
        t_init = sem("t_init")
        kd_ready, vb_ready, gb_ready, qe_ready = sem("kd_ready"), sem("vb_ready"), sem("gb_ready"), sem("qe_ready")
        vn_ready, s2_ready = sem("vn_ready"), sem("s2_ready")
        kqm_ready, del_ready, dm_ready, dmn_ready, st_ready = (sem(n) for n in (
            "kqm_ready", "del_ready", "dm_ready", "dmn_ready", "st_ready"))
        bcx_ready, og_ready, lfd_ready = sem("bcx_ready"), sem("og_ready"), sem("lfd_ready")
        mx_ready, dg_ready, sp_in, sp_exp, sp_ready, of_ready = (sem(n) for n in (
            "mx_ready", "dg_ready", "sp_in", "sp_exp", "sp_ready", "of_ready"))
        mt_ready, x1_ready, x2_ready = sem("mt_ready"), sem("x1_ready"), sem("x2_ready")
        re_in, re_exp, res_ready = sem("re_in"), sem("re_exp"), sem("res_ready")
        oha_ready, ohb_ready = sem("oha_ready"), sem("ohb_ready")
        gelu_ready, a_blk = sem("gelu_ready"), sem("a_blk")
        y_added = sem("y_added")
        pw_done, pw_used, fin_ready = sem("pw_done"), sem("pw_used"), sem("fin_ready")
        lf_saved = sem("lf_saved")
        conv_copied, cs_saved, kv_saved, sp_saved, qs_copied = (sem(n) for n in (
            "conv_copied", "cs_saved", "kv_saved", "sp_saved", "qs_copied"))
        eg_ready, convs_ready = sem("eg_ready"), sem("convs_ready")
        mg_step, oh_step = sem("merge_step"), sem("onehot_step")

        def wait_done(eng, n):
            s = stream_of(n)
            if s is None:
                eng.wait_ge(pe_job, PJ[n])
            else:
                eng.wait_ge(quarter_done, 4 * (split_index(s) + 1))

        def wait_evac(eng, n):
            eng.wait_ge(evac[n % 4], n // 4 + 1)

        def claim(pe, n):
            if n >= 4:
                wait_evac(pe, n - 4)

        def bank(n):
            return ps[:, n % 4, :]

        class Chain:

            def __init__(self, eng, s):
                self.eng, self.s, self.n = eng, s, 0

            def __call__(self, ins):
                self.n += 1
                ins.then_inc(self.s, 1)
                self.eng.wait_ge(self.s, self.n)

        def wait_high_part(eng, it, m, s, q):
            eng.wait_ge(hi_ready, it * (4 * m) + (4 * split_index(s) + q + 1))

        def wait_low_part(eng, it, m, s, q):
            eng.wait_ge(lo_ready, it * (4 * m) + (4 * split_index(s) + q + 1))

        def wait_quarter(eng, it, m, s, q):
            eng.wait_ge(quarter_done, it * (4 * m) + (4 * split_index(s) + q + 1))

        def wait_slot(eng, it, m, s, back=0):
            if S0["up"] <= s < S0["out"]:
                eng.wait_ge(pe_job, it * m + (PJ[JOB["up"] + s - S0["up"]] - back))
            else:
                eng.wait_ge(lo_ready, it * (4 * m) + 4 * (split_index(s) + 1 - back))

        def high_part(act, it, m, s, q):
            if q == 0:
                act.wait_ge(w_loaded[s % 4], it * (4 * m) + 16 * (s // 4 + 1))
            c = split_index(s)
            if c:
                act.wait_ge(quarter_done, it * (4 * m) + (4 * (c - 1) + q + 1))
            nc.scalar.activation(ckh(q), at(WR + (s % 4) * D_MODEL + q * QW, QW), ACT.Copy).then_inc(hi_ready, 1)

        def low_part(dve, it, m, s, q):
            wait_high_part(dve, it, m, s, q)
            nc.vector.tensor_tensor(ckl(q), at(WR + (s % 4) * D_MODEL + q * QW, QW), as_f32(ckh(q)),
                                    ALU.subtract).then_inc(lo_ready, 1)

        def dense_steps(eng, s0, its, part, finish):
            for q in range(RING):
                part(eng, 0, 4, s0, q)

            def step(it, j, last=False):
                for q in range(RING):
                    if not last:
                        part(eng, it, 4, s0 + j + 1, q)
                finish(it, j)
            with eng.Fori(0, its - 1) as it:
                for j in range(RING):
                    step(it, j)
            for j in range(RING):
                step(its - 1, j, j == RING - 1)

        def load_pages(eng, part, s, odd, some=range(PAGES)):
            for j in some[odd::2]:
                if part == 0 and isinstance(s, int) and s == 0 and j < 4:
                    eng.wait_ge(st_ready, 64)
                else:
                    eng.wait_ge(page_done, s * 8 + (64 * part + j - 3))
                r = eng.value_load(ptb[0:1, bass.ds(s * PAGES + j, 1)])
                src = (kx, vx)[part]
                eng.dma_start(page(j), src[bass.ds(r, 1)].rearrange("o p c -> (o p) c")).then_inc(pg_loaded[j], 16)

        block = ctx.enter_context(nc.Block())

        @block.sync
        def _(sp):
            sp.dma_start(at(XT, KT * T), xT).then_inc(x_in, 16)
            sp.dma_start(at(CST, C_END), consts).then_inc(c_in, 16)
            sp.dma_start(at(PAR, G_END), params).then_inc(p_in, 16)
            sp.dma_start(at(SC + 4224, 384), wsmall).then_inc(ws_in, 16)
            sp.dma_start(ptb[:, :], ptab).then_inc(pt_in, 16)

            def load_w(it, m, s, src, n):
                if isinstance(it, int):
                    sp.dma_start(wr(s % 4), src[n]).then_inc(w_loaded[s % 4], 16)
                else:
                    sp.dma_start(wr(s % 4), src[bass.ds(it * m + n, 1)].rearrange("o p c -> (o p) c")).then_inc(w_loaded[s % 4], 16)

            def peel(s0, n0, late=None):
                for j in range(RING):
                    if s0:
                        wait_slot(sp, 0, 0, s0 + j - RING)
                    if late is not None and j >= 2:
                        sp.wait_ge(pe_job, late)
                    load_w(0, 0, s0 + j, wd, n0 + j)

            def loop(s0, n0, its):
                peel(s0, n0)
                with sp.Fori(1, its) as it:
                    for j in range(RING):
                        wait_slot(sp, it, 4, s0 + j, RING)
                        load_w(it, 4, s0 + j, wd, n0 + j)

            loop(S0["A"], 0, 14)

            sp.wait_ge(pt_in, 16)
            sp.wait_ge(st_ready, 64)
            for c in range(NS * PAGES):
                r = sp.value_load(ptb[0:1, c:c + 1])
                sp.dma_start(arena[c:c + 1, LFR:LFR + NH * P], lx[bass.ds(r, 1)]).then_inc(lf_in, 16)
            sp.wait_ge(state_saved, 16 * NS)

            def load_gate(it, k):
                g = S0["gates"] + k
                wait_slot(sp, it, 4, g, RING)
                load_w(it, 4, g, wd, g)

            def beside(part, it, j):
                load_pages(sp, part, it * 2 + j // 2, 0, range(4 * (j % 2), 4 * (j % 2) + 4))

            load_gate(0, 0)
            load_gate(0, 1)
            for j in range(4):
                load_gate(0, j + 2)
                beside(0, 0, j)
            with sp.Fori(1, 4) as it:
                for j in range(4):
                    load_gate(it, j + 2)
                    beside(0, it, j)
            with sp.Fori(0, 3) as it:
                for j in range(4):
                    load_gate(it, 16 + j + 2)
                    beside(1, it, j)
            for j in range(4):
                if j < 2:
                    load_gate(0, 28 + j + 2)
                beside(1, 3, j)

            loop(S0["up"], 88, 4)
            loop(S0["out"], 104, 4)
            sp.wait_ge(mt_ready, 1)
            sp.dma_start(at(SK, 16 * P), subk).then_inc(sk_in, 16)
            loop(S0["wq"], 120, 4)

            for half in range(2):
                s0, u0, v0 = S0[f"peer{half}"], 136 + 64 * half, 64 * half
                peel(s0, u0, PJ[JOB[f"wb{half}"] + 32])

                def group(it):
                    for kind in range(2):
                        for j in range(RING):
                            s = s0 + 4 + 4 * kind + j
                            wait_slot(sp, it, 8, s, RING)
                            load_w(it, 4, s, (wd, vd)[kind], ((u0 + 4) + j, v0 + j)[kind])

                with sp.Fori(0, 15) as it:
                    group(it)
                for j in range(RING):
                    wait_slot(sp, 0, 0, s0 + 120 + j)
                    load_w(0, 0, s0 + 124 + j, vd, v0 + 60 + j)
            loop(S0["ple"], 264, 4)
            for q in range(4):
                sp.wait_ge(fin_ready, 4 * q + 4)
                sp.dma_start(o_x[:, 4 * q * T:(4 * q + 4) * T], at(XT + 4 * q * T, 4 * T)).then_inc(out_dma, 16)
            sp.wait_ge(out_dma, 16 * 4)
            sp.wait_ge(lf_saved, 16)
            sp.wait_ge(cs_saved, 16)
            sp.wait_ge(kv_saved, 32)
            sp.wait_ge(sp_saved, 16)
            sp.wait_ge(state_saved, 16 * NS)

        @block.tensor
        def _(pe):
            mm = nc.tensor.matmul

            def norm(r):
                n = JOB[f"norm{r}"]
                claim(pe, n)
                if r == 0:
                    pe.wait_ge(c_in, 16)
                pe.wait_ge(sq_ready, r + 1)
                for k in range(KT):
                    last = mm(bank(n)[:, 0:T], ones, blk(SQ, k), start=(k == 0), stop=(k == KT - 1))
                last.then_inc(pe_job, 1)

            def products(out, wh, wl, xh, xl, start, stop):
                mm(out, wh, xh, start=start, stop=False)
                mm(out, wh, xl, start=False, stop=False)
                return mm(out, wl, xh, start=False, stop=stop)

            def split_unit(it, m, s, n, mj=4):
                if n >= 4 or not isinstance(it, int):
                    pe.wait_ge(evac[n % 4], it * (mj // 4) + n // 4)
                for q in range(RING):
                    wait_low_part(pe, it, m, s, q)
                    for kk in range(QK):
                        k = q * QK + kk
                        last = products(bank(n)[:, 0:T], ckh(q)[:, kk * P:(kk + 1) * P], ckl(q)[:, kk * P:(kk + 1) * P],
                                        hh3[:, k, :], hl3[:, k, :], k == 0, k == KT - 1)
                    last.then_inc(quarter_done, 1)

            def dense(name, its):
                with pe.Fori(0, its) as it:
                    for j in range(RING):
                        split_unit(it, 4, S0[name] + j, JOB[name] + j)

            norm(0)
            pe.wait_ge(ht_ready, 16)
            for j in range(RING):
                split_unit(0, 4, S0["A"] + j, JOB["A"] + j)
            with pe.Fori(1, 14) as it:
                for j in range(RING):
                    split_unit(it, 4, S0["A"] + j, JOB["A"] + j)

            n = JOB["small"]
            claim(pe, n)
            pe.wait_ge(ws_lo, 1)
            for c, m in ((0, P), (1, P), (2, NS)):
                for k in range(KT):
                    out, tk = bank(n)[0:m, c * 24:c * 24 + 24], slice(c * P, c * P + m)
                    mm(out, hh3[:, k, tk], sp_(WSH + k * 24, 24), start=(k == 0), stop=False)
                    mm(out, hh3[:, k, tk], sp_(WSL + k * 24, 24), start=False, stop=False)
                    last = mm(out, hl3[:, k, tk], sp_(WSH + k * 24, 24), start=False, stop=(k == KT - 1))
            last.then_inc(pe_job, 1)

            def block_norm(name, count, c0):
                for b in range(count):
                    n = JOB[name] + b
                    claim(pe, n)
                    pe.wait_ge(bsq_ready, c0 + b + 1)
                    mm(bank(n)[:, 0:T], ones, at(SC + (b % 2) * T, T), start=True, stop=True).then_inc(pe_job, 1)

            block_norm("fqk", 16, 0)
            block_norm("gqk", 16, 16)

            n = JOB["cum"]
            claim(pe, n)
            pe.wait_ge(gates_ready, 1)
            g2 = lgb[:, 0:2, 8:16]
            for q, lhs in enumerate((upi, low, ones)):
                last = mm(bank(n)[:, 16 * q:16 * q + 16].rearrange("p (c h) -> p c h", c=2), lhs, g2, start=True, stop=True)
            last.then_inc(pe_job, 1)

            n = JOB["bc"]
            claim(pe, n)
            pe.wait_ge(bcx_ready, 1)
            mm(bank(n)[:, 0:128], cst(C_ONE, P, NS), at(SC + 1200, 128, NS), start=True, stop=True)
            mm(bank(n)[:, 128:192], ones, at(SC + 1328, 64), start=True, stop=True)
            mm(bank(n)[:, 192:256], ones, at(SC + 1392, 64), start=True, stop=True).then_inc(pe_job, 1)

            for q in range(4):
                n = JOB["fvt"] + q
                claim(pe, n)
                for i in range(4):
                    last = nc.tensor.transpose(bank(n)[:, i * P:(i + 1) * P],
                                               pt3[:, 16 + 2 * q + i // 2, (i % 2) * P:(i % 2 + 1) * P], ident)
                last.then_inc(pe_job, 1)
            wait_evac(pe, JOB["fvt"] + 3)
            pe.wait_ge(bn_ready, 32)
            for h in range(NH):
                n = JOB["fs"] + h
                claim(pe, n)
                pe.wait_ge(lfl_ready, 3 * h + 3)
                lfl = lambda i: at(OT + (h % 2) * 384 + i * P, P)
                q, k = pt3[:, h, :], pt3[:, 8 + h, :]
                b = bank(n)
                mm(b[:, 0:P], q[:, 0:P], k[:, 0:P], start=True, stop=False)
                mm(b[:, 0:P], upi, lfl(0), start=False, stop=True)
                mm(b[:, P:2 * P], q[:, P:2 * P], k[:, 0:P], start=True, stop=False)
                mm(b[:, P:2 * P], ones, lfl(0), start=False, stop=False)
                mm(b[:, P:2 * P], upi, lfl(2), start=False, stop=True)
                mm(b[:, 2 * P:3 * P], q[:, P:2 * P], k[:, P:2 * P], start=True, stop=False)
                mm(b[:, 2 * P:3 * P], upi, lfl(1), start=False, stop=True).then_inc(pe_job, 1)
            for h in range(NH):
                n = JOB["fpt"] + h
                claim(pe, n)
                pe.wait_ge(prob_ready, 2 * h + 2)
                for i in range(3):
                    last = nc.tensor.transpose(bank(n)[:, i * P:(i + 1) * P], at(SC + h * 384 + i * P, P), ident)
                last.then_inc(pe_job, 1)
            vn = lambda h, c: at(OT + (8 + h) * T + c * P, P)
            for g in range(4):
                n = JOB["fo"] + g
                claim(pe, n)
                wait_evac(pe, JOB["fpt"] + 2 * g + 1)
                for i in range(2):
                    h = 2 * g + i
                    b = bank(n)[:, i * 256:i * 256 + 256]
                    pt_ = lambda c: at(SC + 3072 + h * 384 + c * P, P)
                    mm(b[:, 0:P], vn(h, 0), pt_(0), start=True, stop=True)
                    mm(b[:, P:2 * P], vn(h, 0), pt_(1), start=True, stop=False)
                    last = mm(b[:, P:2 * P], vn(h, 1), pt_(2), start=False, stop=True)
                last.then_inc(pe_job, 1)

            B1, B2, B3 = SC, SC + 2048, SC + 4096
            B4, B5, B6 = PT, PT + 2048, PT + 4096
            pair = lambda base, h, c: at(base + (2 * h + c) * P, P)
            wait_evac(pe, JOB["fo"] + 3)
            for h in range(NH):
                n = JOB["gdk"] + 2 * h
                claim(pe, n)
                pe.wait_ge(lfl_ready, 24 + 2 * h + 2)
                for c in range(2):
                    gl = at(OT + 8 * T + (h % 2) * 256 + c * P, P)
                    mm(bank(n)[:, c * P:(c + 1) * P], upi, gl, start=True, stop=True)
                    last = mm(bank(n)[:, (2 + c) * P:(3 + c) * P], gl, upi, start=True, stop=True)
                last.then_inc(pe_job, 1)
                n += 1
                claim(pe, n)
                for c in range(2):
                    k = pt3[:, 32 + h, c * P:(c + 1) * P]
                    q = pt3[:, 24 + h, c * P:(c + 1) * P]
                    mm(bank(n)[:, c * P:(c + 1) * P], k, k, start=True, stop=True)
                    last = mm(bank(n)[:, (2 + c) * P:(3 + c) * P], k, q, start=True, stop=True)
                last.then_inc(pe_job, 1)
            for g in range(4):
                n = JOB["gat"] + g
                claim(pe, n)
                pe.wait_ge(a_ready, 2 * g + 2)
                for i in range(4):
                    last = nc.tensor.transpose(bank(n)[:, i * P:(i + 1) * P], at(B1 + (4 * g + i) * P, P), ident)
                last.then_inc(pe_job, 1)
            inv = lambda lv, kind, g: JOB["inv"] + 12 * lv + (g if kind == 0 else 4 + 2 * g + kind - 1)
            pe.wait_ge(t_init, 2)
            for lv in range(LEVELS):
                for g in range(4):
                    n = inv(lv, 0, g)
                    claim(pe, n)
                    if lv == 0:
                        wait_evac(pe, JOB["gat"] + g)
                    else:
                        wait_evac(pe, inv(lv - 1, 1, g))
                    for i in range(4):
                        o = (4 * g + i) * P
                        last = mm(bank(n)[:, i * P:(i + 1) * P], at(B2 + o, P), at(B3 + o, P), start=True, stop=True)
                    last.then_inc(pe_job, 1)
                for g in range(4):
                    for kind in (1, 2):
                        n = inv(lv, kind, g)
                        claim(pe, n)
                        wait_evac(pe, inv(lv, 0, g))
                        if lv:
                            wait_evac(pe, inv(lv - 1, 2, g))
                        for i in range(4):
                            o = (4 * g + i) * P
                            lhs, rhs = (B4, B1) if kind == 1 else (B1, B4)
                            last = mm(bank(n)[:, i * P:(i + 1) * P], at(lhs + o, P), at(rhs + o, P), start=True, stop=True)
                        last.then_inc(pe_job, 1)
            for name, blk0 in (("gkt", 32), ("gvt", 40)):
                for g in range(4):
                    n = JOB[name] + g
                    claim(pe, n)
                    for i in range(4):
                        last = nc.tensor.transpose(bank(n)[:, i * P:(i + 1) * P],
                                                   pt3[:, blk0 + 2 * g + i // 2, (i % 2) * P:(i % 2 + 1) * P], ident)
                    last.then_inc(pe_job, 1)
            for g in range(4):
                n = JOB["gu"] + g
                claim(pe, n)
                wait_evac(pe, JOB["gvt"] + g)
                wait_evac(pe, inv(LEVELS - 1, 2, g))
                for i in range(4):
                    o = (4 * g + i) * P
                    last = mm(bank(n)[:, i * P:(i + 1) * P], at(B4 + o, P), at(B1 + o, P), start=True, stop=True)
                last.then_inc(pe_job, 1)
            for g in range(2):
                n = JOB["gw"] + g
                claim(pe, n)
                wait_evac(pe, JOB["gkt"] + 2 * g + 1)
                for i in range(4):
                    h = 4 * g + i
                    last = mm(bank(n)[:, i * P:(i + 1) * P], pair(B2, h, 1), pair(B4, h, 1), start=True, stop=True)
                last.then_inc(pe_job, 1)
            for g in range(2):
                n = JOB["gs1"] + g
                claim(pe, n)
                wait_evac(pe, JOB["gu"] + 2 * g + 1)
                for i in range(4):
                    h = 4 * g + i
                    last = mm(bank(n)[:, i * P:(i + 1) * P], pair(B3, h, 0), pair(B6, h, 0), start=True, stop=True)
                last.then_inc(pe_job, 1)
            for g in range(2):
                n = JOB["gq"] + g
                claim(pe, n)
                pe.wait_ge(gb_ready, 8)
                for i in range(4):
                    h = 4 * g + i
                    last = mm(bank(n)[:, i * P:(i + 1) * P], at(B2 + h * P, P), upi, start=True, stop=True)
                last.then_inc(pe_job, 1)
            for g in range(2):
                n = JOB["gws"] + g
                claim(pe, n)
                wait_evac(pe, JOB["gw"] + g)
                wait_evac(pe, JOB["gs1"] + g)
                for i in range(4):
                    h = 4 * g + i
                    last = mm(bank(n)[:, i * P:(i + 1) * P], at(B1 + h * P, P), at(B1 + 1024 + h * P, P), start=True, stop=True)
                last.then_inc(pe_job, 1)
            for g in range(4):
                n = JOB["go"] + g
                claim(pe, n)
                wait_evac(pe, JOB["gws"] + g // 2)
                pe.wait_ge(qe_ready, 2)
                for i in range(2):
                    h = 2 * g + i
                    b = bank(n)[:, i * 256:i * 256 + 256]
                    mm(b[:, 0:P], pair(B6, h, 0), pair(B5, h, 0), start=True, stop=True)
                    mm(b[:, P:2 * P], at(B1 + 1024 + h * P, P), pt3[:, 24 + h, P:2 * P], start=True, stop=False)
                    last = mm(b[:, P:2 * P], pair(B6, h, 1), pair(B5, h, 1), start=False, stop=True)
                last.then_inc(pe_job, 1)
            for g in range(2):
                n = JOB["gs2"] + g
                claim(pe, n)
                for i in range(4):
                    h = 4 * g + i
                    last = mm(bank(n)[:, i * P:(i + 1) * P], pair(B3, h, 1), pair(B6, h, 1), start=True, stop=True)
                last.then_inc(pe_job, 1)

            n = JOB["sg1"]
            claim(pe, n)
            for s in range(NS):
                pe.wait_ge(st_loaded[s], 16)
                for h in range(NH):
                    c = (s * NH + h) * 2
                    last = mm(bank(n)[:, c:c + 2], state_of(s)[:, h * P:(h + 1) * P],
                              pt3[:, 24 + h:33 + h:8, SEQ + s], start=True, stop=True)
            last.then_inc(pe_job, 1)
            for name, srcs in (("sgk", None), ("sgd", DEL)):
                for g in range(2):
                    n = JOB[name] + g
                    claim(pe, n)
                    if srcs is not None:
                        pe.wait_ge(del_ready, 1)
                    for i in range(4):
                        h = 4 * g + i
                        src = pt3[:, 32 + h, SEQ:T] if srcs is None else at(DEL + h * NS, NS)
                        last = nc.tensor.transpose(bank(n)[0:NS, i * P:(i + 1) * P], src, ident)
                    last.then_inc(pe_job, 1)
            for h in range(NH):
                for g in range(2):
                    n = JOB["sgo"] + 2 * h + g
                    claim(pe, n)
                    pe.wait_ge(dmn_ready, h + 1)
                    mm(bank(n), at(B1 + h * P, P, NS), at(B2 + (h % 2) * 1024 + g * 512, 512, NS),
                       start=True, stop=True).then_inc(pe_job, 1)
            block_norm("gn", 8, 32)

            n = JOB["slf"]
            claim(pe, n)
            pe.wait_ge(lf_in, 16 * NS * PAGES)
            for h in range(NH):
                last = nc.tensor.transpose(bank(n)[:, h * 64:(h + 1) * 64], at(LFR + h * P, P, 64), cst(C_ID, 64, 64))
            last.then_inc(pe_job, 1)
            n = JOB["sown"]
            claim(pe, n)
            pe.wait_ge(own_ready, 1)
            mm(bank(n)[0:64, 0:1], at(PSF, 64), cst(C_ONE, 1), start=True, stop=True).then_inc(pe_job, 1)
            score = ps[0:64, 4:6, :].rearrange("p b (j c) -> p (b j) c", c=P)
            for b in range(2):
                mm(ps[0:64, 4 + b, :].rearrange("p (j c) -> p j c", c=P), at(DEL, 64, NS),
                   cst(C_ONE, P, NS).unsqueeze(1).broadcast_to([NS, 4, P]), start=True, stop=True, skip_group_check=True)

            def k_pages(s, some):
                if s == 0:
                    pe.wait_ge(qm_ready, 1)
                for j in some:
                    pe.wait_ge(pg_loaded[j], s * 16 + 16)
                    for h in range(NH):
                        last = mm(score[:, j, :], at(QM + (s * NH + h) * 64, 64), page(j)[:, h * P:(h + 1) * P],
                                  start=False, stop=False, skip_group_check=True)
                    last.then_inc(page_done, 1)

            def v_pages(s, some):
                b = 4 + 2 * (s % 2)
                if s >= 2:
                    pe.wait_ge(on_ready, s - 1)
                for j in some:
                    pe.wait_ge(pg_loaded[j], s * 16 + 144)
                    for i in range(2):
                        last = mm(ps[0:NS, b + i, :], at(PRT + j * 64 + s * NH, NH), page(j)[:, i * 512:(i + 1) * 512],
                                  start=(j == 0), stop=(j == PAGES - 1))
                    last.then_inc(page_done, 1)

            for it in range(4):
                for j in range(4):
                    split_unit(it, 4, S0["gates"] + 0 + j, JOB["gates0"] + j)
                    k_pages(it * 2 + j // 2, range(4 * (j % 2), 4 * (j % 2) + 4))
            pe.wait_ge(lfs_ready, 1)
            for j in range(PAGES):
                mm(score[:, j, :], at(LF + j * 64, 64), low, start=False, stop=False, skip_group_check=True)
                last = mm(score[:, j, :], at(LFS + j * 64, 64), ones, start=False, stop=(j % 4 == 3), skip_group_check=True)
            last.then_inc(score_ready, 1)
            n = JOB["spt"]
            claim(pe, n)
            pe.wait_ge(sp_ready, 1)
            for j in range(PAGES):
                last = nc.tensor.transpose(bank(n)[:, j * 64:(j + 1) * 64], at(PROB + j * P, P, 64), cst(C_ID, 64, 64))
            last.then_inc(pe_job, 1)
            n = JOB["spb"]
            claim(pe, n)
            pe.wait_ge(dg_ready, 1)
            mm(bank(n)[:, 0:64], cst(C_ONE, P, 64), at(OWN + 64, 64, 64), start=True, stop=True).then_inc(pe_job, 1)
            wait_evac(pe, JOB["spt"])
            for it in range(4):
                for j in range(4):
                    split_unit(it, 4, S0["gates"] + 16 + j, JOB["gates1"] + j)
                    v_pages(it * 2 + j // 2, range(4 * (j % 2), 4 * (j % 2) + 4))

            n = JOB["sot"]
            claim(pe, n)
            pe.wait_ge(on_ready, NS)
            for s in range(NS):
                last = nc.tensor.transpose(bank(n)[:, s * NH:(s + 1) * NH], at(ON + s * P, P, NH), cst(C_ID, NH, NH))
            last.then_inc(pe_job, 1)

            pe.wait_ge(of_ready, 1)
            with pe.Fori(0, 4) as it:
                for j in range(RING):
                    n = JOB["up"] + j
                    pe.wait_ge(w_loaded[j], it * 16 + 16 * (S0["up"] // 4 + 1))
                    pe.wait_ge(evac[n % 4], it + n // 4)
                    for half in range(2):
                        for k in range(NH):
                            last = mm(ps[:, n % 4 + 4 * half, 0:T], wr(j)[:, (half * NH + k) * P:(half * NH + k + 1) * P],
                                      ot3[:, half * NH + k, :], start=(k == 0), stop=(k == NH - 1))
                    last.then_inc(pe_job, 1)
            pe.wait_ge(mt_ready, 1)
            dense("out", 4)
            norm(1)
            pe.wait_ge(ht_ready, 32)
            dense("wq", 4)

            pe.wait_ge(sk_in, 16)
            wait_evac(pe, JOB["wq"] + 15)
            def key_scores(c):
                m = P if c < 2 else NS
                for g in range(4):
                    n = RS_JOB[c] + g
                    claim(pe, n)
                    for i in range(4):
                        hp = 4 * g + i
                        last = mm(bank(n)[0:m, i * P:(i + 1) * P], at(QT + hp * T + c * P, m), at(SK + hp * P, P),
                                  start=True, stop=True)
                    last.then_inc(pe_job, 1)

            def turn_results(c):
                m = P if c < 2 else NS
                n = IDX_JOB[c]
                claim(pe, n)
                pe.wait_ge(res_ready, c + 1)
                for i in range(3):
                    last = nc.tensor.transpose(bank(n)[:, i * P:i * P + m], at(RES + i * P, P, m), cst(C_ID, m, m))
                last.then_inc(pe_job, 1)

            key_scores(0)
            key_scores(1)
            turn_results(0)
            key_scores(2)
            turn_results(1)
            turn_results(2)

            for half in range(2):
                wb, ub = JOB[f"wb{half}"], JOB[f"u{half}"]

                def weights_of(it, j):
                    n = wb + j
                    pe.wait_ge(oha_ready, it * 4 + (33 * half + j + 1))
                    pe.wait_ge(ohb_ready, it * 4 + (33 * half + j + 1))
                    pe.wait_ge(evac[n % 4], it + n // 4)
                    for t in range(8):
                        last = mm(bank(n)[:, t * HALF:(t + 1) * HALF], at(OHB + (j % 2) * 8 * P + t * P, P),
                                  at(OHA + (j % 2) * 8 * HALF + t * HALF, HALF), start=True, stop=True)
                    last.then_inc(pe_job, 1)

                with pe.Fori(0, 8) as it:
                    for j in range(4):
                        weights_of(it, j)
                weights_of(8, 0)

                s0 = S0[f"peer{half}"]

                def scores(it, m, s, n):
                    for j in range(RING):
                        split_unit(it, m, s + j, n + j, m // 2)

                def outputs(it, m, s, g, buf):
                    for dq in range(RING):
                        for q in range(RING):
                            if dq == 0 and q == 0:
                                pe.wait_ge(a_blk, it * (m // 2) + (4 * (16 * half + g) + 4))
                            pe.wait_ge(y_added, it * (2 * m) + (16 * (16 * half + g) + 4 * dq + q + 1))
                            wait_low_part(pe, it, m, s + dq, q)
                            for j in range(EG):
                                a = (buf * EG + j) * T
                                last = products(ps[:, 4 + q, 0:T], ckh(q)[:, j * P:(j + 1) * P],
                                                ckl(q)[:, j * P:(j + 1) * P], sp_(AH + a, T), sp_(AL + a, T),
                                                j == 0, j == EG - 1)
                            last.then_inc(quarter_done, 1)

                scores(0, 0, s0, ub)
                with pe.Fori(0, 7) as i2:
                    for b in range(2):
                        scores(i2, 16, s0 + 4 + 8 * b, ub + 4 + 4 * b)
                        outputs(i2, 16, s0 + 8 + 8 * b, b, b)
                scores(0, 0, s0 + 116, ub + 60)
                outputs(0, 0, s0 + 120, 14, 0)
                outputs(0, 0, s0 + 124, 15, 1)

            norm(2)
            pe.wait_ge(ht_ready, 48)
            pe.wait_ge(ple_in, 32)
            for b in range(16):
                if b >= 4:
                    pe.wait_ge(fin_ready, b - 3)
                for k in range(PLE_KT):
                    last = mm(ps[:, 4 + b % 4, 0:T], at(WPL + k * D_MODEL + b * P, P), at(PTI + k * T, T),
                              start=(k == 0), stop=(k == PLE_KT - 1))
                last.then_inc(pw_done, 1)
                split_unit(b // 4, 4, S0["ple"] + b % 4, JOB["ple"] + b % 4)

        @block.scalar
        def _(act):
            A = nc.scalar.activation
            self_ = Chain(act, ach)

            def norm(r):
                if r == 0:
                    act.wait_ge(x_in, 16)
                else:
                    act.wait_ge((x1_ready, x2_ready)[r - 1], 1)
                A(at(SQ, KT * T), at(XT, KT * T), ACT.Square).then_inc(sq_ready, 1)
                n = JOB[f"norm{r}"]
                wait_done(act, n)
                if r == 0:
                    act.wait_ge(c_in, 16)
                A(at(SC + 4608, T), bank(n)[:, 0:T], ACT.Sqrt, bias=eps, scale=1.0 / D_MODEL).then_inc(evac[n % 4], 1)
                for k in range(KT):
                    act.wait_ge(hraw_ready, 16 * r + k + 1)
                    A(hh3[:, k, :], blk(HRAW, k), ACT.Copy).then_inc(hh_ready, 1)

            def each_block(name, its, func, base, s0=None, b0=0):
                s0 = S0[name] if s0 is None else s0

                def read_out(it, j):
                    n = JOB[name] + j
                    wait_quarter(act, it, 4, s0 + j, RING - 1)
                    dst = base + (b0 + j) * T
                    dst = at(dst + it * 4 * T, T) if isinstance(it, int) else arena[:, bass.ds(it * (4 * T) + dst, T)]
                    A(dst, bank(n)[:, 0:T], func).then_inc(evac[n % 4], 1)
                dense_steps(act, s0, its, high_part, read_out)

            norm(0)
            act.wait_ge(ws_in, 16)
            A(sp_(WSH, 384), at(SC + 4224, 384), ACT.Copy).then_inc(ws_hi, 1)
            each_block("A", 14, ACT.Copy, PT)

            act.wait_ge(p_in, 16)
            A(at(ALE, 8), par(G_ALOG, 8), ACT.Exp).then_inc(sm_e, 1)
            act.wait_ge(sm_u, 1)
            A(at(SMY, 72), at(SMU, 72), ACT.Exp, scale=-1.0).then_inc(sm_e, 1)

            def block_norm(name, count, c0, src, scale_bias):
                def square(b):
                    if b >= 2:
                        wait_done(act, JOB[name] + b - 2)
                    A(at(SC + (b % 2) * T, T), src(b), ACT.Square).then_inc(bsq_ready, 1)
                for b in range(2):
                    square(b)
                for b in range(count):
                    n = JOB[name] + b
                    wait_done(act, n)
                    if c0 + b >= 2:
                        act.wait_ge(bn_ready, c0 + b - 1)
                    sc, bi = scale_bias(b)
                    A(at(SC + (2 + b % 2) * T, T), bank(n)[:, 0:T], ACT.Sqrt, bias=bi, scale=sc).then_inc(evac[n % 4], 1)
                    if b + 2 < count:
                        square(b + 2)

            wait_done(act, JOB["small"])
            block_norm("fqk", 16, 0, lambda b: blk(PT, b), lambda b: (1.0, eps128) if b < 8 else (1.0 / P, eps))
            for b in range(24):
                act.wait_ge(conv_acc, b + 1)
                if b == 0:
                    act.wait_ge(conv_copied, 1)
                A(pt3[:, 24 + b, 0:SEQ], at(CACC + (b % 2) * SEQ, SEQ), ACT.Silu).then_inc(conv_out, 1)
            act.wait_ge(convs_ready, 1)
            A(pt3[:, 24:48, SEQ:T], at(CSAMP, 192).rearrange("p (b s) -> p b s", s=NS), ACT.Silu).then_inc(conv_out, 1)
            A(at(PT + 48 * T, 8 * T), at(PT + 48 * T, 8 * T), ACT.Silu).then_inc(conv_out, 1)
            act.wait_ge(conv_out, 26)
            block_norm("gqk", 16, 16, lambda b: blk(PT, 24 + b), lambda b: (float(P), eps128) if b < 8 else (1.0, eps))

            n = JOB["cum"]
            wait_done(act, n)
            A(at(EXS, 48), bank(n)[:, 0:48], ACT.Exp).then_inc(evac[n % 4], 1)

            wait_evac(act, JOB["bc"])
            A(at(BCS, 64), at(BCS, 64), ACT.Exp).then_inc(eg_ready, 1)

            for h in range(NH):
                act.wait_ge(neg_ready, h + 1)
                s = at(SC + h * 384, 384)
                A(s[:, 0:P], s[:, 0:P], ACT.Exp, bias=at(NEGM + 2 * h, 1), accum_out=at(SUMS + 2 * h, 1)).then_inc(prob_raw, 1)
                A(s[:, P:384], s[:, P:384], ACT.Exp, bias=at(NEGM + 2 * h + 1, 1),
                  accum_out=at(SUMS + 2 * h + 1, 1)).then_inc(prob_raw, 1)
            for h in range(NH):
                n = JOB["fpt"] + h
                wait_done(act, n)
                A(at(SC + 3072 + h * 384, 384), bank(n)[:, 0:384], ACT.Copy).then_inc(evac[n % 4], 1)
            for g in range(4):
                n = JOB["fo"] + g
                wait_done(act, n)
                A(ot3[:, 2 * g:2 * g + 2, 0:SEQ], bank(n).rearrange("p (h t) -> p h t", h=2), ACT.Copy).then_inc(evac[n % 4], 1)

            act.wait_ge(kv_saved, 32)
            act.wait_ge(qs_copied, 3)
            B1, B2, B3 = SC, SC + 2048, SC + 4096
            B4, B5, B6 = PT, PT + 2048, PT + 4096
            for h in range(NH):
                n = JOB["gdk"] + 2 * h
                wait_done(act, n)
                if h >= 2:
                    wait_evac(act, n - 3)
                A(at(B6 + (h % 2) * 512, 512), bank(n), ACT.Exp).then_inc(evac[n % 4], 1)
            for g in range(4):
                n = JOB["gat"] + g
                wait_done(act, n)
                A(at(B2 + g * 512, 512), bank(n), ACT.Copy).then_inc(evac[n % 4], 1)
            for name, dst in (("gu", B6), ("gw", B1), ("gs1", B1 + 1024)):
                for g in range(4 if name == "gu" else 2):
                    n = JOB[name] + g
                    wait_done(act, n)
                    if name == "gw" and g == 0:
                        wait_done(act, JOB["gu"] + 3)
                    A(at(dst + g * 512, 512), bank(n), ACT.Copy).then_inc(evac[n % 4], 1)
            for g in range(2):
                n = JOB["gq"] + g
                wait_done(act, n)
                A(at(B2 + 1024 + g * 512, 512), bank(n), ACT.Exp).then_inc(evac[n % 4], 1)
            for g in range(4):
                n = JOB["go"] + g
                wait_done(act, n)
                A(ot3[:, NH + 2 * g:NH + 2 * g + 2, 0:SEQ], bank(n).rearrange("p (h t) -> p h t", h=2), ACT.Copy).then_inc(evac[n % 4], 1)
            for name, dst in (("sgk", B1), ("sgd", B3)):
                for g in range(2):
                    n = JOB[name] + g
                    wait_done(act, n)
                    A(at(dst + g * 512, 512, NS), bank(n)[0:NS, :], ACT.Copy).then_inc(evac[n % 4], 1)
            act.wait_ge(st_ready, 64)
            for s in range(NS):
                act.dma_start(o_ss[s], state_of(s)).then_inc(state_saved, 16)
            act.wait_ge(og_ready, 1)
            act.wait_ge(sp_saved, 16)
            block_norm("gn", 8, 32, lambda b: blk(OT, NH + b), lambda b: (1.0 / P, eps))

            each_block("gates0", 4, ACT.Sigmoid, GT, S0["gates"])
            act.wait_ge(sp_in, 1)
            own = lambda c, w=1: at(OWN + c, w, 64)
            for b in range(2):
                A(at(PROB + b * 512, 512, 64), ps[0:64, 4 + b, :], ACT.Exp, bias=own(3), accum_out=own(4 + b)).then_inc(sp_exp, 1)
            A(own(6), own(0), ACT.Exp, bias=own(3)).then_inc(sp_exp, 1)
            each_block("gates1", 4, ACT.Sigmoid, GT, S0["gates"] + 16, 16)

            with act.Fori(0, 4) as it:
                for j in range(RING):
                    act.wait_ge(merged, it * 4 + (j + 1))
                    A(split[:, bass.ds(it * (4 * T) + (HH + j * T), T)], at(TMU + (j % 2) * 2 * T, T), ACT.Copy).then_inc(mh_ready, 1)

            def high_only(name):
                dense_steps(act, S0[name], 4, high_part, lambda it, j: None)
            high_only("out")

            norm(1)
            each_block("wq", 4, ACT.Copy, QT)
            for c in range(3):
                m = P if c < 2 else NS
                for g in range(4):
                    n = RS_JOB[c] + g
                    wait_done(act, n)
                    if c and g == 0:
                        act.wait_ge(res_ready, c)
                    A(at(RS + 512 * g, 512, m), bank(n)[0:m, :], ACT.Copy).then_inc(evac[n % 4], 1)
                act.wait_ge(re_in, c + 1)
                A(at(RES + 2 * P, P, m), at(RES + 2 * P, P, m), ACT.Exp).then_inc(re_exp, 1)

            wh3 = at(WH, HALF * T).rearrange("p (a t) -> p t a", t=T)
            for half in range(2):
                wb, ub = JOB[f"wb{half}"], JOB[f"u{half}"]
                if half:
                    act.wait_ge(a_blk, 64)
                else:
                    wait_evac(act, IDX_JOB[2])

                def weights_of(it, j):
                    n = wb + j
                    act.wait_ge(pe_job, it * 4 + PJ[n])
                    A(wh3[:, bass.ds(it * 32 + 8 * j, 8), :], bank(n).rearrange("p (t a) -> p t a", t=8),
                      ACT.Copy).then_inc(evac[n % 4], 1)

                with act.Fori(0, 8) as it:
                    for j in range(4):
                        weights_of(it, j)
                weights_of(8, 0)

                s0 = S0[f"peer{half}"]

                def gelus(it, m, s, n, g):
                    for j in range(RING):
                        for q in range(RING):
                            high_part(act, it, m, s + j + 1, q)
                        wait_quarter(act, it, m, s + j, RING - 1)
                        if half or g or j >= 2:
                            act.wait_ge(a_blk, it * (m // 2) + (4 * (16 * half + g) + j - 1))
                        A(at(AB + (j % 2) * T, T), bank(n + j)[:, 0:T], ACT.Gelu).then_inc(evac[(n + j) % 4], 1)

                def values(it, m, s, last=False):
                    for j in range(RING):
                        for q in range(RING):
                            if not (last and j == RING - 1):
                                high_part(act, it, m, s + j + 1, q)

                for q in range(RING):
                    high_part(act, 0, 0, s0, q)
                gelus(0, 0, s0, ub, 0)
                with act.Fori(0, 7) as i2:
                    for b in range(2):
                        gelus(i2, 16, s0 + 4 + 8 * b, ub + 4 + 4 * b, b + 1)
                        values(i2, 16, s0 + 8 + 8 * b)
                gelus(0, 0, s0 + 116, ub + 60, 15)
                values(0, 0, s0 + 120)
                values(0, 0, s0 + 124, True)

            norm(2)
            each_block("ple", 4, ACT.Sigmoid, GPL)

        @block.gpsimd
        def _(pool):
            pc = Chain(pool, pch)
            pool.wait_ge(ht_ready, 16)
            pool.dma_start(at(CST_ST, 576), convst).then_inc(cs_in, 16)
            wait_slot(pool, 0, 0, S0["gates"] - 1)
            for s in range(NS):
                pool.dma_start(state_of(s), state[s]).then_inc(st_loaded[s], 16)

            pool.wait_ge(bn_ready, 16)
            pool.dma_start(o_k, at(PT + 8 * T, 8 * T)).then_inc(kv_saved, 16)
            pool.dma_start(o_v, at(PT + 16 * T, 8 * T)).then_inc(kv_saved, 16)
            pool.wait_ge(gates_ready, 1)
            pool.dma_start(o_lf, lgb[:, :, 0:8]).then_inc(lf_saved, 16)
            pool.wait_ge(conv_copied, 1)
            pool.dma_start(o_cs, at(CCOPY, 24 * 27)).then_inc(cs_saved, 16)
            pool.wait_ge(gates_ready, 1)
            wait_evac(pool, JOB["A"] + 55)
            for h in range(NH):
                if h >= 2:
                    wait_done(pool, JOB["fs"] + h - 2)
                for i, (c, m) in enumerate(((0, low), (1, low), (1, ones))):
                    nc.gpsimd.tensor_scalar(at(OT + (h % 2) * 384 + i * P, P), m, lgb[:, c, h:h + 1], 1.0,
                                            ALU.mult, ALU.mult).then_inc(lfl_ready, 1)
            pool.wait_ge(kv_saved, 32)
            pool.wait_ge(qs_copied, 3)
            wait_done(pool, JOB["fo"] + 3)
            for h in range(NH):
                if h >= 2:
                    wait_done(pool, JOB["gdk"] + 2 * h - 4)
                for c in range(2):
                    nc.gpsimd.tensor_scalar(at(OT + 8 * T + (h % 2) * 256 + c * P, P), low, lgb[:, c, 8 + h:9 + h], 1.0,
                                            ALU.mult, ALU.mult).then_inc(lfl_ready, 1)
            B2, B3, B4 = SC + 2048, SC + 4096, PT
            for base in (B3, B4):
                nc.gpsimd.tensor_copy(at(base, 2048).rearrange("p (a b) -> p a b", b=P),
                                      ident.unsqueeze(1).broadcast_to([P, 16, P])).then_inc(t_init, 1)
            wait_done(pool, JOB["gw"] + 1)
            for h in range(NH):
                nc.gpsimd.tensor_scalar(at(B2 + h * P, P), ones, lgb[:, 1, 8 + h:9 + h], 1.0,
                                        ALU.mult, ALU.mult).then_inc(gb_ready, 1)
            pool.wait_ge(s2_ready, 8)
            pool.dma_start(o_sp, at(SC + 1024, 1024)).then_inc(sp_saved, 16)

            pool.wait_ge(bn_ready, 40)
            pool.wait_ge(sp_saved, 16)
            nc.gpsimd.memset(at(QM, 4096), 0.0).then_inc(qm_zero, 1)
            pool.wait_ge(pt_in, 16)
            for part in range(2):
                load_pages(pool, part, 0, 1)
                with pool.Fori(1, 8) as s:
                    load_pages(pool, part, s, 1)

            pool.wait_ge(of_ready, 1)
            pool.dma_start(at(XT, KT * T), xT).then_inc(x_again, 16)

            pool.wait_ge(y_added, 516)
            pool.dma_start(at(WPL, PLE_KT * D_MODEL), wple).then_inc(ple_in, 16)
            pool.dma_start(at(PTI, PLE_KT * T), pT).then_inc(ple_in, 16)

        @block.vector
        def _(dve):
            V = nc.vector
            ch = Chain(dve, dch)

            def norm(r, gain):
                n = JOB[f"norm{r}"]
                wait_evac(dve, n)
                rt = at(SC + 4608, T)
                ch(V.reciprocal(rt, rt))
                if r == 0:
                    dve.wait_ge(p_in, 16)
                for k in range(KT):
                    V.scalar_tensor_tensor(out=blk(HRAW, k), in0=xt3[:, k, :], scalar=par(gain + k), in1=rt,
                                           op0=ALU.mult, op1=ALU.mult).then_inc(hraw_ready, 1)
                for k in range(KT):
                    dve.wait_ge(hh_ready, 16 * r + k + 1)
                    V.tensor_tensor(hl3[:, k, :], blk(HRAW, k), as_f32(hh3[:, k, :]), ALU.subtract).then_inc(ht_ready, 1)

            def low_parts(name, its=4, s0=None):
                dense_steps(dve, S0[name] if s0 is None else s0, its, low_part, lambda it, j: None)

            for b in range(4):
                dve.sem_inc(y_added, 1)
            norm(0, G_MIX)
            dve.wait_ge(ws_hi, 1)
            V.tensor_tensor(sp_(WSL, 384), at(SC + 4224, 384), as_f32(sp_(WSH, 384)), ALU.subtract).then_inc(ws_lo, 1)
            low_parts("A", 14)

            smx = at(SMX, 72).rearrange("p (c k) -> p c k", c=3)
            smu = at(SMU, 72).rearrange("p (c k) -> p c k", c=3)
            dve.wait_ge(ws_in, 16)
            wait_done(dve, JOB["small"])
            ch(V.memset(at(SMX, 72), 0.0))
            bias = par(G_BIAS, 24)
            b3 = bank(JOB["small"])[:, 0:72].rearrange("p (c k) -> p c k", c=3)
            ch(V.tensor_tensor(smx[:, 0:2, :], b3[:, 0:2, :], bias.unsqueeze(1).broadcast_to([P, 2, 24]), ALU.add))
            V.tensor_tensor(smx[0:NS, 2, :], b3[0:NS, 2, :], par(G_BIAS, 24, NS), ALU.add).then_inc(evac[JOB["small"] % 4], 1)
            wait_evac(dve, JOB["small"])
            ch(V.tensor_scalar(smx[:, :, 0:8], smx[:, :, 0:8], -1.0, None, ALU.mult))
            ch(V.scalar_tensor_tensor(out=smu[:, :, 0:16], in0=smx[:, :, 0:16], scalar=-1.0, in1=smx[:, :, 0:16],
                                      op0=ALU.mult, op1=ALU.max))
            V.tensor_copy(smu[:, :, 16:24], smx[:, :, 16:24]).then_inc(sm_u, 1)
            dve.wait_ge(sm_e, 2)
            y, z, z2, pl = at(SMY, 72), at(SMZ, 72), at(SMZ2, 72), at(SMP, 72)
            ch(V.tensor_scalar(z, y, 2.0, None, ALU.add))
            ch(V.reciprocal(z, z))
            ch(V.tensor_tensor(z, z, y, ALU.mult))
            ch(V.tensor_tensor(z2, z, z, ALU.mult))
            ch(V.tensor_scalar(pl, z2, 1.0 / 21, None, ALU.mult))
            for k in (19, 17, 15, 13, 11, 9, 7, 5, 3):
                ch(V.scalar_tensor_tensor(out=pl, in0=pl, scalar=1.0 / k, in1=z2, op0=ALU.add, op1=ALU.mult))
            ch(V.scalar_tensor_tensor(out=pl, in0=pl, scalar=1.0, in1=z, op0=ALU.add, op1=ALU.mult))
            ch(V.tensor_scalar(at(SMX, 72), at(SMX, 72), 0.0, None, ALU.max))
            ch(V.scalar_tensor_tensor(out=pl, in0=pl, scalar=2.0, in1=at(SMX, 72), op0=ALU.mult, op1=ALU.add))
            pl3 = pl.rearrange("p (c k) -> p c k", c=3)
            y3 = y.rearrange("p (c k) -> p c k", c=3)
            V.tensor_scalar(lgb[:, :, 0:8], pl3[:, :, 0:8], -1.0, None, ALU.mult).then_inc(dch, 1)
            ch.n += 1
            ch(V.scalar_tensor_tensor(out=lgb[:, :, 8:16], in0=pl3[:, :, 8:16], scalar=-1.0,
                                      in1=at(ALE, 8).unsqueeze(1).broadcast_to([P, 3, 8]), op0=ALU.mult, op1=ALU.mult))
            ch(V.tensor_scalar(y3[:, :, 16:24], y3[:, :, 16:24], 1.0, None, ALU.add))
            V.reciprocal(lgb[:, :, 16:24], y3[:, :, 16:24]).then_inc(gates_ready, 1)

            def block_norm(name, count, c0, src, factor, extra=None):
                for b in range(count):
                    n = JOB[name] + b
                    wait_evac(dve, n)
                    rt = at(SC + (2 + b % 2) * T, T)
                    ch(V.reciprocal(rt, rt))
                    x = src(b)
                    ins = V.scalar_tensor_tensor(out=x, in0=x, scalar=factor(b), in1=rt, op0=ALU.mult, op1=ALU.mult)
                    if extra is None:
                        ins.then_inc(bn_ready, 1)
                    else:
                        ch(ins)
                        V.tensor_tensor(x, x, extra(b), ALU.mult).then_inc(bn_ready, 1)

            block_norm("fqk", 16, 0, lambda b: blk(PT, b), lambda b: par(G_FQ if b < 8 else G_FK))
            dve.wait_ge(bn_ready, 16)
            for dst, b0 in ((QS, 0), (KS, 8), (VS, 16)):
                V.tensor_copy(at(dst, 64).rearrange("p (h s) -> p h s", s=NS), pt3[:, b0:b0 + 8, SEQ:T]).then_inc(qs_copied, 1)

            dve.wait_ge(cs_in, 16)
            st4 = at(CST_ST, 576).rearrange("p (b s j) -> p b s j", s=NS, j=3)
            cp3 = at(CCOPY, 24 * 27).rearrange("p (b c) -> p b c", c=27)
            cps = cp3[:, :, 3:27].rearrange("p b (s j) -> p b s j", j=3)
            wj = lambda j: par(G_CONV + 24 * j, 24).unsqueeze(2).broadcast_to([P, 24, NS])
            c24 = lambda a: at(a, 192).rearrange("p (b s) -> p b s", s=NS)
            V.tensor_copy(cp3[:, :, 0:3], pt3[:, 24:48, SEQ - 3:SEQ])
            V.tensor_copy(cps[:, :, :, 0:2], st4[:, :, :, 1:3])
            V.tensor_copy(cps[:, :, :, 2], pt3[:, 24:48, SEQ:T]).then_inc(conv_copied, 1)
            ch(V.tensor_tensor(c24(CSAMP), pt3[:, 24:48, SEQ:T], wj(3), ALU.mult))
            for j in range(3):
                ch(V.tensor_tensor(c24(CPROD), st4[:, :, :, j], wj(j), ALU.mult))
                ch(V.tensor_tensor(c24(CSAMP), c24(CSAMP), c24(CPROD), ALU.add))
            dve.sem_inc(convs_ready, 1)
            for b in range(24):
                if b >= 2:
                    dve.wait_ge(conv_out, b - 1)
                a0 = CACC + (b % 2) * SEQ
                x = pt3[:, 24 + b, :]
                w = lambda j: par(G_CONV + 24 * j + b)
                ch(V.tensor_scalar(at(a0, SEQ), x[:, 0:SEQ], w(3), None, ALU.mult))
                for j in (2, 1, 0):
                    d = 3 - j
                    ins = V.scalar_tensor_tensor(out=at(a0 + d, SEQ - d), in0=x[:, 0:SEQ - d], scalar=w(j),
                                                 in1=at(a0 + d, SEQ - d), op0=ALU.mult, op1=ALU.add)
                    if j:
                        ch(ins)
                    else:
                        ins.then_inc(conv_acc, 1)
            block_norm("gqk", 16, 16, lambda b: blk(PT, 24 + b), lambda b: 1.0)
            dve.wait_ge(bn_ready, 32)

            wait_evac(dve, JOB["cum"])
            ch(V.tensor_tensor(at(BEG, 16).rearrange("p (c h) -> p c h", c=2), lgb[:, 0:2, 16:24],
                               at(EXS, 16).rearrange("p (c h) -> p c h", c=2), ALU.mult))
            eyeb = cst(C_ID, NS, NS).unsqueeze(2).broadcast_to([NS, NS, NH])
            x3 = lambda a: at(a, 64, NS).rearrange("p (s h) -> p s h", h=NH)
            V.tensor_tensor(x3(SC + 1200), lgb[0:NS, 2, 8:16].unsqueeze(1).broadcast_to([NS, NS, NH]), eyeb, ALU.mult)
            V.tensor_tensor(x3(SC + 1264), lgb[0:NS, 2, 16:24].unsqueeze(1).broadcast_to([NS, NS, NH]), eyeb, ALU.mult)
            sh = lambda a: at(a, 64).rearrange("p (s h) -> p h s", h=NH)
            hs = lambda a: at(a, 64).rearrange("p (h s) -> p h s", s=NS)
            dve.wait_ge(qs_copied, 3)
            V.tensor_tensor(sh(SC + 1328), hs(QS), hs(KS), ALU.mult)
            V.tensor_tensor(sh(SC + 1392), pt3[:, 24:32, SEQ:T], pt3[:, 32:40, SEQ:T], ALU.mult).then_inc(bcx_ready, 1)
            n = JOB["bc"]
            wait_done(dve, n)
            V.tensor_copy(at(BCS, 256), bank(n)[:, 0:256]).then_inc(evac[n % 4], 1)

            for q in range(4):
                n = JOB["fvt"] + q
                wait_done(dve, n)
                V.tensor_copy(ot3[:, 8 + 2 * q:10 + 2 * q, 0:SEQ], bank(n).rearrange("p (h t) -> p h t", h=2)).then_inc(evac[n % 4], 1)

            dve.wait_ge(cs_saved, 16)
            for h in range(NH):
                n = JOB["fs"] + h
                wait_done(dve, n)
                s = at(SC + h * 384, 384)
                V.tensor_tensor(s, bank(n)[:, 0:384], cst(C_CAUS, 384), ALU.add).then_inc(evac[n % 4], 1)
                wait_evac(dve, n)
                ch(V.tensor_reduce(at(NEGM + 2 * h, 1), s[:, 0:P], AX.X, ALU.max, negate=True))
                V.tensor_reduce(at(NEGM + 2 * h + 1, 1), s[:, P:384], AX.X, ALU.max, negate=True).then_inc(neg_ready, 1)
            for h in range(NH):
                dve.wait_ge(prob_raw, 2 * h + 2)
                ch(V.reciprocal(at(SUMS + 2 * h, 2), at(SUMS + 2 * h, 2)))
                s = at(SC + h * 384, 384)
                V.tensor_scalar(s[:, 0:P], s[:, 0:P], at(SUMS + 2 * h, 1), None, ALU.mult).then_inc(prob_ready, 1)
                V.tensor_scalar(s[:, P:384], s[:, P:384], at(SUMS + 2 * h + 1, 1), None, ALU.mult).then_inc(prob_ready, 1)

            B1, B2, B3 = SC, SC + 2048, SC + 4096
            B4, B5, B6 = PT, PT + 2048, PT + 4096
            dve.wait_ge(kv_saved, 32)
            for h in range(NH):
                nd, nk = JOB["gdk"] + 2 * h, JOB["gdk"] + 2 * h + 1
                wait_evac(dve, nd)
                d0 = B6 + (h % 2) * 512
                two = lambda a: at(a, 256).rearrange("p (c t) -> p c t", c=2)
                V.tensor_tensor(two(d0), two(d0), low.unsqueeze(1).broadcast_to([P, 2, P]), ALU.mult).then_inc(dch, 1)
                ch.n += 1
                ch(V.tensor_tensor(two(d0 + 256), two(d0 + 256), upi.unsqueeze(1).broadcast_to([P, 2, P]), ALU.mult))
                wait_done(dve, nk)
                for c in range(2):
                    ins = V.scalar_tensor_tensor(out=at(B1 + (2 * h + c) * P, P), in0=bank(nk)[:, c * P:(c + 1) * P],
                                                 scalar=lgb[:, c, 16 + h:17 + h], in1=at(d0 + c * P, P),
                                                 op0=ALU.mult, op1=ALU.mult)
                ins.then_inc(a_ready, 1)
                V.tensor_tensor(at(B5 + h * 256, 256), bank(nk)[:, 256:512], at(d0 + 256, 256), ALU.mult).then_inc(evac[nk % 4], 1)
            inv = lambda lv, kind, g: JOB["inv"] + 12 * lv + (g if kind == 0 else 4 + 2 * g + kind - 1)
            dve.wait_ge(t_init, 2)
            for lv in range(LEVELS):
                mask = cst(C_INV + lv * P).unsqueeze(1).broadcast_to([P, 4, P])
                for g in range(4):
                    n = inv(lv, 0, g)
                    wait_done(dve, n)
                    V.tensor_tensor(at(B1 + g * 512, 512).rearrange("p (a b) -> p a b", b=P),
                                    bank(n).rearrange("p (a b) -> p a b", b=P), mask, ALU.mult).then_inc(evac[n % 4], 1)
                for g in range(4):
                    for kind, base in ((1, B3), (2, B4)):
                        n = inv(lv, kind, g)
                        wait_done(dve, n)
                        if lv:
                            wait_evac(dve, inv(lv - 1, kind, g))
                        t = at(base + g * 512, 512)
                        V.tensor_tensor(t, t, bank(n), ALU.subtract).then_inc(evac[n % 4], 1)
            for g in range(4):
                n = JOB["gkt"] + g
                wait_done(dve, n)
                for i in range(4):
                    h, c = 2 * g + i // 2, i % 2
                    o = (4 * g + i) * P
                    V.tensor_scalar(at(B2 + o, P), bank(n)[:, i * P:(i + 1) * P], at(BEG + c * 8 + h, 1), None, ALU.mult)
                    ins = V.tensor_scalar(at(B3 + o, P), bank(n)[:, i * P:(i + 1) * P], at(EXS + 16 + c * 8 + h, 1), None, ALU.mult)
                ins.then_inc(evac[n % 4], 1)
            for g in range(4):
                n = JOB["gvt"] + g
                wait_done(dve, n)
                for i in range(4):
                    h, c = 2 * g + i // 2, i % 2
                    ins = V.tensor_scalar(at(B1 + (4 * g + i) * P, P), bank(n)[:, i * P:(i + 1) * P],
                                          lgb[:, c, 16 + h:17 + h], None, ALU.mult)
                ins.then_inc(evac[n % 4], 1)
            for g in range(2):
                wait_evac(dve, JOB["gq"] + g)
                q = pt3[:, 24 + 4 * g:28 + 4 * g, P:2 * P]
                V.tensor_tensor(q, q, at(B2 + 1024 + g * 512, 512).rearrange("p (h t) -> p h t", t=P), ALU.mult).then_inc(qe_ready, 1)
            u1 = at(B6, 2048).rearrange("p (h c t) -> p h c t", c=2, t=P)[:, :, 1, :]
            for g in range(2):
                n = JOB["gws"] + g
                wait_done(dve, n)
                V.tensor_tensor(u1[:, 4 * g:4 * g + 4, :], u1[:, 4 * g:4 * g + 4, :],
                                bank(n).rearrange("p (h t) -> p h t", t=P), ALU.subtract).then_inc(evac[n % 4], 1)
            for g in range(2):
                n = JOB["gs2"] + g
                wait_done(dve, n)
                for i in range(4):
                    h = 4 * g + i
                    s1 = at(B1 + 1024 + h * P, P)
                    ins = V.scalar_tensor_tensor(out=s1, in0=s1, scalar=at(EXS + 40 + h, 1), in1=bank(n)[:, i * P:(i + 1) * P],
                                                 op0=ALU.mult, op1=ALU.add)
                    if i < 3:
                        ins.then_inc(s2_ready, 1)
                    else:
                        ins.then_inc(evac[n % 4], 1)
                wait_evac(dve, n)
                dve.sem_inc(s2_ready, 1)

            n = JOB["sg1"]
            wait_done(dve, n)
            sg = bank(n)[:, 0:128].rearrange("p (s h q) -> p h s q", h=NH, q=2)
            egs, bes, kqs = sh(BCS), sh(BCS + 64), sh(BCS + 192)
            dve.wait_ge(eg_ready, 1)
            dl, os_ = hs(DEL), ot3[:, 8:16, SEQ:T]
            ch(V.tensor_tensor(dl, sg[:, :, :, 1], egs, ALU.mult))
            V.tensor_tensor(os_, sg[:, :, :, 0], egs, ALU.mult).then_inc(evac[n % 4], 1)
            wait_evac(dve, n)
            ch(V.tensor_tensor(dl, pt3[:, 40:48, SEQ:T], dl, ALU.subtract))
            V.tensor_tensor(dl, dl, bes, ALU.mult).then_inc(del_ready, 1)
            dve.wait_ge(del_ready, 1)
            ch(V.tensor_tensor(hs(PSF), dl, kqs, ALU.mult))
            ch(V.tensor_tensor(os_, os_, hs(PSF), ALU.add))
            for g in range(4):
                wait_evac(dve, JOB["go"] + g)
            dve.sem_inc(og_ready, 1)
            wait_evac(dve, JOB["sgd"])
            wait_evac(dve, JOB["sgd"] + 1)
            for h in range(NH):
                if h >= 2:
                    wait_done(dve, JOB["sgo"] + 2 * h - 3)
                V.tensor_tensor(at(B2 + (h % 2) * 1024, 1024, NS).rearrange("p (s e) -> p s e", e=P),
                                at(B3 + h * P, P, NS).unsqueeze(1).broadcast_to([NS, NS, P]),
                                cst(C_ID, NS, NS).unsqueeze(2).broadcast_to([NS, NS, P]), ALU.mult).then_inc(dmn_ready, 1)
                for g in range(2):
                    n = JOB["sgo"] + 2 * h + g
                    wait_done(dve, n)
                    for i in range(4):
                        s = 4 * g + i
                        st = state_of(s)[:, h * P:(h + 1) * P]
                        ins = V.scalar_tensor_tensor(out=st, in0=st, scalar=at(BCS + s * NH + h, 1),
                                                     in1=bank(n)[:, i * P:(i + 1) * P], op0=ALU.mult, op1=ALU.add)
                    ins.then_inc(evac[n % 4], 1)
            wait_evac(dve, JOB["sgo"] + 15)
            dve.sem_inc(st_ready, 64)
            block_norm("gn", 8, 32, lambda b: blk(OT, NH + b), lambda b: par(G_GN), extra=lambda b: blk(PT, 48 + b))

            V.tensor_tensor(x3(DEL), lgb[0:NS, 2, 0:8].unsqueeze(1).broadcast_to([NS, NS, NH]), eyeb, ALU.mult)
            V.tensor_tensor(sh(PSF), hs(QS), hs(KS), ALU.mult).then_inc(own_ready, 1)
            n = JOB["slf"]
            wait_done(dve, n)
            V.memset(at(LFS + 448, 64), 0.0)
            V.tensor_copy(at(LF, 512).rearrange("p (j s h) -> p h s j", j=PAGES, s=NS),
                          bank(n).rearrange("p (h s j) -> p h s j", h=NH, s=NS)).then_inc(evac[n % 4], 1)
            wait_evac(dve, n)
            n = JOB["sown"]
            wait_done(dve, n)
            own = lambda c, w=1: at(OWN + c, w, 64)
            V.tensor_copy(own(0), bank(n)[0:64, 0:1]).then_inc(evac[n % 4], 1)
            dve.wait_ge(qm_zero, 1)
            V.tensor_copy(at(QM, 64 * 65).rearrange("p (s h c) -> p s h c", h=NH, c=65)[:, :, :, 0],
                          at(QS, 64).rearrange("p (h s) -> p s h", s=NS)).then_inc(qm_ready, 1)
            for q in range(RING):
                low_part(dve, 0, 0, S0["gates"], q)
            for j in range(PAGES - 2, -1, -1):
                ins = V.tensor_tensor(at(LFS + j * 64, 64), at(LFS + (j + 1) * 64, 64), at(LF + (j + 1) * 64, 64), ALU.add)
                if j:
                    ch(ins)
            ins.then_inc(lfs_ready, 1)
            with dve.Fori(0, 3) as it:
                for j in range(RING):
                    for q in range(RING):
                        low_part(dve, it, 4, S0["gates"] + j + 1, q)
            for j in range(RING - 1):
                for q in range(RING):
                    low_part(dve, 0, 0, S0["gates"] + 13 + j, q)
            dve.wait_ge(score_ready, 1)
            wait_evac(dve, JOB["sown"])
            ch(V.tensor_reduce(own(1, 2), ps[0:64, 4:6, :], AX.X, ALU.max))
            ch(V.tensor_reduce(own(3), own(1, 2), AX.X, ALU.max))
            V.tensor_scalar(own(3), own(3), own(0), -1.0, ALU.max, ALU.mult).then_inc(sp_in, 1)
            dve.wait_ge(sp_exp, 3)
            ch(V.tensor_reduce(own(7), own(4, 3), AX.X, ALU.add))
            ch(V.reciprocal(own(7), own(7)))
            V.tensor_scalar(at(PROB, PAGES * P, 64), at(PROB, PAGES * P, 64), own(7), None, ALU.mult).then_inc(sp_ready, 1)
            ch(V.tensor_scalar(own(6), own(6), own(7), None, ALU.mult))
            V.tensor_scalar(own(64, 64), cst(C_ID, 64, 64), own(6), None, ALU.mult).then_inc(dg_ready, 1)
            n = JOB["spt"]
            wait_done(dve, n)
            V.tensor_copy(at(PRT, 512), bank(n)).then_inc(evac[n % 4], 1)
            n = JOB["spb"]
            wait_done(dve, n)
            V.tensor_copy(at(PSF, 64), bank(n)[:, 0:64]).then_inc(evac[n % 4], 1)
            for q in range(RING):
                low_part(dve, 0, 0, S0["gates"] + 16, q)
            for s in range(NS):
                for i in range(2):
                    for q in range(RING):
                        if 2 * s + i < 15:
                            low_part(dve, 0, 0, S0["gates"] + 17 + 2 * s + i, q)
                dve.wait_ge(page_done, 64 + 8 * s + 8)
                b = 4 + 2 * (s % 2)
                ch(V.tensor_tensor(at(OSEL, NH * P, NH).rearrange("p (h d) -> p h d", d=P),
                                   ps[0:NH, b:b + 2, :].rearrange("p b (h d) -> p (b h) d", d=P),
                                   cst(C_ID, NH, NH).unsqueeze(2).broadcast_to([NH, NH, P]), ALU.mult))
                V.tensor_reduce(at(ON + s * P, P, NH), at(OSEL, NH * P, NH).rearrange("p (h d) -> p d h", d=P),
                                AX.X, ALU.add).then_inc(on_ready, 1)
            wait_evac(dve, JOB["spb"])
            ch(V.tensor_tensor(hs(LF), hs(VS), sh(PSF), ALU.mult))
            n = JOB["sot"]
            wait_done(dve, n)
            V.tensor_tensor(ot3[:, 0:8, SEQ:T], hs(LF), bank(n)[:, 0:64].rearrange("p (s h) -> p h s", h=NH),
                            ALU.add).then_inc(of_ready, 1)
            dve.wait_ge(of_ready, 1)
            dve.sem_inc(evac[n % 4], 1)
            wait_evac(dve, JOB["gates1"] + 15)

            dve.wait_ge(of_ready, 1)
            with dve.Fori(0, 4) as it:
                for j in range(RING):
                    n = JOB["up"] + j
                    dve.wait_ge(pe_job, it * 4 + PJ[n])
                    ga = arena[:, bass.ds(it * (4 * T) + (GT + j * T), T)]
                    gb = arena[:, bass.ds(it * (4 * T) + (GT + (16 + j) * T), T)]
                    m, t = at(TMU + (j % 2) * 2 * T, T), at(TMU + ((j % 2) * 2 + 1) * T, T)
                    V.tensor_tensor(t, gb, ps[:, 4 + n % 4, 0:T], ALU.mult).then_inc(mg_step, 1)
                    V.tensor_tensor(m, ga, ps[:, n % 4, 0:T], ALU.mult).then_inc(evac[n % 4], 1)
                    dve.wait_ge(mg_step, it * 8 + (2 * j + 1))
                    dve.wait_ge(evac[n % 4], it + (n // 4 + 1))
                    V.tensor_tensor(m, m, t, ALU.add).then_inc(merged, 1)
                    dve.wait_ge(mh_ready, it * 4 + (j + 1))
                    V.tensor_tensor(split[:, bass.ds(it * (4 * T) + (HL + j * T), T)], m,
                                    as_f32(split[:, bass.ds(it * (4 * T) + (HH + j * T), T)]), ALU.subtract).then_inc(mg_step, 1)
            dve.wait_ge(mg_step, 32)
            dve.sem_inc(mt_ready, 1)

            def add_to_x(it, j):
                n = JOB["out"] + j
                wait_quarter(dve, it, 4, S0["out"] + j, RING - 1)
                x = XT + j * T
                x = at(x + it * 4 * T, T) if isinstance(it, int) else arena[:, bass.ds(it * (4 * T) + x, T)]
                V.tensor_tensor(x, x, bank(n)[:, 0:T], ALU.add).then_inc(evac[n % 4], 1)

            dve.wait_ge(x_again, 16)
            dense_steps(dve, S0["out"], 4, low_part, add_to_x)
            for j in range(RING):
                wait_evac(dve, JOB["out"] + 12 + j)
            dve.sem_inc(x1_ready, 1)
            norm(1, G_FFN)
            low_parts("wq")

            for c in range(3):
                m = P if c < 2 else NS

                def v(a, n):
                    return at(a, n, m)

                for g in range(4):
                    wait_evac(dve, RS_JOB[c] + g)

                def top16(src, src2, vals, idxs, count, width):
                    for q in range(count):
                        ch(V.max(out=v(vals + 16 * q, 8), in_=v(src + width * q, width)))
                        V.max_index(v(idxs + 16 * q, 8).bitcast(U32), v(vals + 16 * q, 8), v(src + width * q, width))
                        ch(V.match_replace(v(src2 + width * q, width), v(vals + 16 * q, 8), v(src + width * q, width), BIGNEG))
                        ch(V.max(out=v(vals + 16 * q + 8, 8), in_=v(src2 + width * q, width)))
                        ch(V.max_index(v(idxs + 16 * q + 8, 8).bitcast(U32), v(vals + 16 * q + 8, 8), v(src2 + width * q, width)))

                top16(RS, RS2, SV, SI, 16, P)
                sv = v(SV, 256).rearrange("p (h q k) -> p h q k", q=2, k=16)
                ca = v(CA, 2048).rearrange("p (h i j) -> p h i j", i=16, j=16)
                for h in range(NH):
                    ch(V.tensor_tensor(ca[:, h], sv[:, h, 0, :].unsqueeze(2).broadcast_to([m, 16, 16]),
                                       sv[:, h, 1, :].unsqueeze(1).broadcast_to([m, 16, 16]), ALU.add))
                top16(CA, CA2, CV, CI, 8, 256)
                ch(V.tensor_copy(v(SIF, 256), v(SI, 256).bitcast(U32)))
                ch(V.tensor_scalar(v(CSA, P).bitcast(U32), v(CI, P).bitcast(U32), 4, None, ALU.logical_shift_right))
                ch(V.tensor_scalar(v(CSB, P).bitcast(U32), v(CI, P).bitcast(U32), 15, None, ALU.bitwise_and))
                ch(V.tensor_copy(v(CFA, P), v(CSA, P).bitcast(U32)))
                ch(V.tensor_copy(v(CFB, P), v(CSB, P).bitcast(U32)))
                if c:
                    wait_done(dve, IDX_JOB[c - 1])
                for side, cf in ((0, CFA), (1, CFB)):
                    eq = v(CA, 2048).rearrange("p (a j) -> p a j", j=16)
                    ch(V.tensor_tensor(eq, v(cf, P).unsqueeze(2).broadcast_to([m, P, 16]),
                                       cst(C_IOTA, 16, m).unsqueeze(1).broadcast_to([m, P, 16]), ALU.is_equal))
                    e4 = v(CA, 2048).rearrange("p (h k j) -> p h k j", k=16, j=16)
                    sif = v(SIF, 256).rearrange("p (h q k) -> p h q k", q=2, k=16)
                    for h in range(NH):
                        ins = V.tensor_tensor(e4[:, h], e4[:, h], sif[:, h, side, :].unsqueeze(1).broadcast_to([m, 16, 16]), ALU.mult)
                    ch(ins)
                    ch(V.tensor_reduce(v(RES + side * P, P), eq, AX.X, ALU.add))
                cv = v(CV, P).rearrange("p (h k) -> p h k", k=16)
                gt = v(RES + 2 * P, P).rearrange("p (h k) -> p h k", k=16)
                V.tensor_tensor(gt, cv, cv[:, :, 0:1].broadcast_to([m, 8, 16]), ALU.subtract).then_inc(re_in, 1)
                dve.wait_ge(re_exp, c + 1)
                ch(V.tensor_reduce(v(RSM, 8), gt, AX.X, ALU.add))
                ch(V.reciprocal(v(RSM, 8), v(RSM, 8)))
                V.tensor_tensor(gt, gt, v(RSM, 8).unsqueeze(2).broadcast_to([m, 8, 16]), ALU.mult).then_inc(res_ready, 1)
                n = IDX_JOB[c]
                wait_done(dve, n)
                V.tensor_copy(at(IDX, 3 * T).rearrange("p (i t) -> p i t", t=T)[:, :, c * P:c * P + m],
                              bank(n)[:, 0:384].rearrange("p (i t) -> p i t", t=P)[:, :, 0:m]).then_inc(evac[n % 4], 1)
            wait_evac(dve, IDX_JOB[2])

            for half in range(2):
                wb, ub = JOB[f"wb{half}"], JOB[f"u{half}"]

                def onehot_a(it, j, lead):
                    if not lead:
                        dve.wait_ge(pe_job, it * 4 + (PJ[wb + j] - 2))
                    oh = at(OHA + (j % 2) * 8 * HALF, 8 * HALF).rearrange("p (t a) -> p t a", a=HALF)
                    col = lambda q: arena[:, bass.ds(it * 32 + (IDX + q * T + 8 * j), 8)].unsqueeze(2).broadcast_to([P, 8, HALF])
                    V.tensor_tensor(oh, cst(C_IOTA + half * HALF, HALF).unsqueeze(1).broadcast_to([P, 8, HALF]), col(0),
                                    ALU.is_equal).then_inc(oh_step, 1)
                    dve.wait_ge(oh_step, it * 4 + (33 * half + j + 1))
                    V.tensor_tensor(at(OHB + (j % 2) * 8 * P, 8 * P).rearrange("p (t b) -> p t b", b=P),
                                    cst(C_IOTA).unsqueeze(1).broadcast_to([P, 8, P]),
                                    arena[:, bass.ds(it * 32 + (IDX + T + 8 * j), 8)].unsqueeze(2).broadcast_to([P, 8, P]),
                                    ALU.is_equal).then_inc(ohb_ready, 1)
                    V.tensor_tensor(oh, oh, col(2), ALU.mult).then_inc(oha_ready, 1)

                if half:
                    wait_done(dve, JOB["wb0"] + 32)
                for j in range(4):
                    onehot_a(0, j, j < 2)
                with dve.Fori(1, 8) as it:
                    for j in range(4):
                        onehot_a(it, j, False)
                onehot_a(8, 0, False)
                for b in range(4):
                    wait_evac(dve, wb + 29 + b)

                s0 = S0[f"peer{half}"]

                def weigh(it, m, s, n, g, buf):
                    for j in range(RING):
                        for q in range(RING):
                            low_part(dve, it, m, s + j + 1, q)
                        dve.wait_ge(evac[(n + j) % 4], it * (m // 8) + ((n + j) // 4 + 1))
                        a, o = at(AB + (j % 2) * T, T), (buf * EG + j) * T
                        w = WH + (4 * g + j) * T
                        w = arena[:, bass.ds(it * (8 * T) + w, T)] if m else at(w, T)
                        blk_n = 4 * (16 * half + g) + j + 1
                        V.tensor_tensor(sp_(AH + o, T), a, w, ALU.mult).then_inc(ah_ready, 1)
                        V.tensor_tensor(a, a, w, ALU.mult).then_inc(aw_ready, 1)
                        dve.wait_ge(ah_ready, it * (m // 2) + blk_n)
                        dve.wait_ge(aw_ready, it * (m // 2) + blk_n)
                        V.tensor_tensor(sp_(AL + o, T), a, as_f32(sp_(AH + o, T)), ALU.subtract).then_inc(a_blk, 1)

                def add_outputs(it, m, s, last=False):
                    for dq in range(RING):
                        for q in range(RING):
                            if not (last and dq == RING - 1):
                                low_part(dve, it, m, s + dq + 1, q)
                            wait_quarter(dve, it, m, s + dq, q)
                            d = 4 * dq + q
                            V.tensor_tensor(xt3[:, d, :], xt3[:, d, :], ps[:, 4 + q, 0:T], ALU.add).then_inc(y_added, 1)

                for q in range(RING):
                    low_part(dve, 0, 0, s0, q)
                weigh(0, 0, s0, ub, 0, 0)
                with dve.Fori(0, 7) as i2:
                    for b in range(2):
                        weigh(i2, 16, s0 + 4 + 8 * b, ub + 4 + 4 * b, b + 1, 1 - b)
                        add_outputs(i2, 16, s0 + 8 + 8 * b)
                weigh(0, 0, s0 + 116, ub + 60, 15, 1)
                add_outputs(0, 0, s0 + 120)
                add_outputs(0, 0, s0 + 124, True)
            dve.wait_ge(y_added, 516)
            dve.sem_inc(x2_ready, 1)
            norm(2, G_PLE)
            def add_embedding(it, j):
                b = 4 * it + j
                n = JOB["ple"] + b
                wait_evac(dve, n)
                dve.wait_ge(pw_done, b + 1)
                t = at(TMP + (b % 2) * T, T)
                ch(V.tensor_tensor(t, blk(GPL, b), ps[:, 4 + b % 4, 0:T], ALU.mult))
                V.tensor_tensor(xt3[:, b, :], xt3[:, b, :], t, ALU.add).then_inc(fin_ready, 1)

            for q in range(RING):
                low_part(dve, 0, 0, S0["ple"], q)
            for b in range(16):
                for q in range(RING):
                    if b < 15:
                        low_part(dve, 0, 0, S0["ple"] + b + 1, q)
                add_embedding(b // 4, b % 4)


def kernel(**inputs):
    import concourse.bacc as bacc
    from concourse.bass_utils import run_bass_kernel_spmd

    x = {k: np.asarray(v) for k, v in inputs.items()}
    c = np.ascontiguousarray
    FW = NH * P
    OFF_F, OFF_G = 3 * FW, 3 * FW + NH
    OFF_A = OFF_G + 3 * FW
    OFF_Z = OFF_A + 2 * NH
    OFF_GATE = OFF_Z + FW
    w_in = x["w_in"][0]

    def blocks(w):
        k, n = w.shape
        return w.reshape(k // P, P, n // P, P).transpose(2, 1, 0, 3).reshape(n // P, P, k)

    def cols(a, tiles):
        return c(a.reshape(T, tiles, P).transpose(2, 1, 0)).reshape(P, tiles * T)

    up = np.concatenate([x["w_up_fox"][0], x["w_up_gdn"][0]], 0)
    wd = np.concatenate([
        blocks(w_in[:, 0:OFF_F]), blocks(w_in[:, OFF_G:OFF_A]), blocks(w_in[:, OFF_Z:OFF_GATE]),
        blocks(w_in[:, OFF_GATE:]), blocks(up), blocks(x["w_out"][0]), blocks(x["peer_w_q"][0]),
        x["peer_u"][0].reshape(N_KEYS, P, KT, P).transpose(0, 3, 2, 1).reshape(N_KEYS, P, D_MODEL),
        blocks(x["w_ple_gate"][0])], 0)
    small = np.concatenate([w_in[:, OFF_F:OFF_G], w_in[:, OFF_A:OFF_Z]], 1)
    rows = lambda v: np.broadcast_to(v, (P, v.shape[-1]))
    gain = lambda v: v.reshape(-1, P).T
    params = np.zeros((P, G_END), np.float32)
    params[:, G_MIX:G_FFN] = gain(x["norm_mix_g"][0])
    params[:, G_FFN:G_PLE] = gain(x["norm_ffn_g"][0])
    params[:, G_PLE:G_FQ] = gain(x["norm_ple_g"][0])
    params[:, G_FQ] = x["fox_q_norm"][0]
    params[:, G_FK] = x["fox_k_norm"][0]
    params[:, G_GN] = x["gdn_norm_g"][0]
    params[:, G_CONV:G_BIAS] = x["gdn_conv_w"][0].reshape(4, 24, P).transpose(2, 0, 1).reshape(P, 96)
    params[:, G_BIAS:G_BIAS + 8] = rows(x["fox_f_bias"])
    params[:, G_BIAS + 8:G_BIAS + 16] = rows(x["gdn_dt_bias"])
    params[:, G_ALOG:G_END] = rows(x["gdn_a_log"])

    arrays = {
        "xT": cols(np.concatenate([x["x_prompt"][0], x["x_sample"][:, 0]], 0), KT),
        "pT": cols(np.concatenate([x["p_prompt"][0, 0], x["p_sample"][0, :, 0]], 0), PLE_KT),
        "wd": wd, "vd": c(x["peer_v"][0].reshape(N_KEYS // EG, EG, P, RING, QK, P).transpose(0, 3, 2, 4, 1, 5)).reshape(N_KEYS, P, D_MODEL),
        "wsmall": c(small.reshape(KT, P, 24).transpose(1, 0, 2)).reshape(P, KT * 24),
        "wple": c(x["w_ple"][0].reshape(PLE_KT, P, D_MODEL).transpose(1, 0, 2)).reshape(P, PLE_KT * D_MODEL),
        "subk": c(x["peer_sub_keys"][0].transpose(3, 0, 1, 2)).reshape(P, 16 * P),
        "kx": x["cache_fox_k"][0].transpose(0, 3, 2, 1).reshape(POOL, P, FW),
        "vx": x["cache_fox_v"][0].reshape(POOL, P, FW), "lx": x["cache_fox_logf"][0].transpose(0, 2, 1).reshape(POOL, FW),
        "state": x["state_gdn"][0].transpose(0, 2, 1, 3).reshape(NS, P, FW),
        "convst": x["state_conv"][0].reshape(NS, 3, 24, P).transpose(3, 2, 0, 1).reshape(P, 576),
        "params": params, "consts": constants(),
        "ptab": x["page_table"].reshape(1, NS * PAGES).astype(np.int32),
    }
    nc = bacc.Bacc("TRN2", target_bir_lowering=False, num_devices=1)
    args = []
    for k, a in arrays.items():
        arrays[k] = a = c(a)
        args.append(nc.dram_tensor("in_" + k, a.shape, mybir.dt.from_np(a.dtype), kind="ExternalInput").ap())
    outs = {"o_x": (P, KT * T), "o_k": (P, NH * T), "o_v": (P, NH * T), "o_lf": (P, 3, NH), "o_sp": (P, FW),
            "o_ss": (NS, P, FW), "o_cs": (P, 24 * 27)}
    for k, s in outs.items():
        args.append(nc.dram_tensor(k, s, F32, kind="ExternalOutput").ap())
    build(nc, *args)
    r = run_bass_kernel_spmd(nc, [{"in_" + k: a for k, a in arrays.items()}], core_ids=[0]).results[0]

    tok = lambda a, tiles: np.asarray(a).reshape(P, tiles, T).transpose(2, 1, 0)
    y = tok(r["o_x"], KT).reshape(T, D_MODEL)
    k, v = tok(r["o_k"], NH), tok(r["o_v"], NH)
    lf = np.asarray(r["o_lf"]).transpose(1, 0, 2)
    sp = np.asarray(r["o_sp"]).reshape(P, NH, P).transpose(1, 0, 2)
    ss = np.asarray(r["o_ss"]).reshape(NS, P, NH, P).transpose(0, 2, 1, 3)
    cs = np.asarray(r["o_cs"]).reshape(P, 24, 27)
    cp = cs[:, :, 0:3].transpose(2, 1, 0).reshape(3, 3 * FW)
    css = cs[:, :, 3:].reshape(P, 24, NS, 3).transpose(2, 3, 1, 0).reshape(NS, 3, 3 * FW)
    return (c(y[None, :SEQ]), c(y[SEQ:, None]), c(k[None, None, :SEQ]), c(v[None, None, :SEQ]),
            c(lf[0:2].reshape(1, 1, SEQ, NH)), c(sp[None, None]), c(cp[None, None]),
            c(k[None, SEQ:, None]), c(v[None, SEQ:, None]), c(lf[2, 0:NS].reshape(1, NS, 1, NH)),
            c(ss[None]), c(css[None]))
```

```python
from contextlib import ExitStack

import numpy as np
import concourse.bass as bass
from concourse import mybir

ALU = mybir.AluOpType
ACT = mybir.ActivationFunctionType
AX = mybir.AxisListType
F32 = mybir.dt.float32
F32R = mybir.dt.float32r
I32 = mybir.dt.int32
U32 = mybir.dt.uint32

P = 128
D_MODEL = 2048
KT = D_MODEL // P
SEQ, NS = 256, 8
T = SEQ + NS
NH = 8
PAGES = 8
POOL = 80
N_KEYS = 128
PLE_KT = 2
EPS = 1e-6
NEG = -1e30
BIGNEG = -3e38
LEVELS = 7
RING = 4
QK = KT // RING
HALF = N_KEYS // 2
PGW = NH * P
EG = 4

STREAM = [("A", 56), ("gates", 32), ("up", 16), ("out", 16), ("wq", 16), ("peer0", 128), ("peer1", 128), ("ple", 16)]
S0 = {}
_n = 0
for _name, _c in STREAM:
    S0[_name] = _n
    _n += _c

JOB_LIST = [("norm0", 1), ("A", 56), ("small", 1), ("smallt", 1), ("fqks", 1), ("fqk", 16), ("gqks", 1), ("gqk", 16), ("cum", 1), ("bc", 1), ("fvt", 4),
            ("fs", 8), ("fpt", 8), ("fo", 4),
            ("gdk", 16), ("gat", 4), ("inv", 12 * LEVELS), ("gkt", 4), ("gvt", 4), ("gu", 4), ("gw", 2),
            ("gs1", 2), ("gq", 2), ("gws", 2), ("go", 4), ("gs2", 2),
            ("sg1", 1), ("sgk", 2), ("sgd", 2), ("sgo", 16), ("slf", 1), ("sown", 1), ("gns", 1), ("gn", 8),
            ("gates0", 16), ("spt", 1), ("spb", 1), ("gates1", 16), ("sot", 1), ("up", 16), ("out", 16),
            ("norm1", 1), ("wq", 16), ("route", 12)]
for _h in range(2):
    JOB_LIST += [(f"wb{_h}", 66), (f"u{_h}", 64)]
JOB_LIST += [("norm2", 1), ("ple", 16)]
JOB = {}
SPLIT_JOBS = ("A", "gates0", "gates1", "out", "wq", "u0", "u1", "ple")
PJ = []
_n = _p = 0
for _name, _c in JOB_LIST:
    JOB[_name] = _n
    for _ in range(_c):
        _p += _name not in SPLIT_JOBS
        PJ.append(_p)
    _n += _c


def split_index(s):
    return s if s < S0["up"] else s - 16


def stream_of(n):
    for name, s in (("A", S0["A"]), ("gates0", S0["gates"]), ("gates1", S0["gates"] + 16), ("out", S0["out"]),
                    ("wq", S0["wq"]), ("ple", S0["ple"])):
        count = dict(JOB_LIST)[name]
        if JOB[name] <= n < JOB[name] + count:
            return s + n - JOB[name]
    for h in range(2):
        k = n - JOB[f"u{h}"]
        if 0 <= k < 64:
            return S0[f"peer{h}"] + (k if k < 4 else 4 + 8 * ((k - 4) // 4) + k % 4)
    return None


RS_JOBS = [[JOB["route"] + o for o in js] for js in ((0, 1, 2, 3), (4, 5, 6, 7), (9,))]
IDX_JOB = [JOB["route"] + o for o in (8, 10, 11)]
ROUTE_TILES = ((P, NH), (P, NH), (NH * NS, 1))

C_ID, C_ONE, C_UPI, C_LOW, C_IOTA, C_INV, C_CAUS = 0, 128, 256, 384, 512, 640, 1536
C_EPS, C_EPS128, C_SEL, C_RT, C_END = 1984, 1985, 1986, 2017, 2023


def constants():
    i = np.arange(P)[:, None]
    j = np.arange(P)[None, :]
    c = np.zeros((P, C_END), np.float32)
    c[:, C_ID:C_ID + P] = i == j
    c[:, C_ONE:C_ONE + P] = 1
    c[:, C_UPI:C_UPI + P] = i <= j
    c[:, C_LOW:C_LOW + P] = i > j
    c[:, C_IOTA:C_IOTA + P] = j
    for lv in range(LEVELS):
        s = 1 << lv
        c[:, C_INV + lv * P:C_INV + (lv + 1) * P] = (i // (2 * s) == j // (2 * s)) & (i // s % 2 == 1) & (j // s % 2 == 0)
    caus = np.where(j > i, NEG, 0)
    c[:, C_CAUS:C_CAUS + P] = caus
    c[:, C_CAUS + 2 * P:C_CAUS + 3 * P] = caus
    c[:, C_SEL + 15] = 1
    c[0:16, C_RT] = np.repeat([1, 1 / P], 8)
    c[0:16, C_RT + 1] = np.repeat([P * EPS, EPS], 8)
    c[0:16, C_RT + 2] = np.repeat([P, 1], 8)
    c[0:16, C_RT + 3] = np.repeat([P * EPS, EPS], 8)
    c[0:8, C_RT + 4] = 1 / P
    c[0:8, C_RT + 5] = EPS
    c[:, C_EPS] = EPS
    c[:, C_EPS128] = P * EPS
    return c


G_MIX, G_FFN, G_PLE, G_FQ, G_FK, G_GN, G_CONV, G_BIAS, G_ALOG, G_END = 0, 16, 32, 48, 49, 50, 51, 147, 171, 179


def build(nc, xT, pT, wd, vd, wsmall, wple, subk, kx, vx, lx, state, convst, params, consts, ptab,
          o_x, o_k, o_v, o_lf, o_sp, o_ss, o_cs):
    with ExitStack() as ctx:
        NF, NR = 36332, 16768
        arena = ctx.enter_context(nc.sbuf_tensor("arena", [P, NF], F32))
        split = ctx.enter_context(nc.sbuf_tensor("split", [P, NR], F32R))
        ptb = ctx.enter_context(nc.sbuf_tensor("ptb", [1, NS * PAGES], I32))
        ps = ctx.enter_context(nc.psum_tensor("ps", [P, 8, 512], F32))
        top = [0]

        def take(n):
            a = top[0]
            top[0] += n
            assert top[0] <= NF, top[0]
            return a

        def at(a, n, p=P):
            return arena[0:p, a:a + n]

        CST = take(C_END)
        PAR = take(G_END)
        small_base = take(760)
        WR = take(RING * D_MODEL)
        XT = take(KT * T)
        SC = XT
        BIG = top[0]
        take(6144 - KT * T)
        PT = take(56 * T)
        OT = take(2 * NH * T)
        BIG_END = NF
        PG = PT + 32 * T
        SQ = PT
        HRAW = PT + KT * T

        HH, HL = 0, KT * T
        CKH = 2 * KT * T
        CKL = CKH + D_MODEL
        AH = CKL + D_MODEL
        AL = AH + 2 * EG * T
        WSH, WSL = AH, AH + 384
        assert AL + 2 * EG * T <= NR
        sp_ = lambda a, n: split[:, a:a + n]
        as_f32 = lambda ap: ap.bitcast(F32)
        hh3 = sp_(HH, KT * T).rearrange("p (k t) -> p k t", t=T)
        hl3 = sp_(HL, KT * T).rearrange("p (k t) -> p k t", t=T)
        QW = QK * P
        ckh = lambda q: sp_(CKH + q * QW, QW)
        ckl = lambda q: sp_(CKL + q * QW, QW)

        cst = lambda c, n=P, p=P: arena[0:p, CST + c:CST + c + n]
        par = lambda c, n=1, p=P: arena[0:p, PAR + c:PAR + c + n]
        ident, ones, upi, low = cst(C_ID), cst(C_ONE), cst(C_UPI), cst(C_LOW)
        eps = cst(C_EPS, 1)
        wr = lambda j: at(WR + j * D_MODEL, D_MODEL)
        blk = lambda base, b: at(base + b * T, T)
        xt3 = at(XT, KT * T).rearrange("p (k t) -> p k t", t=T)
        pt3 = at(PT, 56 * T).rearrange("p (k t) -> p k t", t=T)
        ot3 = at(OT, 2 * NH * T).rearrange("p (k t) -> p k t", t=T)
        page = lambda j: at(PG + (j % 4) * PGW, PGW)
        state_of = lambda s: at(WR + s * NH * P, NH * P)

        st_top = [small_base]

        def stake(n):
            a = st_top[0]
            st_top[0] += n
            assert st_top[0] <= small_base + 760, st_top[0] - small_base
            return a

        LGB = stake(72)
        EXS = stake(48)
        BEG = stake(16)
        BCS = stake(256)
        QS = stake(64)
        KS = stake(64)
        VS = stake(64)
        NEGM = stake(16)
        SUMS = stake(16)
        DEL = stake(64)
        ALE = stake(8)
        PSF = stake(64)
        lgb = at(LGB, 72).rearrange("p (c k) -> p c k", c=3)

        SMX, SMU, SMY, SMZ, SMZ2, SMP = (SC + 5184 + 72 * i for i in range(6))
        CST_ST = SC + 3100
        CACC, CSAMP, CPROD, CCOPY = SC + 1500, SC + 2012, SC + 2204, SC + 2396

        WH = BIG
        AB = WH + HALF * T
        IDX = AB + 2 * T
        assert IDX + 3 * T <= BIG_END, IDX + 3 * T
        OHA = WR + 2 * D_MODEL
        OHB = OHA + 2 * 8 * HALF
        assert OHB + 2 * 8 * P <= WR + RING * D_MODEL
        QT = BIG
        RS = QT + 16 * T
        RS2 = RS + 2048
        CA = RS2 + 2048
        CA2 = CA + 2048
        SV = CA2 + 2048
        SI = SV + 256
        SIF = SI + 256
        CV = SIF + 256
        CI = CV + 128
        CSA = CI + 128
        CSB = CSA + 128
        CFA = CSB + 128
        CFB = CFA + 128
        RES = CFB + 128
        RSM = RES + 384
        SK = RSM + 32
        assert SK >= HRAW + KT * T and SK + 16 * P <= IDX
        QZ = IDX + 3 * T
        assert QZ + 64 + NH * 136 <= BIG_END
        ROW_H, ROW_T = RSM + 8, RSM + 16
        LX = CA2
        GPL = BIG
        WPL = HRAW + KT * T
        PTI = WPL + PLE_KT * D_MODEL
        TMP = PTI + PLE_KT * T

        GT = PT
        TMU = PT + 40 * T

        def sem(name):
            return ctx.enter_context(nc.semaphore(name))

        QM = SC
        LFR = SC + 4096
        LF = LFR + NH * P
        LFS = LF + 512
        PROB = SC
        PRT = PROB + PAGES * P
        OSEL = PRT + 1024
        ON = OSEL + NH * P
        OWN = LFR

        pe_job = sem("pe_job")
        evac = [sem(f"evac{b}") for b in range(4)]
        w_loaded = [sem(f"w_loaded{j}") for j in range(RING)]
        quarter_done = sem("quarter_done")
        hi_ready, lo_ready = sem("hi_ready"), sem("lo_ready")
        hraw_ready, hh_ready = sem("hraw_ready"), sem("hh_ready")
        merged, mh_ready = sem("merged"), sem("mh_ready")
        ws_hi, ws_lo = sem("ws_hi"), sem("ws_lo")
        x_again = sem("x_again")
        aw_ready, ah_ready = sem("aw_ready"), sem("ah_ready")
        pg_loaded = [sem(f"pg_loaded{j}") for j in range(PAGES)]
        st_loaded = [sem(f"st_loaded{s}") for s in range(NS)]
        page_done = sem("page_done")
        x_in, c_in, p_in, ws_in, cs_in, pt_in, sk_in, ple_in = (sem(n) for n in (
            "x_in", "c_in", "p_in", "ws_in", "cs_in", "pt_in", "sk_in", "ple_in"))
        out_dma = sem("out_dma")
        state_saved = [sem(f"state_saved{j}") for j in range(RING)]
        sq_ready, ht_ready = sem("sq_ready"), sem("ht_ready")
        bsq_used = sem("bsq_used")
        bsq_ready, brt_ready, bn_ready = sem("bsq_ready"), sem("brt_ready"), sem("bn_ready")
        dch = sem("dve_chain")
        sm_u, sm_e = sem("small_u"), sem("small_e")
        gates_ready = sem("token_gates_ready")
        conv_acc, conv_out, conv_step = sem("conv_acc"), sem("conv_out"), sem("conv_step")
        lfl_ready = sem("lfl_ready")
        lf_in, qm_zero, qm_ready, own_ready = sem("lf_in"), sem("qm_zero"), sem("qm_ready"), sem("own_ready")
        lfs_ready, score_ready, on_ready = sem("lfs_ready"), sem("score_ready"), sem("on_ready")
        neg_ready, prob_raw, prob_ready = sem("neg_ready"), sem("prob_raw"), sem("prob_ready")
        a_ready = sem("a_ready")
        t_init = sem("t_init")
        gb_ready, qe_ready = sem("gb_ready"), sem("qe_ready")
        s2_ready = sem("s2_ready")
        del_ready, dmn_ready, st_ready = sem("del_ready"), sem("dmn_ready"), sem("st_ready")
        bcx_ready, og_ready = sem("bcx_ready"), sem("og_ready")
        dg_ready, sp_in, sp_exp, sp_ready, of_ready = (sem(n) for n in ("dg_ready", "sp_in", "sp_exp", "sp_ready", "of_ready"))
        mt_ready, x1_ready, x2_ready = sem("mt_ready"), sem("x1_ready"), sem("x2_ready")
        re_in, re_exp, res_ready = sem("re_in"), sem("re_exp"), sem("res_ready")
        qz_ready, sel_step = sem("qz_ready"), sem("sel_step")
        oha_ready, ohb_ready = sem("oha_ready"), sem("ohb_ready")
        a_blk = sem("a_blk")
        y_added = sem("y_added")
        pw_done, fin_ready = sem("pw_done"), sem("fin_ready")
        lf_saved = sem("lf_saved")
        conv_copied, cs_saved, kv_saved, sp_saved, qs_copied = (sem(n) for n in (
            "conv_copied", "cs_saved", "kv_saved", "sp_saved", "qs_copied"))
        eg_ready, convs_ready = sem("eg_ready"), sem("convs_ready")
        mg_step, oh_step = sem("merge_step"), sem("onehot_step")

        def wait_done(eng, n):
            s = stream_of(n)
            if s is None:
                eng.wait_ge(pe_job, PJ[n])
            else:
                eng.wait_ge(quarter_done, 4 * (split_index(s) + 1))

        def wait_evac(eng, n):
            eng.wait_ge(evac[n % 4], n // 4 + 1)

        def claim(pe, n):
            if n >= 4:
                wait_evac(pe, n - 4)

        def bank(n):
            return ps[:, n % 4, :]

        class Chain:

            def __init__(self, eng, s):
                self.eng, self.s, self.n = eng, s, 0

            def __call__(self, ins):
                self.n += 1
                ins.then_inc(self.s, 1)
                self.eng.wait_ge(self.s, self.n)

        def wait_high_part(eng, it, m, s, q):
            eng.wait_ge(hi_ready, it * (4 * m) + (4 * split_index(s) + q + 1))

        def wait_low_part(eng, it, m, s, q):
            eng.wait_ge(lo_ready, it * (4 * m) + (4 * split_index(s) + q + 1))

        def wait_quarter(eng, it, m, s, q):
            eng.wait_ge(quarter_done, it * (4 * m) + (4 * split_index(s) + q + 1))

        def wait_slot(eng, it, m, s, back=0):
            if S0["up"] <= s < S0["out"]:
                eng.wait_ge(pe_job, it * m + (PJ[JOB["up"] + s - S0["up"]] - back))
            else:
                eng.wait_ge(lo_ready, it * (4 * m) + 4 * (split_index(s) + 1 - back))

        def high_part(act, it, m, s, q):
            if q == 0:
                act.wait_ge(w_loaded[s % 4], it * (4 * m) + 16 * (s // 4 + 1))
            c = split_index(s)
            if c:
                act.wait_ge(quarter_done, it * (4 * m) + (4 * (c - 1) + q + 1))
            nc.scalar.activation(ckh(q), at(WR + (s % 4) * D_MODEL + q * QW, QW), ACT.Copy).then_inc(hi_ready, 1)

        def low_part(dve, it, m, s, q):
            wait_high_part(dve, it, m, s, q)
            nc.vector.tensor_tensor(ckl(q), at(WR + (s % 4) * D_MODEL + q * QW, QW), as_f32(ckh(q)),
                                    ALU.subtract).then_inc(lo_ready, 1)

        def dense_steps(eng, s0, its, part, finish, first=True, final=True):
            for q in range(RING if first else 0):
                part(eng, 0, 4, s0, q)

            def step(it, j, last=False):
                for q in range(RING):
                    if not last:
                        part(eng, it, 4, s0 + j + 1, q)
                finish(it, j)
            if its > 1:
                with eng.Fori(0, its - 1) as it:
                    for j in range(RING):
                        step(it, j)
            for j in range(RING):
                step(its - 1, j, final and j == RING - 1)

        def load_pages(eng, part, s, odd, some=range(PAGES)):
            for j in some[odd::2]:
                if part == 0 and isinstance(s, int) and s == 0 and j < 4:
                    eng.wait_ge(st_ready, 64)
                else:
                    eng.wait_ge(page_done, s * 8 + (64 * part + j - 3))
                r = eng.value_load(ptb[0:1, bass.ds(s * PAGES + j, 1)])
                src = (kx, vx)[part]
                eng.dma_start(page(j), src[bass.ds(r, 1)].rearrange("o p c -> (o p) c")).then_inc(pg_loaded[j], 16)

        block = ctx.enter_context(nc.Block())

        @block.sync
        def _(sp):
            sp.dma_start(at(XT, KT * T), xT).then_inc(x_in, 16)
            sp.dma_start(at(CST, C_END), consts).then_inc(c_in, 16)
            sp.dma_start(at(PAR, G_END), params).then_inc(p_in, 16)
            sp.dma_start(at(SC + 4224, 384), wsmall).then_inc(ws_in, 16)
            sp.dma_start(ptb[:, :], ptab).then_inc(pt_in, 16)

            def load_w(it, m, s, src, n):
                if isinstance(it, int):
                    sp.dma_start(wr(s % 4), src[n]).then_inc(w_loaded[s % 4], 16)
                else:
                    sp.dma_start(wr(s % 4), src[bass.ds(it * m + n, 1)].rearrange("o p c -> (o p) c")).then_inc(w_loaded[s % 4], 16)

            def peel(s0, n0, late=None):
                for j in range(RING):
                    if s0:
                        wait_slot(sp, 0, 0, s0 + j - RING)
                    if late is not None and j >= 2:
                        sp.wait_ge(pe_job, late)
                    load_w(0, 0, s0 + j, wd, n0 + j)

            def loop(s0, n0, its):
                peel(s0, n0)
                with sp.Fori(1, its) as it:
                    for j in range(RING):
                        wait_slot(sp, it, 4, s0 + j, RING)
                        load_w(it, 4, s0 + j, wd, n0 + j)

            loop(S0["A"], 0, 14)

            sp.wait_ge(pt_in, 16)
            sp.wait_ge(s2_ready, 8)
            for c in range(NS * PAGES):
                r = sp.value_load(ptb[0:1, c:c + 1])
                sp.dma_start(arena[c:c + 1, LFR:LFR + NH * P], lx[bass.ds(r, 1)]).then_inc(lf_in, 16)

            def load_gate(it, k):
                g = S0["gates"] + k
                if isinstance(it, int) and k < RING:
                    sp.wait_ge(state_saved[k], 32)
                wait_slot(sp, it, 4, g, RING)
                load_w(it, 4, g, wd, g)

            def beside(part, it, j):
                load_pages(sp, part, it * 2 + j // 2, 0, range(4 * (j % 2), 4 * (j % 2) + 4))

            load_gate(0, 0)
            load_gate(0, 1)
            for j in range(4):
                load_gate(0, j + 2)
                beside(0, 0, j)
            with sp.Fori(1, 4) as it:
                for j in range(4):
                    load_gate(it, j + 2)
                    beside(0, it, j)
            with sp.Fori(0, 3) as it:
                for j in range(4):
                    load_gate(it, 16 + j + 2)
                    beside(1, it, j)
            for j in range(4):
                if j < 2:
                    load_gate(0, 28 + j + 2)
                beside(1, 3, j)

            loop(S0["up"], 88, 4)
            loop(S0["out"], 104, 4)
            sp.wait_ge(mt_ready, 1)
            sp.dma_start(at(SK, 16 * P), subk).then_inc(sk_in, 16)
            loop(S0["wq"], 120, 4)

            for half in range(2):
                s0, u0, v0 = S0[f"peer{half}"], 136 + 64 * half, 64 * half
                peel(s0, u0, PJ[JOB[f"wb{half}"] + 65])

                def group(it):
                    for kind in range(2):
                        for j in range(RING):
                            s = s0 + 4 + 4 * kind + j
                            wait_slot(sp, it, 8, s, RING)
                            load_w(it, 4, s, (wd, vd)[kind], ((u0 + 4) + j, v0 + j)[kind])

                with sp.Fori(0, 15) as it:
                    group(it)
                for j in range(RING):
                    wait_slot(sp, 0, 0, s0 + 120 + j)
                    load_w(0, 0, s0 + 124 + j, vd, v0 + 60 + j)
            loop(S0["ple"], 264, 4)
            for q in range(4):
                sp.wait_ge(fin_ready, 4 * q + 4)
                sp.dma_start(o_x[:, 4 * q * T:(4 * q + 4) * T], at(XT + 4 * q * T, 4 * T)).then_inc(out_dma, 16)
            sp.wait_ge(out_dma, 16 * 4)
            sp.wait_ge(lf_saved, 16)
            sp.wait_ge(cs_saved, 16)
            sp.wait_ge(kv_saved, 32)
            sp.wait_ge(sp_saved, 16)

        @block.tensor
        def _(pe):
            mm = nc.tensor.matmul

            def norm(r):
                n = JOB[f"norm{r}"]
                claim(pe, n)
                if r == 0:
                    pe.wait_ge(c_in, 16)
                for k in range(KT):
                    if k % 4 == 0:
                        pe.wait_ge(sq_ready, 4 * r + k // 4 + 1)
                    last = mm(bank(n)[:, 0:T], ones, blk(SQ, k), start=(k == 0), stop=(k == KT - 1))
                last.then_inc(pe_job, 1)

            def products(out, wh, wl, xh, xl, start, stop):
                mm(out, wh, xh, start=start, stop=False)
                mm(out, wh, xl, start=False, stop=False)
                return mm(out, wl, xh, start=False, stop=stop)

            def split_unit(it, m, s, n, mj=4, h0=None):
                if n >= 4 or not isinstance(it, int):
                    pe.wait_ge(evac[n % 4], it * (mj // 4) + n // 4)
                for q in range(RING):
                    wait_low_part(pe, it, m, s, q)
                    for kk in range(QK):
                        k = q * QK + kk
                        if h0 is not None:
                            pe.wait_ge(ht_ready, h0 + k + 1)
                        last = products(bank(n)[:, 0:T], ckh(q)[:, kk * P:(kk + 1) * P], ckl(q)[:, kk * P:(kk + 1) * P],
                                        hh3[:, k, :], hl3[:, k, :], k == 0, k == KT - 1)
                    last.then_inc(quarter_done, 1)

            def dense(name, its, h0=None):
                with pe.Fori(0, its) as it:
                    for j in range(RING):
                        split_unit(it, 4, S0[name] + j, JOB[name] + j, h0=None if j else h0)

            norm(0)
            for j in range(RING):
                split_unit(0, 4, S0["A"] + j, JOB["A"] + j, h0=None if j else 0)
            with pe.Fori(1, 14) as it:
                for j in range(RING):
                    split_unit(it, 4, S0["A"] + j, JOB["A"] + j)

            n = JOB["small"]
            claim(pe, n)
            pe.wait_ge(ws_lo, 1)
            for k in range(KT):
                last = products(bank(n)[0:24, 0:T], sp_(WSH + k * 24, 24), sp_(WSL + k * 24, 24), hh3[:, k, :], hl3[:, k, :],
                                k == 0, k == KT - 1)
            last.then_inc(pe_job, 1)
            n = JOB["smallt"]
            claim(pe, n)
            wait_evac(pe, JOB["small"])
            for c, m in ((0, P), (1, P), (2, NS)):
                last = nc.tensor.transpose(bank(n)[0:m, c * 24:c * 24 + 24], at(SC + 4608 + c * P, m, 24), cst(C_ID, 24, 24))
            last.then_inc(pe_job, 1)

            def block_norm(name, count, c0, base=SC):
                n = JOB[name + "s"]
                claim(pe, n)
                for b in range(count):
                    pe.wait_ge(bsq_ready, c0 + b + 1)
                    last = mm(bank(n)[0:count, 0:T], cst(C_SEL + 15 - b, count), at(base + (b % 4) * T, T),
                              start=(b == 0), stop=(b == count - 1))
                    last.then_inc(pe_job if b == count - 1 else bsq_used, 1)
                for b in range(count):
                    n = JOB[name] + b
                    claim(pe, n)
                    if b == 0:
                        pe.wait_ge(brt_ready, (c0 + 15) // 16 + 1)
                    mm(bank(n)[:, 0:T], cst(C_ID + b, 1, count).broadcast_to([count, P]), at(base + 4 * T, T, count),
                       start=True, stop=True).then_inc(pe_job, 1)

            block_norm("fqk", 16, 0)
            block_norm("gqk", 16, 16)

            n = JOB["cum"]
            claim(pe, n)
            pe.wait_ge(gates_ready, 1)
            g2 = lgb[:, 0:2, 8:16]
            for q, lhs in enumerate((upi, low, ones)):
                last = mm(bank(n)[:, 16 * q:16 * q + 16].rearrange("p (c h) -> p c h", c=2), lhs, g2, start=True, stop=True)
            last.then_inc(pe_job, 1)

            n = JOB["bc"]
            claim(pe, n)
            pe.wait_ge(bcx_ready, 1)
            mm(bank(n)[:, 0:128], cst(C_ONE, P, NS), at(SC + 1200, 128, NS), start=True, stop=True)
            mm(bank(n)[:, 128:192], ones, at(SC + 1328, 64), start=True, stop=True)
            mm(bank(n)[:, 192:256], ones, at(SC + 1392, 64), start=True, stop=True).then_inc(pe_job, 1)

            for q in range(4):
                n = JOB["fvt"] + q
                claim(pe, n)
                for i in range(4):
                    last = nc.tensor.transpose(bank(n)[:, i * P:(i + 1) * P],
                                               pt3[:, 16 + 2 * q + i // 2, (i % 2) * P:(i % 2 + 1) * P], ident)
                last.then_inc(pe_job, 1)
            wait_evac(pe, JOB["fvt"] + 3)
            pe.wait_ge(bn_ready, 32)
            for h in range(NH):
                n = JOB["fs"] + h
                claim(pe, n)
                pe.wait_ge(lfl_ready, 3 * h + 3)
                lfl = lambda i: at(OT + (h % 2) * 384 + i * P, P)
                q, k = pt3[:, h, :], pt3[:, 8 + h, :]
                b = bank(n)
                mm(b[:, 0:P], q[:, 0:P], k[:, 0:P], start=True, stop=False)
                mm(b[:, 0:P], upi, lfl(0), start=False, stop=True)
                mm(b[:, P:2 * P], q[:, P:2 * P], k[:, 0:P], start=True, stop=False)
                mm(b[:, P:2 * P], ones, lfl(0), start=False, stop=False)
                mm(b[:, P:2 * P], upi, lfl(2), start=False, stop=True)
                mm(b[:, 2 * P:3 * P], q[:, P:2 * P], k[:, P:2 * P], start=True, stop=False)
                mm(b[:, 2 * P:3 * P], upi, lfl(1), start=False, stop=True).then_inc(pe_job, 1)
            for h in range(NH):
                n = JOB["fpt"] + h
                claim(pe, n)
                pe.wait_ge(prob_ready, 2 * h + 2)
                for i in range(3):
                    last = nc.tensor.transpose(bank(n)[:, i * P:(i + 1) * P], at(SC + h * 384 + i * P, P), ident)
                last.then_inc(pe_job, 1)
            vn = lambda h, c: at(OT + (8 + h) * T + c * P, P)
            for g in range(4):
                n = JOB["fo"] + g
                claim(pe, n)
                wait_evac(pe, JOB["fpt"] + 2 * g + 1)
                for i in range(2):
                    h = 2 * g + i
                    b = bank(n)[:, i * 256:i * 256 + 256]
                    pt_ = lambda c: at(SC + 3072 + h * 384 + c * P, P)
                    mm(b[:, 0:P], vn(h, 0), pt_(0), start=True, stop=True)
                    mm(b[:, P:2 * P], vn(h, 0), pt_(1), start=True, stop=False)
                    last = mm(b[:, P:2 * P], vn(h, 1), pt_(2), start=False, stop=True)
                last.then_inc(pe_job, 1)

            B1, B2, B3 = SC, SC + 2048, SC + 4096
            B4, B5, B6 = PT, PT + 2048, PT + 4096
            pair = lambda base, h, c: at(base + (2 * h + c) * P, P)
            wait_evac(pe, JOB["fo"] + 3)
            for h in range(NH):
                n = JOB["gdk"] + 2 * h
                claim(pe, n)
                pe.wait_ge(lfl_ready, 24 + 2 * h + 2)
                for c in range(2):
                    gl = at(OT + 8 * T + (h % 2) * 256 + c * P, P)
                    mm(bank(n)[:, c * P:(c + 1) * P], upi, gl, start=True, stop=True)
                    last = mm(bank(n)[:, (2 + c) * P:(3 + c) * P], gl, upi, start=True, stop=True)
                last.then_inc(pe_job, 1)
                n += 1
                claim(pe, n)
                for c in range(2):
                    k = pt3[:, 32 + h, c * P:(c + 1) * P]
                    q = pt3[:, 24 + h, c * P:(c + 1) * P]
                    mm(bank(n)[:, c * P:(c + 1) * P], k, k, start=True, stop=True)
                    last = mm(bank(n)[:, (2 + c) * P:(3 + c) * P], k, q, start=True, stop=True)
                last.then_inc(pe_job, 1)
            for g in range(4):
                n = JOB["gat"] + g
                claim(pe, n)
                pe.wait_ge(a_ready, 2 * g + 2)
                for i in range(4):
                    last = nc.tensor.transpose(bank(n)[:, i * P:(i + 1) * P], at(B1 + (4 * g + i) * P, P), ident)
                last.then_inc(pe_job, 1)
            inv = lambda lv, kind, g: JOB["inv"] + 12 * lv + (g if kind == 0 else 4 + 2 * g + kind - 1)
            pe.wait_ge(t_init, 2)
            for lv in range(LEVELS):
                for g in range(4):
                    n = inv(lv, 0, g)
                    claim(pe, n)
                    if lv == 0:
                        wait_evac(pe, JOB["gat"] + g)
                    else:
                        wait_evac(pe, inv(lv - 1, 1, g))
                    for i in range(4):
                        o = (4 * g + i) * P
                        last = mm(bank(n)[:, i * P:(i + 1) * P], at(B2 + o, P), at(B3 + o, P), start=True, stop=True)
                    last.then_inc(pe_job, 1)
                for g in range(4):
                    for kind in (1, 2):
                        n = inv(lv, kind, g)
                        claim(pe, n)
                        wait_evac(pe, inv(lv, 0, g))
                        if lv:
                            wait_evac(pe, inv(lv - 1, 2, g))
                        for i in range(4):
                            o = (4 * g + i) * P
                            lhs, rhs = (B4, B1) if kind == 1 else (B1, B4)
                            last = mm(bank(n)[:, i * P:(i + 1) * P], at(lhs + o, P), at(rhs + o, P), start=True, stop=True)
                        last.then_inc(pe_job, 1)
            for name, blk0 in (("gkt", 32), ("gvt", 40)):
                for g in range(4):
                    n = JOB[name] + g
                    claim(pe, n)
                    for i in range(4):
                        last = nc.tensor.transpose(bank(n)[:, i * P:(i + 1) * P],
                                                   pt3[:, blk0 + 2 * g + i // 2, (i % 2) * P:(i % 2 + 1) * P], ident)
                    last.then_inc(pe_job, 1)
            for g in range(4):
                n = JOB["gu"] + g
                claim(pe, n)
                wait_evac(pe, JOB["gvt"] + g)
                wait_evac(pe, inv(LEVELS - 1, 2, g))
                for i in range(4):
                    o = (4 * g + i) * P
                    last = mm(bank(n)[:, i * P:(i + 1) * P], at(B4 + o, P), at(B1 + o, P), start=True, stop=True)
                last.then_inc(pe_job, 1)
            for g in range(2):
                n = JOB["gw"] + g
                claim(pe, n)
                wait_evac(pe, JOB["gkt"] + 2 * g + 1)
                for i in range(4):
                    h = 4 * g + i
                    last = mm(bank(n)[:, i * P:(i + 1) * P], pair(B2, h, 1), pair(B4, h, 1), start=True, stop=True)
                last.then_inc(pe_job, 1)
            for g in range(2):
                n = JOB["gs1"] + g
                claim(pe, n)
                wait_evac(pe, JOB["gu"] + 2 * g + 1)
                for i in range(4):
                    h = 4 * g + i
                    last = mm(bank(n)[:, i * P:(i + 1) * P], pair(B3, h, 0), pair(B6, h, 0), start=True, stop=True)
                last.then_inc(pe_job, 1)
            for g in range(2):
                n = JOB["gq"] + g
                claim(pe, n)
                pe.wait_ge(gb_ready, 8)
                for i in range(4):
                    h = 4 * g + i
                    last = mm(bank(n)[:, i * P:(i + 1) * P], at(B2 + h * P, P), upi, start=True, stop=True)
                last.then_inc(pe_job, 1)
            for g in range(2):
                n = JOB["gws"] + g
                claim(pe, n)
                wait_evac(pe, JOB["gw"] + g)
                wait_evac(pe, JOB["gs1"] + g)
                for i in range(4):
                    h = 4 * g + i
                    last = mm(bank(n)[:, i * P:(i + 1) * P], at(B1 + h * P, P), at(B1 + 1024 + h * P, P), start=True, stop=True)
                last.then_inc(pe_job, 1)
            for g in range(4):
                n = JOB["go"] + g
                claim(pe, n)
                wait_evac(pe, JOB["gws"] + g // 2)
                pe.wait_ge(qe_ready, 2)
                for i in range(2):
                    h = 2 * g + i
                    b = bank(n)[:, i * 256:i * 256 + 256]
                    mm(b[:, 0:P], pair(B6, h, 0), pair(B5, h, 0), start=True, stop=True)
                    mm(b[:, P:2 * P], at(B1 + 1024 + h * P, P), pt3[:, 24 + h, P:2 * P], start=True, stop=False)
                    last = mm(b[:, P:2 * P], pair(B6, h, 1), pair(B5, h, 1), start=False, stop=True)
                last.then_inc(pe_job, 1)
            for g in range(2):
                n = JOB["gs2"] + g
                claim(pe, n)
                for i in range(4):
                    h = 4 * g + i
                    last = mm(bank(n)[:, i * P:(i + 1) * P], pair(B3, h, 1), pair(B6, h, 1), start=True, stop=True)
                last.then_inc(pe_job, 1)

            n = JOB["sg1"]
            claim(pe, n)
            for s in range(NS):
                pe.wait_ge(st_loaded[s], 16)
                for h in range(NH):
                    c = (s * NH + h) * 2
                    last = mm(bank(n)[:, c:c + 2], state_of(s)[:, h * P:(h + 1) * P],
                              pt3[:, 24 + h:33 + h:8, SEQ + s], start=True, stop=True)
            last.then_inc(pe_job, 1)
            for name, srcs in (("sgk", None), ("sgd", DEL)):
                for g in range(2):
                    n = JOB[name] + g
                    claim(pe, n)
                    if srcs is not None:
                        pe.wait_ge(del_ready, 1)
                    for i in range(4):
                        h = 4 * g + i
                        src = pt3[:, 32 + h, SEQ:T] if srcs is None else at(DEL + h * NS, NS)
                        last = nc.tensor.transpose(bank(n)[0:NS, i * P:(i + 1) * P], src, ident)
                    last.then_inc(pe_job, 1)
            for h in range(NH):
                for g in range(2):
                    n = JOB["sgo"] + 2 * h + g
                    claim(pe, n)
                    pe.wait_ge(dmn_ready, h + 1)
                    mm(bank(n), at(B1 + h * P, P, NS), at(B2 + (h % 2) * 1024 + g * 512, 512, NS),
                       start=True, stop=True).then_inc(pe_job, 1)
            n = JOB["slf"]
            claim(pe, n)
            pe.wait_ge(lf_in, 16 * NS * PAGES)
            for h in range(NH):
                last = nc.tensor.transpose(bank(n)[:, h * 64:(h + 1) * 64], at(LFR + h * P, P, 64), cst(C_ID, 64, 64))
            last.then_inc(pe_job, 1)
            n = JOB["sown"]
            claim(pe, n)
            pe.wait_ge(own_ready, 1)
            mm(bank(n)[0:64, 0:1], at(PSF, 64), cst(C_ONE, 1), start=True, stop=True).then_inc(pe_job, 1)
            block_norm("gn", 8, 32, PT)

            score = ps[0:64, 4:6, :].rearrange("p b (j c) -> p (b j) c", c=P)
            for b in range(2):
                mm(ps[0:64, 4 + b, :].rearrange("p (j c) -> p j c", c=P), at(DEL, 64, NS),
                   cst(C_ONE, P, NS).unsqueeze(1).broadcast_to([NS, 4, P]), start=True, stop=True, skip_group_check=True)

            def k_pages(s, some):
                if s == 0:
                    pe.wait_ge(qm_ready, 1)
                for j in some:
                    pe.wait_ge(pg_loaded[j], s * 16 + 16)
                    for h in range(NH):
                        last = mm(score[:, j, :], at(QM + (s * NH + h) * 64, 64), page(j)[:, h * P:(h + 1) * P],
                                  start=False, stop=False, skip_group_check=True)
                    last.then_inc(page_done, 1)

            def v_pages(s, some):
                b = 4 + 2 * (s % 2)
                if s >= 2:
                    pe.wait_ge(on_ready, s - 1)
                for j in some:
                    pe.wait_ge(pg_loaded[j], s * 16 + 144)
                    for i in range(2):
                        last = mm(ps[0:NS, b + i, :], at(PRT + j * 64 + s * NH, NH), page(j)[:, i * 512:(i + 1) * 512],
                                  start=(j == 0), stop=(j == PAGES - 1))
                    last.then_inc(page_done, 1)

            for it in range(4):
                for j in range(4):
                    split_unit(it, 4, S0["gates"] + 0 + j, JOB["gates0"] + j)
                    k_pages(it * 2 + j // 2, range(4 * (j % 2), 4 * (j % 2) + 4))
            pe.wait_ge(lfs_ready, 1)
            for j in range(PAGES):
                mm(score[:, j, :], at(LF + j * 64, 64), low, start=False, stop=False, skip_group_check=True)
                last = mm(score[:, j, :], at(LFS + j * 64, 64), ones, start=False, stop=(j % 4 == 3), skip_group_check=True)
            last.then_inc(score_ready, 1)
            n = JOB["spt"]
            claim(pe, n)
            pe.wait_ge(sp_ready, 1)
            for j in range(PAGES):
                last = nc.tensor.transpose(bank(n)[:, j * 64:(j + 1) * 64], at(PROB + j * P, P, 64), cst(C_ID, 64, 64))
            last.then_inc(pe_job, 1)
            n = JOB["spb"]
            claim(pe, n)
            pe.wait_ge(dg_ready, 1)
            mm(bank(n)[:, 0:64], cst(C_ONE, P, 64), at(OWN + 64, 64, 64), start=True, stop=True).then_inc(pe_job, 1)
            wait_evac(pe, JOB["spt"])
            for it in range(4):
                for j in range(4):
                    split_unit(it, 4, S0["gates"] + 16 + j, JOB["gates1"] + j)
                    v_pages(it * 2 + j // 2, range(4 * (j % 2), 4 * (j % 2) + 4))

            n = JOB["sot"]
            claim(pe, n)
            pe.wait_ge(on_ready, NS)
            for s in range(NS):
                last = nc.tensor.transpose(bank(n)[:, s * NH:(s + 1) * NH], at(ON + s * P, P, NH), cst(C_ID, NH, NH))
            last.then_inc(pe_job, 1)

            pe.wait_ge(of_ready, 1)
            with pe.Fori(0, 4) as it:
                for j in range(RING):
                    n = JOB["up"] + j
                    pe.wait_ge(w_loaded[j], it * 16 + 16 * (S0["up"] // 4 + 1))
                    pe.wait_ge(evac[n % 4], it + n // 4)
                    for half in range(2):
                        for k in range(NH):
                            last = mm(ps[:, n % 4 + 4 * half, 0:T], wr(j)[:, (half * NH + k) * P:(half * NH + k + 1) * P],
                                      ot3[:, half * NH + k, :], start=(k == 0), stop=(k == NH - 1))
                    last.then_inc(pe_job, 1)
            pe.wait_ge(mt_ready, 1)
            dense("out", 4)
            norm(1)
            dense("wq", 4, 16)

            pe.wait_ge(sk_in, 16)
            wait_evac(pe, JOB["wq"] + 15)
            def key_scores(c):
                if c == 2:
                    n, = RS_JOBS[2]
                    claim(pe, n)
                    pe.wait_ge(qz_ready, 2)
                    for p_ in range(2):
                        for h in range(NH):
                            hp = 2 * h + p_
                            last = mm(bank(n)[0:64, p_ * P:(p_ + 1) * P], at(QZ + hp * 64, 64), at(SK + hp * P, P),
                                      start=(h == 0), stop=(h == NH - 1))
                    last.then_inc(pe_job, 1)
                    return
                for g, n in enumerate(RS_JOBS[c]):
                    claim(pe, n)
                    for i in range(4):
                        hp = 4 * g + i
                        last = mm(bank(n)[:, i * P:(i + 1) * P], at(QT + hp * T + c * P, P), at(SK + hp * P, P),
                                  start=True, stop=True)
                    last.then_inc(pe_job, 1)

            def turn_results(c):
                n = IDX_JOB[c]
                claim(pe, n)
                pe.wait_ge(res_ready, c + 1)
                for i in range(3):
                    if c == 2:
                        last = mm(bank(n)[:, i * P:i * P + NS], at(LX + i * P, P, 64), at(ROW_T, NS, 64), start=True, stop=True)
                    else:
                        last = nc.tensor.transpose(bank(n)[:, i * P:(i + 1) * P], at(RES + i * P, P), ident)
                last.then_inc(pe_job, 1)

            key_scores(0)
            key_scores(1)
            turn_results(0)
            key_scores(2)
            turn_results(1)
            turn_results(2)

            for half in range(2):
                wb, ub = JOB[f"wb{half}"], JOB[f"u{half}"]

                def weights_of(it, j):
                    pe.wait_ge(oha_ready, it * 4 + (33 * half + j + 1))
                    pe.wait_ge(ohb_ready, it * 4 + (33 * half + j + 1))
                    for n in (wb + 2 * j, wb + 2 * j + 1):
                        pe.wait_ge(evac[n % 4], it * 2 + n // 4)
                        for i in range(4):
                            t = 4 * (n - wb - 2 * j) + i
                            oha = at(OHA + (j % 2) * 8 * HALF + t * HALF, HALF)
                            last = mm(bank(n)[:, i * P:(i + 1) * P].rearrange("p (r a) -> p r a", a=HALF),
                                      at(OHB + (j % 2) * 8 * P + t * P, P),
                                      oha.unsqueeze(1).broadcast_to([P, 2, HALF]), start=True, stop=True)
                        last.then_inc(pe_job, 1)

                with pe.Fori(0, 8) as it:
                    for j in range(4):
                        weights_of(it, j)
                weights_of(8, 0)

                s0 = S0[f"peer{half}"]

                def scores(it, m, s, n):
                    for j in range(RING):
                        split_unit(it, m, s + j, n + j, m // 2)

                def outputs(it, m, s, g, buf):
                    for dq in range(RING):
                        for q in range(RING):
                            if dq == 0 and q == 0:
                                pe.wait_ge(a_blk, it * (m // 2) + (4 * (16 * half + g) + 4))
                            pe.wait_ge(y_added, it * (2 * m) + (16 * (16 * half + g) + 4 * dq + q + 1))
                            wait_low_part(pe, it, m, s + dq, q)
                            for j in range(EG):
                                a = (buf * EG + j) * T
                                last = products(ps[:, 4 + q, 0:T], ckh(q)[:, j * P:(j + 1) * P],
                                                ckl(q)[:, j * P:(j + 1) * P], sp_(AH + a, T), sp_(AL + a, T),
                                                j == 0, j == EG - 1)
                            last.then_inc(quarter_done, 1)

                scores(0, 0, s0, ub)
                with pe.Fori(0, 7) as i2:
                    for b in range(2):
                        scores(i2, 16, s0 + 4 + 8 * b, ub + 4 + 4 * b)
                        outputs(i2, 16, s0 + 8 + 8 * b, b, b)
                scores(0, 0, s0 + 116, ub + 60)
                outputs(0, 0, s0 + 120, 14, 0)
                outputs(0, 0, s0 + 124, 15, 1)

            norm(2)
            pe.wait_ge(ple_in, 32)
            for b in range(16):
                if b >= 4:
                    pe.wait_ge(fin_ready, b - 3)
                for k in range(PLE_KT):
                    last = mm(ps[:, 4 + b % 4, 0:T], at(WPL + k * D_MODEL + b * P, P), at(PTI + k * T, T),
                              start=(k == 0), stop=(k == PLE_KT - 1))
                last.then_inc(pw_done, 1)
                split_unit(b // 4, 4, S0["ple"] + b % 4, JOB["ple"] + b % 4, h0=None if b else 32)

        @block.scalar
        def _(act):
            A = nc.scalar.activation

            def norm(r):
                if r == 0:
                    act.wait_ge(x_in, 16)
                else:
                    act.wait_ge((x1_ready, x2_ready)[r - 1], 1)
                for i in range(4):
                    A(at(SQ + 4 * i * T, 4 * T), at(XT + 4 * i * T, 4 * T), ACT.Square).then_inc(sq_ready, 1)
                n = JOB[f"norm{r}"]
                wait_done(act, n)
                if r == 0:
                    act.wait_ge(c_in, 16)
                A(at(SC + 4608, T), bank(n)[:, 0:T], ACT.Sqrt, bias=eps, scale=1.0 / D_MODEL).then_inc(evac[n % 4], 1)
                for k in range(KT):
                    act.wait_ge(hraw_ready, 16 * r + k + 1)
                    A(hh3[:, k, :], blk(HRAW, k), ACT.Copy).then_inc(hh_ready, 1)

            def each_block(name, its, func, base, s0=None, b0=0, n0=0, first=True, final=True,
                           before=None, also=None):
                s0 = (S0[name] if s0 is None else s0) + n0

                def read_out(it, j):
                    n = JOB[name] + n0 + j
                    if before is not None:
                        before(it, j)
                    wait_quarter(act, it, 4, s0 + j, RING - 1)
                    dst = base + (b0 + n0 + j) * T
                    dst = at(dst + it * 4 * T, T) if isinstance(it, int) else arena[:, bass.ds(it * (4 * T) + dst, T)]
                    A(dst, bank(n)[:, 0:T], func).then_inc(evac[n % 4], 1)
                    if also is not None:
                        also(it, j)
                dense_steps(act, s0, its, high_part, read_out, first, final)

            norm(0)
            act.wait_ge(ws_in, 16)
            A(sp_(WSH, 384), at(SC + 4224, 384), ACT.Copy).then_inc(ws_hi, 1)
            each_block("A", 6, ACT.Copy, PT, final=False)

            def silu(it, j):
                dst = PT + (24 + j - 1) * T
                dst = at(dst + it * 4 * T, SEQ) if isinstance(it, int) else arena[:, bass.ds(it * (4 * T) + dst, SEQ)]
                A(dst, at(CACC + ((j + 1) % 2) * SEQ, SEQ), ACT.Silu).then_inc(conv_out, 1)

            def summed(it, j):
                if j:
                    act.wait_ge(conv_acc, it * 4 + j)

            each_block("A", 1, ACT.Copy, PT, n0=24, first=False, final=False, before=summed,
                       also=lambda it, j: j and silu(it, j))
            each_block("A", 5, ACT.Copy, PT, n0=28, first=False, final=False, before=lambda it, j: summed(it, j + 4),
                       also=lambda it, j: silu(it, j + 4))
            summed(0, 24)
            silu(0, 24)
            each_block("A", 2, ACT.Copy, PT, n0=48, first=False)

            act.wait_ge(p_in, 16)
            n = JOB["small"]
            wait_done(act, n)
            A(at(SC + 4608, T, 24), bank(n)[0:24, 0:T], ACT.Copy).then_inc(evac[n % 4], 1)
            A(at(ALE, 8), par(G_ALOG, 8), ACT.Exp).then_inc(sm_e, 1)
            act.wait_ge(sm_u, 1)
            A(at(SMY, 72), at(SMU, 72), ACT.Exp, scale=-1.0).then_inc(sm_e, 1)

            def block_norm(name, count, c0, src, col, base=SC):
                used = c0 - c0 // 16
                for b in range(count):
                    if b >= 4:
                        act.wait_ge(bsq_used, used + b - 3)
                    A(at(base + (b % 4) * T, T), src(b), ACT.Square).then_inc(bsq_ready, 1)
                n = JOB[name + "s"]
                wait_done(act, n)
                A(at(base + 4 * T, T, count), bank(n)[0:count, 0:T], ACT.Sqrt, bias=cst(col + 1, 1, count),
                  scale=cst(col, 1, count)).then_inc(evac[n % 4], 1)

            block_norm("fqk", 16, 0, lambda b: blk(PT, b), C_RT)
            act.wait_ge(convs_ready, 1)
            A(pt3[:, 24:48, SEQ:T], at(CSAMP, 192).rearrange("p (b s) -> p b s", s=NS), ACT.Silu).then_inc(conv_out, 1)
            A(at(PT + 48 * T, 8 * T), at(PT + 48 * T, 8 * T), ACT.Silu).then_inc(conv_out, 1)
            act.wait_ge(conv_out, 26)
            block_norm("gqk", 16, 16, lambda b: blk(PT, 24 + b), C_RT + 2)

            n = JOB["cum"]
            wait_done(act, n)
            A(at(EXS, 48), bank(n)[:, 0:48], ACT.Exp).then_inc(evac[n % 4], 1)

            wait_evac(act, JOB["bc"])
            A(at(BCS, 64), at(BCS, 64), ACT.Exp).then_inc(eg_ready, 1)

            for h in range(NH):
                act.wait_ge(neg_ready, h + 1)
                s = at(SC + h * 384, 384)
                A(s[:, 0:P], s[:, 0:P], ACT.Exp, bias=at(NEGM + 2 * h, 1), accum_out=at(SUMS + 2 * h, 1)).then_inc(prob_raw, 1)
                A(s[:, P:384], s[:, P:384], ACT.Exp, bias=at(NEGM + 2 * h + 1, 1),
                  accum_out=at(SUMS + 2 * h + 1, 1)).then_inc(prob_raw, 1)
            for h in range(NH):
                n = JOB["fpt"] + h
                wait_done(act, n)
                A(at(SC + 3072 + h * 384, 384), bank(n)[:, 0:384], ACT.Copy).then_inc(evac[n % 4], 1)
            for g in range(4):
                n = JOB["fo"] + g
                wait_done(act, n)
                A(ot3[:, 2 * g:2 * g + 2, 0:SEQ], bank(n).rearrange("p (h t) -> p h t", h=2), ACT.Copy).then_inc(evac[n % 4], 1)

            act.wait_ge(kv_saved, 32)
            act.wait_ge(qs_copied, 3)
            B1, B2, B3 = SC, SC + 2048, SC + 4096
            B4, B5, B6 = PT, PT + 2048, PT + 4096
            for h in range(NH):
                n = JOB["gdk"] + 2 * h
                wait_done(act, n)
                if h >= 2:
                    wait_evac(act, n - 3)
                A(at(B6 + (h % 2) * 512, 512), bank(n), ACT.Exp).then_inc(evac[n % 4], 1)
            for g in range(4):
                n = JOB["gat"] + g
                wait_done(act, n)
                A(at(B2 + g * 512, 512), bank(n), ACT.Copy).then_inc(evac[n % 4], 1)
            for name, dst in (("gu", B6), ("gw", B1), ("gs1", B1 + 1024)):
                for g in range(4 if name == "gu" else 2):
                    n = JOB[name] + g
                    wait_done(act, n)
                    if name == "gw" and g == 0:
                        wait_done(act, JOB["gu"] + 3)
                    A(at(dst + g * 512, 512), bank(n), ACT.Copy).then_inc(evac[n % 4], 1)
            for g in range(2):
                n = JOB["gq"] + g
                wait_done(act, n)
                A(at(B2 + 1024 + g * 512, 512), bank(n), ACT.Exp).then_inc(evac[n % 4], 1)
            for g in range(4):
                n = JOB["go"] + g
                wait_done(act, n)
                A(ot3[:, NH + 2 * g:NH + 2 * g + 2, 0:SEQ], bank(n).rearrange("p (h t) -> p h t", h=2), ACT.Copy).then_inc(evac[n % 4], 1)
            for name, dst in (("sgk", B1), ("sgd", B5)):
                for g in range(2):
                    n = JOB[name] + g
                    wait_done(act, n)
                    A(at(dst + g * 512, 512, NS), bank(n)[0:NS, :], ACT.Copy).then_inc(evac[n % 4], 1)
            act.wait_ge(st_ready, 64)
            for s in range(NS):
                act.dma_start(o_ss[s], state_of(s)).then_inc(state_saved[s // 2], 16)
            act.wait_ge(og_ready, 1)
            act.wait_ge(sp_saved, 16)
            block_norm("gn", 8, 32, lambda b: blk(OT, NH + b), C_RT + 4, PT)

            each_block("gates0", 4, ACT.Sigmoid, GT, S0["gates"])
            act.wait_ge(sp_in, 1)
            own = lambda c, w=1: at(OWN + c, w, 64)
            for b in range(2):
                A(at(PROB + b * 512, 512, 64), ps[0:64, 4 + b, :], ACT.Exp, bias=own(3), accum_out=own(4 + b)).then_inc(sp_exp, 1)
            A(own(6), own(0), ACT.Exp, bias=own(3)).then_inc(sp_exp, 1)
            each_block("gates1", 4, ACT.Sigmoid, GT, S0["gates"] + 16, 16)

            with act.Fori(0, 4) as it:
                for j in range(RING):
                    act.wait_ge(merged, it * 4 + (j + 1))
                    A(split[:, bass.ds(it * (4 * T) + (HH + j * T), T)], at(TMU + (j % 2) * 2 * T, T), ACT.Copy).then_inc(mh_ready, 1)

            def high_only(name):
                dense_steps(act, S0[name], 4, high_part, lambda it, j: None)
            high_only("out")

            norm(1)
            each_block("wq", 4, ACT.Copy, QT)
            for c in range(3):
                m, heads = ROUTE_TILES[c]
                for g, n in enumerate(RS_JOBS[c]):
                    wait_done(act, n)
                    if c and g == 0:
                        act.wait_ge(res_ready, c)
                    w = min(512, 2 * heads * P)
                    A(at(RS + 512 * g, w, m), bank(n)[0:m, 0:w], ACT.Copy).then_inc(evac[n % 4], 1)
                act.wait_ge(re_in, c + 1)
                A(at(RES + 2 * P, 16 * heads, m), at(RES + 2 * P, 16 * heads, m), ACT.Exp).then_inc(re_exp, 1)

            wh3 = at(WH, HALF * T).rearrange("p (a t) -> p t a", t=T)
            for half in range(2):
                wb, ub = JOB[f"wb{half}"], JOB[f"u{half}"]
                if half:
                    act.wait_ge(a_blk, 64)
                else:
                    wait_evac(act, IDX_JOB[2])

                def weights_of(it, j):
                    for n in (wb + 2 * j, wb + 2 * j + 1):
                        act.wait_ge(pe_job, it * 8 + PJ[n])
                        A(wh3[:, bass.ds(it * 32 + 4 * (n - wb), 4), :],
                          bank(n).rearrange("p (t r a) -> p t r a", t=4, r=2)[:, :, 0, :], ACT.Copy).then_inc(evac[n % 4], 1)

                with act.Fori(0, 8) as it:
                    for j in range(4):
                        weights_of(it, j)
                weights_of(8, 0)

                s0 = S0[f"peer{half}"]

                def gelus(it, m, s, n, g):
                    for j in range(RING):
                        for q in range(RING):
                            high_part(act, it, m, s + j + 1, q)
                        wait_quarter(act, it, m, s + j, RING - 1)
                        if half or g or j >= 2:
                            act.wait_ge(a_blk, it * (m // 2) + (4 * (16 * half + g) + j - 1))
                        A(at(AB + (j % 2) * T, T), bank(n + j)[:, 0:T], ACT.Gelu).then_inc(evac[(n + j) % 4], 1)

                def values(it, m, s, last=False):
                    for j in range(RING):
                        for q in range(RING):
                            if not (last and j == RING - 1):
                                high_part(act, it, m, s + j + 1, q)

                for q in range(RING):
                    high_part(act, 0, 0, s0, q)
                gelus(0, 0, s0, ub, 0)
                with act.Fori(0, 7) as i2:
                    for b in range(2):
                        gelus(i2, 16, s0 + 4 + 8 * b, ub + 4 + 4 * b, b + 1)
                        values(i2, 16, s0 + 8 + 8 * b)
                gelus(0, 0, s0 + 116, ub + 60, 15)
                values(0, 0, s0 + 120)
                values(0, 0, s0 + 124, True)

            norm(2)
            each_block("ple", 4, ACT.Sigmoid, GPL)

        @block.gpsimd
        def _(pool):
            pool.wait_ge(ht_ready, 16)
            pool.dma_start(at(CST_ST, 576), convst).then_inc(cs_in, 16)
            wait_slot(pool, 0, 0, S0["gates"] - 1)
            for s in range(NS):
                pool.dma_start(state_of(s), state[s]).then_inc(st_loaded[s], 16)

            pool.wait_ge(bn_ready, 16)
            pool.dma_start(o_k, at(PT + 8 * T, 8 * T)).then_inc(kv_saved, 16)
            pool.dma_start(o_v, at(PT + 16 * T, 8 * T)).then_inc(kv_saved, 16)
            pool.wait_ge(gates_ready, 1)
            pool.dma_start(o_lf, lgb[:, :, 0:8]).then_inc(lf_saved, 16)
            pool.wait_ge(conv_copied, 1)
            pool.dma_start(o_cs, at(CCOPY, 24 * 27)).then_inc(cs_saved, 16)
            pool.wait_ge(gates_ready, 1)
            wait_evac(pool, JOB["A"] + 55)
            for h in range(NH):
                if h >= 2:
                    wait_done(pool, JOB["fs"] + h - 2)
                for i, (c, m) in enumerate(((0, low), (1, low), (1, ones))):
                    nc.gpsimd.tensor_scalar(at(OT + (h % 2) * 384 + i * P, P), m, lgb[:, c, h:h + 1], 1.0,
                                            ALU.mult, ALU.mult).then_inc(lfl_ready, 1)
            pool.wait_ge(kv_saved, 32)
            pool.wait_ge(qs_copied, 3)
            wait_done(pool, JOB["fo"] + 3)
            for h in range(NH):
                if h >= 2:
                    wait_done(pool, JOB["gdk"] + 2 * h - 4)
                for c in range(2):
                    nc.gpsimd.tensor_scalar(at(OT + 8 * T + (h % 2) * 256 + c * P, P), low, lgb[:, c, 8 + h:9 + h], 1.0,
                                            ALU.mult, ALU.mult).then_inc(lfl_ready, 1)
            B2, B3, B4 = SC + 2048, SC + 4096, PT
            for base in (B3, B4):
                nc.gpsimd.tensor_copy(at(base, 2048).rearrange("p (a b) -> p a b", b=P),
                                      ident.unsqueeze(1).broadcast_to([P, 16, P])).then_inc(t_init, 1)
            wait_done(pool, JOB["gw"] + 1)
            for h in range(NH):
                nc.gpsimd.tensor_scalar(at(B2 + h * P, P), ones, lgb[:, 1, 8 + h:9 + h], 1.0,
                                        ALU.mult, ALU.mult).then_inc(gb_ready, 1)
            pool.wait_ge(s2_ready, 8)
            pool.dma_start(o_sp, at(SC + 1024, 1024)).then_inc(sp_saved, 16)

            pool.wait_ge(st_ready, 64)
            pool.wait_ge(sp_saved, 16)
            nc.gpsimd.memset(at(QM, 4096), 0.0).then_inc(qm_zero, 1)
            pool.wait_ge(pt_in, 16)
            for part in range(2):
                load_pages(pool, part, 0, 1)
                with pool.Fori(1, 8) as s:
                    load_pages(pool, part, s, 1)

            pool.wait_ge(of_ready, 1)
            pool.dma_start(at(XT, KT * T), xT).then_inc(x_again, 16)

            for half in range(2):
                def gate_rows(it, j):
                    pool.wait_ge(oh_step, it * 4 + (33 * half + j + 1))
                    oh = at(OHA + (j % 2) * 8 * HALF, 8 * HALF).rearrange("p (t a) -> p t a", a=HALF)
                    gate = arena[:, bass.ds(it * 32 + (IDX + 2 * T + 8 * j), 8)].unsqueeze(2).broadcast_to([P, 8, HALF])
                    nc.gpsimd.tensor_tensor(oh, oh, gate, ALU.mult).then_inc(oha_ready, 1)

                with pool.Fori(0, 8) as it:
                    for j in range(4):
                        gate_rows(it, j)
                gate_rows(8, 0)

            pool.wait_ge(y_added, 516)
            pool.dma_start(at(WPL, PLE_KT * D_MODEL), wple).then_inc(ple_in, 16)
            pool.dma_start(at(PTI, PLE_KT * T), pT).then_inc(ple_in, 16)

        @block.vector
        def _(dve):
            V = nc.vector
            ch = Chain(dve, dch)

            def norm(r, gain):
                n = JOB[f"norm{r}"]
                wait_evac(dve, n)
                rt = at(SC + 4608, T)
                ch(V.reciprocal(rt, rt))
                if r == 0:
                    dve.wait_ge(p_in, 16)
                for k in range(KT + 2):
                    if k < KT:
                        V.scalar_tensor_tensor(out=blk(HRAW, k), in0=xt3[:, k, :], scalar=par(gain + k), in1=rt,
                                               op0=ALU.mult, op1=ALU.mult).then_inc(hraw_ready, 1)
                    if k >= 2:
                        dve.wait_ge(hh_ready, 16 * r + k - 1)
                        V.tensor_tensor(hl3[:, k - 2, :], blk(HRAW, k - 2), as_f32(hh3[:, k - 2, :]),
                                        ALU.subtract).then_inc(ht_ready, 1)

            def low_parts(name, its=4, s0=None):
                dense_steps(dve, S0[name] if s0 is None else s0, its, low_part, lambda it, j: None)

            for b in range(4):
                dve.sem_inc(y_added, 1)
            norm(0, G_MIX)
            dve.wait_ge(ws_hi, 1)
            V.tensor_tensor(sp_(WSL, 384), at(SC + 4224, 384), as_f32(sp_(WSH, 384)), ALU.subtract).then_inc(ws_lo, 1)
            dense_steps(dve, S0["A"], 6, low_part, lambda it, j: None, True, False)

            cp3 = at(CCOPY, 24 * 27).rearrange("p (b c) -> p b c", c=27)

            def conv(it, j):
                n = JOB["A"] + 24 + j
                dyn = lambda a, w, m: at(a + it * m, w) if isinstance(it, int) else arena[:, bass.ds(it * m + a, w)]
                dve.wait_ge(evac[n % 4], it + (n // 4 + 1))
                if j >= 2 or not isinstance(it, int):
                    dve.wait_ge(conv_out, it * 4 + (j - 1))
                a0 = CACC + (j % 2) * SEQ
                x = dyn(PT + (24 + j) * T, SEQ, 4 * T)
                w = lambda i: dyn(PAR + G_CONV + 24 * i + j, 1, 4)
                V.tensor_copy(dyn(CCOPY + 27 * j, 3, 4 * 27), dyn(PT + (24 + j) * T + SEQ - 3, 3, 4 * T))
                V.tensor_scalar(at(a0, SEQ), x, w(3), None, ALU.mult).then_inc(conv_step, 1)
                for i in (2, 1, 0):
                    d = 3 - i
                    dve.wait_ge(conv_step, it * 12 + (3 * j + d))
                    V.scalar_tensor_tensor(out=at(a0 + d, SEQ - d), in0=dyn(PT + (24 + j) * T, SEQ - d, 4 * T), scalar=w(i),
                                           in1=at(a0 + d, SEQ - d), op0=ALU.mult,
                                           op1=ALU.add).then_inc(conv_step if i else conv_acc, 1)

            for k in range(4):
                for q in range(RING):
                    low_part(dve, 0, 0, S0["A"] + 25 + k, q)
                conv(0, k)
            with dve.Fori(1, 6) as it:
                for j in range(4):
                    for q in range(RING):
                        low_part(dve, it, 4, S0["A"] + 25 + j, q)
                    conv(it, j)
            dense_steps(dve, S0["A"] + 48, 2, low_part, lambda it, j: None, False)

            smx = at(SMX, 72).rearrange("p (c k) -> p c k", c=3)
            smu = at(SMU, 72).rearrange("p (c k) -> p c k", c=3)
            dve.wait_ge(ws_in, 16)
            wait_done(dve, JOB["smallt"])
            ch(V.memset(at(SMX, 72), 0.0))
            bias = par(G_BIAS, 24)
            b3 = bank(JOB["smallt"])[:, 0:72].rearrange("p (c k) -> p c k", c=3)
            ch(V.tensor_tensor(smx[:, 0:2, :], b3[:, 0:2, :], bias.unsqueeze(1).broadcast_to([P, 2, 24]), ALU.add))
            V.tensor_tensor(smx[0:NS, 2, :], b3[0:NS, 2, :], par(G_BIAS, 24, NS), ALU.add).then_inc(evac[JOB["smallt"] % 4], 1)
            wait_evac(dve, JOB["smallt"])
            ch(V.tensor_scalar(smx[:, :, 0:8], smx[:, :, 0:8], -1.0, None, ALU.mult))
            ch(V.scalar_tensor_tensor(out=smu[:, :, 0:16], in0=smx[:, :, 0:16], scalar=-1.0, in1=smx[:, :, 0:16],
                                      op0=ALU.mult, op1=ALU.max))
            V.tensor_copy(smu[:, :, 16:24], smx[:, :, 16:24]).then_inc(sm_u, 1)
            dve.wait_ge(sm_e, 2)
            y, z, z2, pl = at(SMY, 72), at(SMZ, 72), at(SMZ2, 72), at(SMP, 72)
            ch(V.tensor_scalar(z, y, 2.0, None, ALU.add))
            ch(V.reciprocal(z, z))
            ch(V.tensor_tensor(z, z, y, ALU.mult))
            ch(V.tensor_tensor(z2, z, z, ALU.mult))
            ch(V.tensor_scalar(pl, z2, 1.0 / 21, None, ALU.mult))
            for k in (19, 17, 15, 13, 11, 9, 7, 5, 3):
                ch(V.scalar_tensor_tensor(out=pl, in0=pl, scalar=1.0 / k, in1=z2, op0=ALU.add, op1=ALU.mult))
            ch(V.scalar_tensor_tensor(out=pl, in0=pl, scalar=1.0, in1=z, op0=ALU.add, op1=ALU.mult))
            ch(V.tensor_scalar(at(SMX, 72), at(SMX, 72), 0.0, None, ALU.max))
            ch(V.scalar_tensor_tensor(out=pl, in0=pl, scalar=2.0, in1=at(SMX, 72), op0=ALU.mult, op1=ALU.add))
            pl3 = pl.rearrange("p (c k) -> p c k", c=3)
            y3 = y.rearrange("p (c k) -> p c k", c=3)
            V.tensor_scalar(lgb[:, :, 0:8], pl3[:, :, 0:8], -1.0, None, ALU.mult).then_inc(dch, 1)
            ch.n += 1
            ch(V.scalar_tensor_tensor(out=lgb[:, :, 8:16], in0=pl3[:, :, 8:16], scalar=-1.0,
                                      in1=at(ALE, 8).unsqueeze(1).broadcast_to([P, 3, 8]), op0=ALU.mult, op1=ALU.mult))
            ch(V.tensor_scalar(y3[:, :, 16:24], y3[:, :, 16:24], 1.0, None, ALU.add))
            V.reciprocal(lgb[:, :, 16:24], y3[:, :, 16:24]).then_inc(gates_ready, 1)

            def block_norm(name, count, c0, src, factor, extra=None, base=SC):
                wait_evac(dve, JOB[name + "s"])
                rt = at(base + 4 * T, T, count)
                V.reciprocal(rt, rt).then_inc(brt_ready, 1)
                for b in range(count):
                    n = JOB[name] + b
                    wait_done(dve, n)
                    x = src(b)
                    ins = V.scalar_tensor_tensor(out=x, in0=x, scalar=factor(b), in1=bank(n)[:, 0:T], op0=ALU.mult,
                                                 op1=ALU.mult)
                    if extra is None:
                        ins.then_inc(evac[n % 4], 1)
                    else:
                        ch(ins)
                        V.tensor_tensor(x, x, extra(b), ALU.mult).then_inc(evac[n % 4], 1)
                for b in range(count - 4, count):
                    wait_evac(dve, JOB[name] + b)
                dve.sem_inc(bn_ready, count)

            block_norm("fqk", 16, 0, lambda b: blk(PT, b), lambda b: par(G_FQ if b < 8 else G_FK))
            dve.wait_ge(bn_ready, 16)
            for dst, b0 in ((QS, 0), (KS, 8), (VS, 16)):
                V.tensor_copy(at(dst, 64).rearrange("p (h s) -> p h s", s=NS), pt3[:, b0:b0 + 8, SEQ:T]).then_inc(qs_copied, 1)

            dve.wait_ge(cs_in, 16)
            st4 = at(CST_ST, 576).rearrange("p (b s j) -> p b s j", s=NS, j=3)
            cps = cp3[:, :, 3:27].rearrange("p b (s j) -> p b s j", j=3)
            wj = lambda j: par(G_CONV + 24 * j, 24).unsqueeze(2).broadcast_to([P, 24, NS])
            c24 = lambda a: at(a, 192).rearrange("p (b s) -> p b s", s=NS)
            V.tensor_copy(cps[:, :, :, 0:2], st4[:, :, :, 1:3])
            V.tensor_copy(cps[:, :, :, 2], pt3[:, 24:48, SEQ:T]).then_inc(conv_copied, 1)
            ch(V.tensor_tensor(c24(CSAMP), pt3[:, 24:48, SEQ:T], wj(3), ALU.mult))
            for j in range(3):
                ch(V.tensor_tensor(c24(CPROD), st4[:, :, :, j], wj(j), ALU.mult))
                ch(V.tensor_tensor(c24(CSAMP), c24(CSAMP), c24(CPROD), ALU.add))
            dve.sem_inc(convs_ready, 1)
            block_norm("gqk", 16, 16, lambda b: blk(PT, 24 + b), lambda b: 1.0)
            dve.wait_ge(bn_ready, 32)

            wait_evac(dve, JOB["cum"])
            ch(V.tensor_tensor(at(BEG, 16).rearrange("p (c h) -> p c h", c=2), lgb[:, 0:2, 16:24],
                               at(EXS, 16).rearrange("p (c h) -> p c h", c=2), ALU.mult))
            eyeb = cst(C_ID, NS, NS).unsqueeze(2).broadcast_to([NS, NS, NH])
            x3 = lambda a: at(a, 64, NS).rearrange("p (s h) -> p s h", h=NH)
            V.tensor_tensor(x3(SC + 1200), lgb[0:NS, 2, 8:16].unsqueeze(1).broadcast_to([NS, NS, NH]), eyeb, ALU.mult)
            V.tensor_tensor(x3(SC + 1264), lgb[0:NS, 2, 16:24].unsqueeze(1).broadcast_to([NS, NS, NH]), eyeb, ALU.mult)
            sh = lambda a: at(a, 64).rearrange("p (s h) -> p h s", h=NH)
            hs = lambda a: at(a, 64).rearrange("p (h s) -> p h s", s=NS)
            dve.wait_ge(qs_copied, 3)
            V.tensor_tensor(sh(SC + 1328), hs(QS), hs(KS), ALU.mult)
            V.tensor_tensor(sh(SC + 1392), pt3[:, 24:32, SEQ:T], pt3[:, 32:40, SEQ:T], ALU.mult).then_inc(bcx_ready, 1)
            n = JOB["bc"]
            wait_done(dve, n)
            V.tensor_copy(at(BCS, 256), bank(n)[:, 0:256]).then_inc(evac[n % 4], 1)

            for q in range(4):
                n = JOB["fvt"] + q
                wait_done(dve, n)
                V.tensor_copy(ot3[:, 8 + 2 * q:10 + 2 * q, 0:SEQ], bank(n).rearrange("p (h t) -> p h t", h=2)).then_inc(evac[n % 4], 1)

            dve.wait_ge(cs_saved, 16)
            for h in range(NH):
                n = JOB["fs"] + h
                wait_done(dve, n)
                s = at(SC + h * 384, 384)
                V.tensor_tensor(s, bank(n)[:, 0:384], cst(C_CAUS, 384), ALU.add).then_inc(evac[n % 4], 1)
                wait_evac(dve, n)
                ch(V.tensor_reduce(at(NEGM + 2 * h, 1), s[:, 0:P], AX.X, ALU.max, negate=True))
                V.tensor_reduce(at(NEGM + 2 * h + 1, 1), s[:, P:384], AX.X, ALU.max, negate=True).then_inc(neg_ready, 1)
            for h in range(NH):
                dve.wait_ge(prob_raw, 2 * h + 2)
                ch(V.reciprocal(at(SUMS + 2 * h, 2), at(SUMS + 2 * h, 2)))
                s = at(SC + h * 384, 384)
                V.tensor_scalar(s[:, 0:P], s[:, 0:P], at(SUMS + 2 * h, 1), None, ALU.mult).then_inc(prob_ready, 1)
                V.tensor_scalar(s[:, P:384], s[:, P:384], at(SUMS + 2 * h + 1, 1), None, ALU.mult).then_inc(prob_ready, 1)

            B1, B2, B3 = SC, SC + 2048, SC + 4096
            B4, B5, B6 = PT, PT + 2048, PT + 4096
            dve.wait_ge(kv_saved, 32)
            for h in range(NH):
                nd, nk = JOB["gdk"] + 2 * h, JOB["gdk"] + 2 * h + 1
                wait_evac(dve, nd)
                d0 = B6 + (h % 2) * 512
                two = lambda a: at(a, 256).rearrange("p (c t) -> p c t", c=2)
                V.tensor_tensor(two(d0), two(d0), low.unsqueeze(1).broadcast_to([P, 2, P]), ALU.mult).then_inc(dch, 1)
                ch.n += 1
                ch(V.tensor_tensor(two(d0 + 256), two(d0 + 256), upi.unsqueeze(1).broadcast_to([P, 2, P]), ALU.mult))
                wait_done(dve, nk)
                for c in range(2):
                    ins = V.scalar_tensor_tensor(out=at(B1 + (2 * h + c) * P, P), in0=bank(nk)[:, c * P:(c + 1) * P],
                                                 scalar=lgb[:, c, 16 + h:17 + h], in1=at(d0 + c * P, P),
                                                 op0=ALU.mult, op1=ALU.mult)
                ins.then_inc(a_ready, 1)
                V.tensor_tensor(at(B5 + h * 256, 256), bank(nk)[:, 256:512], at(d0 + 256, 256), ALU.mult).then_inc(evac[nk % 4], 1)
            inv = lambda lv, kind, g: JOB["inv"] + 12 * lv + (g if kind == 0 else 4 + 2 * g + kind - 1)
            dve.wait_ge(t_init, 2)
            for lv in range(LEVELS):
                mask = cst(C_INV + lv * P).unsqueeze(1).broadcast_to([P, 4, P])
                for g in range(4):
                    n = inv(lv, 0, g)
                    wait_done(dve, n)
                    V.tensor_tensor(at(B1 + g * 512, 512).rearrange("p (a b) -> p a b", b=P),
                                    bank(n).rearrange("p (a b) -> p a b", b=P), mask, ALU.mult).then_inc(evac[n % 4], 1)
                for g in range(4):
                    for kind, base in ((1, B3), (2, B4)):
                        n = inv(lv, kind, g)
                        wait_done(dve, n)
                        if lv:
                            wait_evac(dve, inv(lv - 1, kind, g))
                        t = at(base + g * 512, 512)
                        V.tensor_tensor(t, t, bank(n), ALU.subtract).then_inc(evac[n % 4], 1)
            for g in range(4):
                n = JOB["gkt"] + g
                wait_done(dve, n)
                for i in range(4):
                    h, c = 2 * g + i // 2, i % 2
                    o = (4 * g + i) * P
                    V.tensor_scalar(at(B2 + o, P), bank(n)[:, i * P:(i + 1) * P], at(BEG + c * 8 + h, 1), None, ALU.mult)
                    ins = V.tensor_scalar(at(B3 + o, P), bank(n)[:, i * P:(i + 1) * P], at(EXS + 16 + c * 8 + h, 1), None, ALU.mult)
                ins.then_inc(evac[n % 4], 1)
            for g in range(4):
                n = JOB["gvt"] + g
                wait_done(dve, n)
                for i in range(4):
                    h, c = 2 * g + i // 2, i % 2
                    ins = V.tensor_scalar(at(B1 + (4 * g + i) * P, P), bank(n)[:, i * P:(i + 1) * P],
                                          lgb[:, c, 16 + h:17 + h], None, ALU.mult)
                ins.then_inc(evac[n % 4], 1)
            for g in range(2):
                wait_evac(dve, JOB["gq"] + g)
                q = pt3[:, 24 + 4 * g:28 + 4 * g, P:2 * P]
                V.tensor_tensor(q, q, at(B2 + 1024 + g * 512, 512).rearrange("p (h t) -> p h t", t=P), ALU.mult).then_inc(qe_ready, 1)
            u1 = at(B6, 2048).rearrange("p (h c t) -> p h c t", c=2, t=P)[:, :, 1, :]
            for g in range(2):
                n = JOB["gws"] + g
                wait_done(dve, n)
                V.tensor_tensor(u1[:, 4 * g:4 * g + 4, :], u1[:, 4 * g:4 * g + 4, :],
                                bank(n).rearrange("p (h t) -> p h t", t=P), ALU.subtract).then_inc(evac[n % 4], 1)
            for g in range(2):
                n = JOB["gs2"] + g
                wait_done(dve, n)
                for i in range(4):
                    h = 4 * g + i
                    s1 = at(B1 + 1024 + h * P, P)
                    ins = V.scalar_tensor_tensor(out=s1, in0=s1, scalar=at(EXS + 40 + h, 1), in1=bank(n)[:, i * P:(i + 1) * P],
                                                 op0=ALU.mult, op1=ALU.add)
                    if i < 3:
                        ins.then_inc(s2_ready, 1)
                    else:
                        ins.then_inc(evac[n % 4], 1)
                wait_evac(dve, n)
                dve.sem_inc(s2_ready, 1)

            n = JOB["sg1"]
            wait_done(dve, n)
            sg = bank(n)[:, 0:128].rearrange("p (s h q) -> p h s q", h=NH, q=2)
            egs, bes, kqs = sh(BCS), sh(BCS + 64), sh(BCS + 192)
            dve.wait_ge(eg_ready, 1)
            dl, os_ = hs(DEL), ot3[:, 8:16, SEQ:T]
            ch(V.tensor_tensor(dl, sg[:, :, :, 1], egs, ALU.mult))
            V.tensor_tensor(os_, sg[:, :, :, 0], egs, ALU.mult).then_inc(evac[n % 4], 1)
            wait_evac(dve, n)
            ch(V.tensor_tensor(dl, pt3[:, 40:48, SEQ:T], dl, ALU.subtract))
            V.tensor_tensor(dl, dl, bes, ALU.mult).then_inc(del_ready, 1)
            dve.wait_ge(del_ready, 1)
            ch(V.tensor_tensor(hs(PSF), dl, kqs, ALU.mult))
            ch(V.tensor_tensor(os_, os_, hs(PSF), ALU.add))
            for g in range(4):
                wait_evac(dve, JOB["go"] + g)
            dve.sem_inc(og_ready, 1)
            wait_evac(dve, JOB["sgd"])
            wait_evac(dve, JOB["sgd"] + 1)
            def spread_delta(h):
                if h >= 2:
                    wait_done(dve, JOB["sgo"] + 2 * h - 3)
                V.tensor_tensor(at(B2 + (h % 2) * 1024, 1024, NS).rearrange("p (s e) -> p s e", e=P),
                                at(B5 + h * P, P, NS).unsqueeze(1).broadcast_to([NS, NS, P]),
                                cst(C_ID, NS, NS).unsqueeze(2).broadcast_to([NS, NS, P]), ALU.mult).then_inc(dmn_ready, 1)

            spread_delta(0)
            for h in range(NH):
                if h + 1 < NH:
                    spread_delta(h + 1)
                for g in range(2):
                    n = JOB["sgo"] + 2 * h + g
                    wait_done(dve, n)
                    for i in range(4):
                        s = 4 * g + i
                        st = state_of(s)[:, h * P:(h + 1) * P]
                        ins = V.scalar_tensor_tensor(out=st, in0=st, scalar=at(BCS + s * NH + h, 1),
                                                     in1=bank(n)[:, i * P:(i + 1) * P], op0=ALU.mult, op1=ALU.add)
                    ins.then_inc(evac[n % 4], 1)
            wait_evac(dve, JOB["sgo"] + 15)
            dve.sem_inc(st_ready, 64)
            V.tensor_tensor(x3(DEL), lgb[0:NS, 2, 0:8].unsqueeze(1).broadcast_to([NS, NS, NH]), eyeb, ALU.mult)
            V.tensor_tensor(sh(PSF), hs(QS), hs(KS), ALU.mult).then_inc(own_ready, 1)
            n = JOB["slf"]
            wait_done(dve, n)
            V.memset(at(LFS + 448, 64), 0.0)
            V.tensor_copy(at(LF, 512).rearrange("p (j s h) -> p h s j", j=PAGES, s=NS),
                          bank(n).rearrange("p (h s j) -> p h s j", h=NH, s=NS)).then_inc(evac[n % 4], 1)
            wait_evac(dve, n)
            n = JOB["sown"]
            wait_done(dve, n)
            own = lambda c, w=1: at(OWN + c, w, 64)
            V.tensor_copy(own(0), bank(n)[0:64, 0:1]).then_inc(evac[n % 4], 1)
            block_norm("gn", 8, 32, lambda b: blk(OT, NH + b), lambda b: par(G_GN), extra=lambda b: blk(PT, 48 + b), base=PT)

            dve.wait_ge(qm_zero, 1)
            V.tensor_copy(at(QM, 64 * 65).rearrange("p (s h c) -> p s h c", h=NH, c=65)[:, :, :, 0],
                          at(QS, 64).rearrange("p (h s) -> p s h", s=NS)).then_inc(qm_ready, 1)
            for q in range(RING):
                low_part(dve, 0, 0, S0["gates"], q)
            for j in range(PAGES - 2, -1, -1):
                ins = V.tensor_tensor(at(LFS + j * 64, 64), at(LFS + (j + 1) * 64, 64), at(LF + (j + 1) * 64, 64), ALU.add)
                if j:
                    ch(ins)
            ins.then_inc(lfs_ready, 1)
            with dve.Fori(0, 3) as it:
                for j in range(RING):
                    for q in range(RING):
                        low_part(dve, it, 4, S0["gates"] + j + 1, q)
            for j in range(RING - 1):
                for q in range(RING):
                    low_part(dve, 0, 0, S0["gates"] + 13 + j, q)
            dve.wait_ge(score_ready, 1)
            wait_evac(dve, JOB["sown"])
            ch(V.tensor_reduce(own(1, 2), ps[0:64, 4:6, :], AX.X, ALU.max))
            ch(V.tensor_reduce(own(3), own(1, 2), AX.X, ALU.max))
            V.tensor_scalar(own(3), own(3), own(0), -1.0, ALU.max, ALU.mult).then_inc(sp_in, 1)
            dve.wait_ge(sp_exp, 3)
            ch(V.tensor_reduce(own(7), own(4, 3), AX.X, ALU.add))
            ch(V.reciprocal(own(7), own(7)))
            V.tensor_scalar(at(PROB, PAGES * P, 64), at(PROB, PAGES * P, 64), own(7), None, ALU.mult).then_inc(sp_ready, 1)
            ch(V.tensor_scalar(own(6), own(6), own(7), None, ALU.mult))
            V.tensor_scalar(own(64, 64), cst(C_ID, 64, 64), own(6), None, ALU.mult).then_inc(dg_ready, 1)
            n = JOB["spt"]
            wait_done(dve, n)
            V.tensor_copy(at(PRT, 512), bank(n)).then_inc(evac[n % 4], 1)
            n = JOB["spb"]
            wait_done(dve, n)
            V.tensor_copy(at(PSF, 64), bank(n)[:, 0:64]).then_inc(evac[n % 4], 1)
            for q in range(RING):
                low_part(dve, 0, 0, S0["gates"] + 16, q)
            for s in range(NS):
                for i in range(2):
                    for q in range(RING):
                        if 2 * s + i < 15:
                            low_part(dve, 0, 0, S0["gates"] + 17 + 2 * s + i, q)
                dve.wait_ge(page_done, 64 + 8 * s + 8)
                b = 4 + 2 * (s % 2)
                ch(V.tensor_tensor(at(OSEL, NH * P, NH).rearrange("p (h d) -> p h d", d=P),
                                   ps[0:NH, b:b + 2, :].rearrange("p b (h d) -> p (b h) d", d=P),
                                   cst(C_ID, NH, NH).unsqueeze(2).broadcast_to([NH, NH, P]), ALU.mult))
                V.tensor_reduce(at(ON + s * P, P, NH), at(OSEL, NH * P, NH).rearrange("p (h d) -> p d h", d=P),
                                AX.X, ALU.add).then_inc(on_ready, 1)
            wait_evac(dve, JOB["spb"])
            ch(V.tensor_tensor(hs(LF), hs(VS), sh(PSF), ALU.mult))
            n = JOB["sot"]
            wait_done(dve, n)
            V.tensor_tensor(ot3[:, 0:8, SEQ:T], hs(LF), bank(n)[:, 0:64].rearrange("p (s h) -> p h s", h=NH),
                            ALU.add).then_inc(of_ready, 1)
            dve.wait_ge(of_ready, 1)
            dve.sem_inc(evac[n % 4], 1)
            wait_evac(dve, JOB["gates1"] + 15)

            dve.wait_ge(of_ready, 1)
            with dve.Fori(0, 4) as it:
                for j in range(RING):
                    n = JOB["up"] + j
                    dve.wait_ge(pe_job, it * 4 + PJ[n])
                    ga = arena[:, bass.ds(it * (4 * T) + (GT + j * T), T)]
                    gb = arena[:, bass.ds(it * (4 * T) + (GT + (16 + j) * T), T)]
                    m, t = at(TMU + (j % 2) * 2 * T, T), at(TMU + ((j % 2) * 2 + 1) * T, T)
                    V.tensor_tensor(t, gb, ps[:, 4 + n % 4, 0:T], ALU.mult).then_inc(mg_step, 1)
                    V.tensor_tensor(m, ga, ps[:, n % 4, 0:T], ALU.mult).then_inc(evac[n % 4], 1)
                    dve.wait_ge(mg_step, it * 8 + (2 * j + 1))
                    dve.wait_ge(evac[n % 4], it + (n // 4 + 1))
                    V.tensor_tensor(m, m, t, ALU.add).then_inc(merged, 1)
                    dve.wait_ge(mh_ready, it * 4 + (j + 1))
                    V.tensor_tensor(split[:, bass.ds(it * (4 * T) + (HL + j * T), T)], m,
                                    as_f32(split[:, bass.ds(it * (4 * T) + (HH + j * T), T)]), ALU.subtract).then_inc(mg_step, 1)
            dve.wait_ge(mg_step, 32)
            dve.sem_inc(mt_ready, 1)

            def add_to_x(it, j):
                n = JOB["out"] + j
                wait_quarter(dve, it, 4, S0["out"] + j, RING - 1)
                x = XT + j * T
                x = at(x + it * 4 * T, T) if isinstance(it, int) else arena[:, bass.ds(it * (4 * T) + x, T)]
                V.tensor_tensor(x, x, bank(n)[:, 0:T], ALU.add).then_inc(evac[n % 4], 1)

            dve.wait_ge(x_again, 16)
            dense_steps(dve, S0["out"], 4, low_part, add_to_x)
            for j in range(RING):
                wait_evac(dve, JOB["out"] + 12 + j)
            dve.sem_inc(x1_ready, 1)
            norm(1, G_FFN)
            low_parts("wq")

            V.memset(at(QZ, 64 + NH * 136), 0.0).then_inc(qz_ready, 1)
            dve.wait_ge(qz_ready, 1)
            for j in range(RING):
                wait_evac(dve, JOB["wq"] + 12 + j)
            for p_ in range(2):
                ins = V.tensor_copy(at(QZ + 64 * p_, NH * 136).rearrange("p (h c) -> p h c", c=136)[:, :, 0:NS],
                                    at(QT, 16 * T).rearrange("p (h q t) -> p h q t", q=2, t=T)[:, :, p_, SEQ:T])
            ins.then_inc(qz_ready, 1)
            for c in range(3):
                m, heads = ROUTE_TILES[c]
                ex = 16 * heads

                def v(a, n):
                    return at(a, n, m)

                for n in RS_JOBS[c]:
                    wait_evac(dve, n)

                def top16(src, src2, vals, idxs, count, width):
                    rows = range(count)
                    sv_ = lambda q, o: v(vals + 16 * q + o, 8)
                    si_ = lambda q, o: v(idxs + 16 * q + o, 8).bitcast(U32)
                    a, b = (lambda q: v(src + width * q, width)), (lambda q: v(src2 + width * q, width))
                    for q in rows:
                        ins = V.max(out=sv_(q, 0), in_=a(q))
                    ch(ins)
                    for q in rows:
                        ins = V.match_replace(b(q), sv_(q, 0), a(q), BIGNEG)
                    ch(ins)
                    for q in rows:
                        V.max_index(si_(q, 0), sv_(q, 0), a(q))
                        ins = V.max(out=sv_(q, 8), in_=b(q))
                    ch(ins)
                    for q in rows:
                        ins = V.max_index(si_(q, 8), sv_(q, 8), b(q))
                    ch(ins)

                top16(RS, RS2, SV, SI, 2 * heads, P)
                sv = v(SV, 2 * ex).rearrange("p (h q k) -> p h q k", q=2, k=16)
                ca = v(CA, 16 * ex).rearrange("p (h i j) -> p h i j", i=16, j=16)
                for h in range(heads):
                    ins = V.tensor_tensor(ca[:, h], sv[:, h, 0, :].unsqueeze(2).broadcast_to([m, 16, 16]),
                                          sv[:, h, 1, :].unsqueeze(1).broadcast_to([m, 16, 16]), ALU.add)
                ch(ins)
                top16(CA, CA2, CV, CI, heads, 256)
                V.tensor_copy(v(SIF, 2 * ex), v(SI, 2 * ex).bitcast(U32))
                V.tensor_scalar(v(CSA, ex).bitcast(U32), v(CI, ex).bitcast(U32), 4, None, ALU.logical_shift_right)
                ch(V.tensor_scalar(v(CSB, ex).bitcast(U32), v(CI, ex).bitcast(U32), 15, None, ALU.bitwise_and))
                V.tensor_copy(v(CFA, ex), v(CSA, ex).bitcast(U32))
                ch(V.tensor_copy(v(CFB, ex), v(CSB, ex).bitcast(U32)))
                if c:
                    wait_done(dve, IDX_JOB[c - 1])
                cv = v(CV, ex).rearrange("p (h k) -> p h k", k=16)
                gt = v(RES + 2 * P, ex).rearrange("p (h k) -> p h k", k=16)
                V.tensor_tensor(gt, cv, cv[:, :, 0:1].broadcast_to([m, heads, 16]), ALU.subtract).then_inc(re_in, 1)
                for side, (cf, sel) in enumerate(((CFA, CA), (CFB, CA2))):
                    V.tensor_tensor(v(sel, 16 * ex).rearrange("p (a j) -> p a j", j=16),
                                    v(cf, ex).unsqueeze(2).broadcast_to([m, ex, 16]),
                                    cst(C_IOTA, 16, m).unsqueeze(1).broadcast_to([m, ex, 16]), ALU.is_equal).then_inc(sel_step, 1)
                dve.wait_ge(sel_step, 2 * c + 2)
                sif = v(SIF, 2 * ex).rearrange("p (h q k) -> p h q k", q=2, k=16)
                for side, sel in enumerate((CA, CA2)):
                    e4 = v(sel, 16 * ex).rearrange("p (h k j) -> p h k j", k=16, j=16)
                    for h in range(heads):
                        ins = V.tensor_tensor(e4[:, h], e4[:, h], sif[:, h, side, :].unsqueeze(1).broadcast_to([m, 16, 16]), ALU.mult)
                ch(ins)
                for side, sel in enumerate((CA, CA2)):
                    ins = V.tensor_reduce(v(RES + side * P, ex), v(sel, 16 * ex).rearrange("p (a j) -> p a j", j=16), AX.X, ALU.add)
                ch(ins)
                dve.wait_ge(re_exp, c + 1)
                ch(V.tensor_reduce(v(RSM, heads), gt, AX.X, ALU.add))
                ch(V.reciprocal(v(RSM, heads), v(RSM, heads)))
                ins = V.tensor_tensor(gt, gt, v(RSM, heads).unsqueeze(2).broadcast_to([m, heads, 16]), ALU.mult)
                if c == 2:
                    ch(ins)
                    V.tensor_reduce(v(ROW_T, NS), cst(C_ID, m, m).rearrange("p (h t) -> p t h", t=NS), AX.X, ALU.add)
                    ch(V.tensor_reduce(v(ROW_H, NH), cst(C_ID, m, m).rearrange("p (h t) -> p h t", t=NS), AX.X, ALU.add))
                    for i in range(3):
                        ins = V.tensor_tensor(v(LX + i * P, P).rearrange("p (h k) -> p h k", k=16),
                                              v(RES + i * P, 16).unsqueeze(1).broadcast_to([m, NH, 16]),
                                              v(ROW_H, NH).unsqueeze(2).broadcast_to([m, NH, 16]), ALU.mult)
                ins.then_inc(res_ready, 1)
                n = IDX_JOB[c]
                wait_done(dve, n)
                w = P if c < 2 else NS
                V.tensor_copy(at(IDX, 3 * T).rearrange("p (i t) -> p i t", t=T)[:, :, c * P:c * P + w],
                              bank(n)[:, 0:384].rearrange("p (i t) -> p i t", t=P)[:, :, 0:w]).then_inc(evac[n % 4], 1)
            wait_evac(dve, IDX_JOB[2])

            for half in range(2):
                wb, ub = JOB[f"wb{half}"], JOB[f"u{half}"]

                def onehot_a(it, j, lead):
                    if not lead:
                        dve.wait_ge(pe_job, it * 8 + (PJ[wb + 2 * j] - 3))
                    oh = at(OHA + (j % 2) * 8 * HALF, 8 * HALF).rearrange("p (t a) -> p t a", a=HALF)
                    ia = arena[:, bass.ds(it * 32 + (IDX + 8 * j), 8)].unsqueeze(2).broadcast_to([P, 8, HALF])
                    V.tensor_tensor(oh, cst(C_IOTA + half * HALF, HALF).unsqueeze(1).broadcast_to([P, 8, HALF]), ia,
                                    ALU.is_equal).then_inc(oh_step, 1)
                    V.tensor_tensor(at(OHB + (j % 2) * 8 * P, 8 * P).rearrange("p (t b) -> p t b", b=P),
                                    cst(C_IOTA).unsqueeze(1).broadcast_to([P, 8, P]),
                                    arena[:, bass.ds(it * 32 + (IDX + T + 8 * j), 8)].unsqueeze(2).broadcast_to([P, 8, P]),
                                    ALU.is_equal).then_inc(ohb_ready, 1)

                if half:
                    wait_done(dve, JOB["wb0"] + 65)
                for j in range(4):
                    onehot_a(0, j, j < 2)
                with dve.Fori(1, 8) as it:
                    for j in range(4):
                        onehot_a(it, j, False)
                onehot_a(8, 0, False)
                for b in range(4):
                    wait_evac(dve, wb + 62 + b)

                s0 = S0[f"peer{half}"]

                def weigh(it, m, s, n, g, buf):
                    for j in range(RING):
                        for q in range(RING):
                            low_part(dve, it, m, s + j + 1, q)
                        dve.wait_ge(evac[(n + j) % 4], it * (m // 8) + ((n + j) // 4 + 1))
                        a, o = at(AB + (j % 2) * T, T), (buf * EG + j) * T
                        w = WH + (4 * g + j) * T
                        w = arena[:, bass.ds(it * (8 * T) + w, T)] if m else at(w, T)
                        blk_n = 4 * (16 * half + g) + j + 1
                        V.tensor_tensor(sp_(AH + o, T), a, w, ALU.mult).then_inc(ah_ready, 1)
                        V.tensor_tensor(a, a, w, ALU.mult).then_inc(aw_ready, 1)
                        dve.wait_ge(ah_ready, it * (m // 2) + blk_n)
                        dve.wait_ge(aw_ready, it * (m // 2) + blk_n)
                        V.tensor_tensor(sp_(AL + o, T), a, as_f32(sp_(AH + o, T)), ALU.subtract).then_inc(a_blk, 1)

                def add_outputs(it, m, s, last=False):
                    for dq in range(RING):
                        for q in range(RING):
                            if not (last and dq == RING - 1):
                                low_part(dve, it, m, s + dq + 1, q)
                            wait_quarter(dve, it, m, s + dq, q)
                            d = 4 * dq + q
                            V.tensor_tensor(xt3[:, d, :], xt3[:, d, :], ps[:, 4 + q, 0:T], ALU.add).then_inc(y_added, 1)

                for q in range(RING):
                    low_part(dve, 0, 0, s0, q)
                weigh(0, 0, s0, ub, 0, 0)
                with dve.Fori(0, 7) as i2:
                    for b in range(2):
                        weigh(i2, 16, s0 + 4 + 8 * b, ub + 4 + 4 * b, b + 1, 1 - b)
                        add_outputs(i2, 16, s0 + 8 + 8 * b)
                weigh(0, 0, s0 + 116, ub + 60, 15, 1)
                add_outputs(0, 0, s0 + 120)
                add_outputs(0, 0, s0 + 124, True)
            dve.wait_ge(y_added, 516)
            dve.sem_inc(x2_ready, 1)
            norm(2, G_PLE)
            def add_embedding(it, j):
                b = 4 * it + j
                n = JOB["ple"] + b
                wait_evac(dve, n)
                dve.wait_ge(pw_done, b + 1)
                t = at(TMP + (b % 2) * T, T)
                ch(V.tensor_tensor(t, blk(GPL, b), ps[:, 4 + b % 4, 0:T], ALU.mult))
                V.tensor_tensor(xt3[:, b, :], xt3[:, b, :], t, ALU.add).then_inc(fin_ready, 1)

            for q in range(RING):
                low_part(dve, 0, 0, S0["ple"], q)
            for b in range(16):
                for q in range(RING):
                    if b < 15:
                        low_part(dve, 0, 0, S0["ple"] + b + 1, q)
                add_embedding(b // 4, b % 4)


def kernel(**inputs):
    import concourse.bacc as bacc
    from concourse.bass_utils import run_bass_kernel_spmd

    x = {k: np.asarray(v) for k, v in inputs.items()}
    c = np.ascontiguousarray
    FW = NH * P
    OFF_F, OFF_G = 3 * FW, 3 * FW + NH
    OFF_A = OFF_G + 3 * FW
    OFF_Z = OFF_A + 2 * NH
    OFF_GATE = OFF_Z + FW
    w_in = x["w_in"][0]

    def blocks(w):
        k, n = w.shape
        return w.reshape(k // P, P, n // P, P).transpose(2, 1, 0, 3).reshape(n // P, P, k)

    def cols(a, tiles):
        return c(a.reshape(T, tiles, P).transpose(2, 1, 0)).reshape(P, tiles * T)

    up = np.concatenate([x["w_up_fox"][0], x["w_up_gdn"][0]], 0)
    wd = np.concatenate([
        blocks(w_in[:, 0:OFF_F]), blocks(w_in[:, OFF_G:OFF_A]), blocks(w_in[:, OFF_Z:OFF_GATE]),
        blocks(w_in[:, OFF_GATE:]), blocks(up), blocks(x["w_out"][0]), blocks(x["peer_w_q"][0]),
        x["peer_u"][0].reshape(N_KEYS, P, KT, P).transpose(0, 3, 2, 1).reshape(N_KEYS, P, D_MODEL),
        blocks(x["w_ple_gate"][0])], 0)
    small = np.concatenate([w_in[:, OFF_F:OFF_G], w_in[:, OFF_A:OFF_Z]], 1)
    rows = lambda v: np.broadcast_to(v, (P, v.shape[-1]))
    gain = lambda v: v.reshape(-1, P).T
    params = np.zeros((P, G_END), np.float32)
    params[:, G_MIX:G_FFN] = gain(x["norm_mix_g"][0])
    params[:, G_FFN:G_PLE] = gain(x["norm_ffn_g"][0])
    params[:, G_PLE:G_FQ] = gain(x["norm_ple_g"][0])
    params[:, G_FQ] = x["fox_q_norm"][0]
    params[:, G_FK] = x["fox_k_norm"][0]
    params[:, G_GN] = x["gdn_norm_g"][0]
    params[:, G_CONV:G_BIAS] = x["gdn_conv_w"][0].reshape(4, 24, P).transpose(2, 0, 1).reshape(P, 96)
    params[:, G_BIAS:G_BIAS + 8] = rows(x["fox_f_bias"])
    params[:, G_BIAS + 8:G_BIAS + 16] = rows(x["gdn_dt_bias"])
    params[:, G_ALOG:G_END] = rows(x["gdn_a_log"])

    arrays = {
        "xT": cols(np.concatenate([x["x_prompt"][0], x["x_sample"][:, 0]], 0), KT),
        "pT": cols(np.concatenate([x["p_prompt"][0, 0], x["p_sample"][0, :, 0]], 0), PLE_KT),
        "wd": wd, "vd": c(x["peer_v"][0].reshape(N_KEYS // EG, EG, P, RING, QK, P).transpose(0, 3, 2, 4, 1, 5)).reshape(N_KEYS, P, D_MODEL),
        "wsmall": c(small.reshape(KT, P, 24).transpose(1, 0, 2)).reshape(P, KT * 24),
        "wple": c(x["w_ple"][0].reshape(PLE_KT, P, D_MODEL).transpose(1, 0, 2)).reshape(P, PLE_KT * D_MODEL),
        "subk": c(x["peer_sub_keys"][0].transpose(3, 0, 1, 2)).reshape(P, 16 * P),
        "kx": x["cache_fox_k"][0].transpose(0, 3, 2, 1).reshape(POOL, P, FW),
        "vx": x["cache_fox_v"][0].reshape(POOL, P, FW), "lx": x["cache_fox_logf"][0].transpose(0, 2, 1).reshape(POOL, FW),
        "state": x["state_gdn"][0].transpose(0, 2, 1, 3).reshape(NS, P, FW),
        "convst": x["state_conv"][0].reshape(NS, 3, 24, P).transpose(3, 2, 0, 1).reshape(P, 576),
        "params": params, "consts": constants(),
        "ptab": x["page_table"].reshape(1, NS * PAGES).astype(np.int32),
    }
    nc = bacc.Bacc("TRN2", target_bir_lowering=False, num_devices=1)
    args = []
    for k, a in arrays.items():
        arrays[k] = a = c(a)
        args.append(nc.dram_tensor("in_" + k, a.shape, mybir.dt.from_np(a.dtype), kind="ExternalInput").ap())
    outs = {"o_x": (P, KT * T), "o_k": (P, NH * T), "o_v": (P, NH * T), "o_lf": (P, 3, NH), "o_sp": (P, FW),
            "o_ss": (NS, P, FW), "o_cs": (P, 24 * 27)}
    for k, s in outs.items():
        args.append(nc.dram_tensor(k, s, F32, kind="ExternalOutput").ap())
    build(nc, *args)
    r = run_bass_kernel_spmd(nc, [{"in_" + k: a for k, a in arrays.items()}], core_ids=[0]).results[0]

    tok = lambda a, tiles: np.asarray(a).reshape(P, tiles, T).transpose(2, 1, 0)
    y = tok(r["o_x"], KT).reshape(T, D_MODEL)
    k, v = tok(r["o_k"], NH), tok(r["o_v"], NH)
    lf = np.asarray(r["o_lf"]).transpose(1, 0, 2)
    sp = np.asarray(r["o_sp"]).reshape(P, NH, P).transpose(1, 0, 2)
    ss = np.asarray(r["o_ss"]).reshape(NS, P, NH, P).transpose(0, 2, 1, 3)
    cs = np.asarray(r["o_cs"]).reshape(P, 24, 27)
    cp = cs[:, :, 0:3].transpose(2, 1, 0).reshape(3, 3 * FW)
    css = cs[:, :, 3:].reshape(P, 24, NS, 3).transpose(2, 3, 1, 0).reshape(NS, 3, 3 * FW)
    return (c(y[None, :SEQ]), c(y[SEQ:, None]), c(k[None, None, :SEQ]), c(v[None, None, :SEQ]),
            c(lf[0:2].reshape(1, 1, SEQ, NH)), c(sp[None, None]), c(cp[None, None]),
            c(k[None, SEQ:, None]), c(v[None, SEQ:, None]), c(lf[2, 0:NS].reshape(1, NS, 1, NH)),
            c(ss[None]), c(css[None]))
```
